# Optimizing a Trainium2 kernel written in Bass

```python
import math
import jax, jax.numpy as jnp
from jax import lax
import numpy as np

D_MODEL = 1024
BATCH = 1
SEQ = 512
DEPTH = 1

N_Q_HEADS = 8
N_KV_HEADS = 2
Q_PER_KV = N_Q_HEADS // N_KV_HEADS
HEAD_DIM = D_MODEL // 16
WINDOW = 128
BLOCK = 128
BRANCH_WIDTH = D_MODEL // 2
KV_WIDTH = N_KV_HEADS * HEAD_DIM
LRU_BLOCKS = 8
LRU_BLOCK_DIM = BRANCH_WIDTH // LRU_BLOCKS
CONV_WIDTH = 4
CONV_PAD = (2, 1)
LRU_C = 8.0
SSM_GROUP = 16
SSM_GROUPS = BRANCH_WIDTH // SSM_GROUP
SSM_STATE = 64
N_BRANCH = 3
IN_COLS = BRANCH_WIDTH + 2 * KV_WIDTH + 3 * BRANCH_WIDTH + N_BRANCH * D_MODEL
N_GROUPS = 4
EXPERTS_PER_GROUP = 4
TOP_K = 2
D_EXPERT = D_MODEL // 4
NORM_EPS = 1e-6
MASK_VALUE = -1e30

kernel_name = 'hybrid_gated_swa_rglru_s5_hmoe'

def rms_norm(x, g):
    xf = x.astype(jnp.float32)
    y = xf * lax.rsqrt(jnp.mean(xf * xf, axis=-1, keepdims=True) + NORM_EPS)
    return (y * g.astype(jnp.float32)).astype(x.dtype)

def _linear_combine(e1, e2):
    a1, b1 = e1
    a2, b2 = e2
    return a1 * a2, a2 * b1 + b2

def _complex_combine(e1, e2):
    ar1, ai1, br1, bi1 = e1
    ar2, ai2, br2, bi2 = e2
    return (ar1 * ar2 - ai1 * ai2,
            ar1 * ai2 + ai1 * ar2,
            ar2 * br1 - ai2 * bi1 + br2,
            ar2 * bi1 + ai2 * br1 + bi2)

def alibi_slopes():
    return jnp.asarray(2.0 ** (-8.0 * (np.arange(N_Q_HEADS) + 1) / N_Q_HEADS), dtype=jnp.float32)

def window_attention(q, k, v, sink):
    b, l = q.shape[0], q.shape[1]
    nb = l // BLOCK
    qb = q.reshape(b, nb, BLOCK, N_KV_HEADS, Q_PER_KV, HEAD_DIM)

    def band(t):
        tp = jnp.pad(t, ((0, 0), (BLOCK, BLOCK), (0, 0), (0, 0)))
        tp = tp.reshape(b, nb + 2, BLOCK, N_KV_HEADS, HEAD_DIM)
        return jnp.concatenate([tp[:, :-2], tp[:, 1:-1], tp[:, 2:]], axis=2)

    kb, vb = band(k), band(v)
    s = jnp.einsum('bnqhgd,bnshd->bnhgqs', qb, kb,
                   preferred_element_type=jnp.float32) * (HEAD_DIM ** -0.5)
    qi = jnp.arange(BLOCK)
    kj = jnp.arange(3 * BLOCK)
    rel = qi[:, None] - kj[None, :] + BLOCK
    key_pos = jnp.arange(nb)[:, None] * BLOCK - BLOCK + kj[None, :]
    valid = (jnp.abs(rel) <= WINDOW)[None] & ((key_pos >= 0) & (key_pos < l))[:, None, :]
    dist = jnp.abs(rel).astype(jnp.float32)
    bias = (-alibi_slopes()[:, None, None] * dist).reshape(N_KV_HEADS, Q_PER_KV, BLOCK, 3 * BLOCK)
    s = jnp.where(valid[None, :, None, None], s + bias, MASK_VALUE)
    sk = sink.astype(jnp.float32).reshape(N_KV_HEADS, Q_PER_KV)[:, :, None, None]
    m = jnp.maximum(jnp.max(s, axis=-1, keepdims=True), sk)
    p = jnp.exp(s - m)
    probs = p / (jnp.sum(p, axis=-1, keepdims=True) + jnp.exp(sk - m))
    o = jnp.einsum('bnhgqs,bnshd->bnqhgd', probs, vb.astype(jnp.float32))
    return o.reshape(b, l, N_Q_HEADS * HEAD_DIM).astype(q.dtype)

def centred_dwconv(x, w, bias):
    y = lax.conv_general_dilated(x, w[:, None, :].astype(x.dtype), window_strides=(1,),
                                 padding=[CONV_PAD], dimension_numbers=('NWC', 'WIO', 'NWC'),
                                 feature_group_count=x.shape[-1])
    return y + bias.astype(x.dtype)

def rg_lru_dir(xc, w_r, b_r, w_i, b_i, lam, reverse):
    b, l, _ = xc.shape
    xb = xc.reshape(b, l, LRU_BLOCKS, LRU_BLOCK_DIM)
    r = jax.nn.sigmoid(jnp.einsum('blhi,hij->blhj', xb, w_r.astype(jnp.float32)).reshape(b, l, BRANCH_WIDTH) + b_r)
    i = jax.nn.sigmoid(jnp.einsum('blhi,hij->blhj', xb, w_i.astype(jnp.float32)).reshape(b, l, BRANCH_WIDTH) + b_i)
    log_a = -LRU_C * r * jax.nn.softplus(-lam)
    a = jnp.exp(log_a)
    u = jnp.sqrt(-jnp.expm1(2.0 * log_a)) * (i * xc)
    _, h = lax.associative_scan(_linear_combine, (a, u), axis=1, reverse=reverse)
    return h

def s5_dir(u, a_re, a_im, log_step, b_re, b_im, reverse):
    bsz, l = u.shape[0], u.shape[1]
    step = jnp.exp(log_step)[:, None]
    mag = jnp.exp(a_re * step)
    abar_r = mag * jnp.cos(a_im * step)
    abar_i = mag * jnp.sin(a_im * step)
    den = a_re * a_re + a_im * a_im
    nr = abar_r - 1.0
    sr = (nr * a_re + abar_i * a_im) / den
    si = (abar_i * a_re - nr * a_im) / den
    bbar_r = sr[..., None] * b_re - si[..., None] * b_im
    bbar_i = sr[..., None] * b_im + si[..., None] * b_re
    bu_r = jnp.einsum('blgc,gnc->blgn', u, bbar_r)
    bu_i = jnp.einsum('blgc,gnc->blgn', u, bbar_i)
    ar = jnp.broadcast_to(abar_r[None, None], (bsz, l, SSM_GROUPS, SSM_STATE))
    ai = jnp.broadcast_to(abar_i[None, None], (bsz, l, SSM_GROUPS, SSM_STATE))
    _, _, hr, hi = lax.associative_scan(_complex_combine, (ar, ai, bu_r, bu_i), axis=1, reverse=reverse)
    return hr, hi

def hybrid_mixer(h, w_in, attn_sink, conv_w, conv_b, w_r, b_r, w_i, b_i, lam,
                 a_re, a_im, log_step, b_re, b_im, c_re, c_im, d_skip, w_glu, b_glu,
                 w_branch, w_out):
    b, l, _ = h.shape
    f32 = jnp.float32
    z = h @ w_in
    cuts = [BRANCH_WIDTH, BRANCH_WIDTH + KV_WIDTH, BRANCH_WIDTH + 2 * KV_WIDTH,
            2 * BRANCH_WIDTH + 2 * KV_WIDTH, 3 * BRANCH_WIDTH + 2 * KV_WIDTH,
            4 * BRANCH_WIDTH + 2 * KV_WIDTH]
    q, k, v, xr, gr, u, gates = jnp.split(z, cuts, axis=-1)

    o_attn = window_attention(q.reshape(b, l, N_Q_HEADS, HEAD_DIM),
                              k.reshape(b, l, N_KV_HEADS, HEAD_DIM),
                              v.reshape(b, l, N_KV_HEADS, HEAD_DIM), attn_sink)

    xc = centred_dwconv(xr, conv_w, conv_b).astype(f32)
    h_f = rg_lru_dir(xc, w_r[0], b_r[0].astype(f32), w_i[0], b_i[0].astype(f32), lam[0].astype(f32), False)
    h_b = rg_lru_dir(xc, w_r[1], b_r[1].astype(f32), w_i[1], b_i[1].astype(f32), lam[1].astype(f32), True)
    o_lru = (jax.nn.gelu(gr.astype(f32)) * (h_f + h_b)).astype(h.dtype)

    uf = u.astype(f32).reshape(b, l, SSM_GROUPS, SSM_GROUP)
    hr_f, hi_f = s5_dir(uf, a_re[0].astype(f32), a_im[0].astype(f32), log_step[0].astype(f32),
                        b_re[0].astype(f32), b_im[0].astype(f32), False)
    hr_b, hi_b = s5_dir(uf, a_re[1].astype(f32), a_im[1].astype(f32), log_step[1].astype(f32),
                        b_re[1].astype(f32), b_im[1].astype(f32), True)
    hr = hr_f + hr_b
    hi = hi_f + hi_b
    y = (jnp.einsum('blgn,gcn->blgc', hr, c_re.astype(f32))
         - jnp.einsum('blgn,gcn->blgc', hi, c_im.astype(f32))
         + d_skip.astype(f32).reshape(SSM_GROUPS, SSM_GROUP) * uf)
    y = y.reshape(b, l, BRANCH_WIDTH)
    zg = jax.nn.gelu(y) @ w_glu.astype(f32) + b_glu.astype(f32)
    o_ssm = (zg[..., :BRANCH_WIDTH] * jax.nn.sigmoid(zg[..., BRANCH_WIDTH:])).astype(h.dtype)

    g = jax.nn.sigmoid(gates.reshape(b, l, N_BRANCH, D_MODEL))
    branches = jnp.stack([o_attn, o_lru, o_ssm], axis=2)
    proj = jnp.einsum('blkw,kwd->blkd', branches, w_branch)
    mixed = jnp.sum(proj * g, axis=2)
    return mixed @ w_out

def hier_moe(x, w_group, b_group, w_expert, b_expert, w1, w3, w2):
    b, l, d = x.shape
    t = b * l
    xt = x.reshape(t, d)
    g_logits = (xt @ w_group).astype(jnp.float32) + b_group.astype(jnp.float32)
    g_prob = jax.nn.softmax(g_logits, axis=-1)
    _, g_idx = lax.top_k(g_logits, 1)
    g_w = jnp.take_along_axis(g_prob, g_idx, axis=-1)
    e_logits = ((xt @ w_expert).astype(jnp.float32) + b_expert.astype(jnp.float32)).reshape(t, N_GROUPS, EXPERTS_PER_GROUP)
    g_onehot = jax.nn.one_hot(g_idx[:, 0], N_GROUPS, dtype=jnp.float32)
    e_sel = jnp.sum(e_logits * g_onehot[:, :, None], axis=1)
    top_v, top_i = lax.top_k(e_sel, TOP_K)
    top_w = jax.nn.softmax(top_v, axis=-1) * g_w
    w_e = jnp.sum(jax.nn.one_hot(top_i, EXPERTS_PER_GROUP, dtype=jnp.float32) * top_w[..., None], axis=1)
    combine = w_e[:, None, :] * g_onehot[:, :, None]
    y = jnp.zeros((t, d), jnp.float32)
    for gi in range(N_GROUPS):
        hg = jax.nn.silu(jnp.einsum('td,edf->tef', xt, w1[gi])) * jnp.einsum('td,edf->tef', xt, w3[gi])
        hg = hg.astype(jnp.float32) * combine[:, gi, :, None]
        y = y + jnp.einsum('tef,efd->td', hg, w2[gi].astype(jnp.float32))
    return y.reshape(b, l, d).astype(x.dtype)

def setup_inputs(seed: int = 0) -> dict:
    key = jax.random.key(seed)
    ks = iter(jax.random.split(key, 64))
    f32 = jnp.float32

    def nrm(shape, scale):
        return scale * jax.random.normal(next(ks), shape, f32)

    def unif(shape, lo, hi):
        return jax.random.uniform(next(ks), shape, f32, lo, hi)

    lam_u = unif((DEPTH, 2, BRANCH_WIDTH), 0.9, 0.999) ** (1.0 / LRU_C)
    lru_lambda = jnp.log(lam_u) - jnp.log1p(-lam_u)
    a_im_base = jnp.pi * jnp.arange(SSM_STATE, dtype=f32)
    return {
        'x': nrm((BATCH, SEQ, D_MODEL), 1.0),
        'norm1_g': 1.0 + nrm((DEPTH, D_MODEL), 0.01),
        'w_in': nrm((DEPTH, D_MODEL, IN_COLS), D_MODEL ** -0.5),
        'attn_sink': nrm((DEPTH, N_Q_HEADS), 0.5),
        'lru_conv_w': nrm((DEPTH, CONV_WIDTH, BRANCH_WIDTH), CONV_WIDTH ** -0.5),
        'lru_conv_b': nrm((DEPTH, BRANCH_WIDTH), 0.01),
        'lru_w_r': nrm((DEPTH, 2, LRU_BLOCKS, LRU_BLOCK_DIM, LRU_BLOCK_DIM), LRU_BLOCK_DIM ** -0.5),
        'lru_b_r': nrm((DEPTH, 2, BRANCH_WIDTH), 0.01),
        'lru_w_i': nrm((DEPTH, 2, LRU_BLOCKS, LRU_BLOCK_DIM, LRU_BLOCK_DIM), LRU_BLOCK_DIM ** -0.5),
        'lru_b_i': nrm((DEPTH, 2, BRANCH_WIDTH), 0.01),
        'lru_lambda': lru_lambda,
        'ssm_a_re': -0.5 + nrm((DEPTH, 2, SSM_GROUPS, SSM_STATE), 0.01),
        'ssm_a_im': a_im_base + nrm((DEPTH, 2, SSM_GROUPS, SSM_STATE), 0.01),
        'ssm_log_step': unif((DEPTH, 2, SSM_GROUPS), math.log(1e-3), math.log(1e-1)),
        'ssm_b_re': nrm((DEPTH, 2, SSM_GROUPS, SSM_STATE, SSM_GROUP), (2 * SSM_GROUP) ** -0.5),
        'ssm_b_im': nrm((DEPTH, 2, SSM_GROUPS, SSM_STATE, SSM_GROUP), (2 * SSM_GROUP) ** -0.5),
        'ssm_c_re': nrm((DEPTH, SSM_GROUPS, SSM_GROUP, SSM_STATE), (2 * SSM_STATE) ** -0.5),
        'ssm_c_im': nrm((DEPTH, SSM_GROUPS, SSM_GROUP, SSM_STATE), (2 * SSM_STATE) ** -0.5),
        'ssm_d': nrm((DEPTH, BRANCH_WIDTH), 1.0),
        'ssm_w_glu': nrm((DEPTH, BRANCH_WIDTH, 2 * BRANCH_WIDTH), BRANCH_WIDTH ** -0.5),
        'ssm_b_glu': nrm((DEPTH, 2 * BRANCH_WIDTH), 0.01),
        'w_branch': nrm((DEPTH, N_BRANCH, BRANCH_WIDTH, D_MODEL), BRANCH_WIDTH ** -0.5),
        'w_out': nrm((DEPTH, D_MODEL, D_MODEL), D_MODEL ** -0.5),
        'norm2_g': 1.0 + nrm((DEPTH, D_MODEL), 0.01),
        'moe_w_group': nrm((DEPTH, D_MODEL, N_GROUPS), D_MODEL ** -0.5),
        'moe_b_group': nrm((DEPTH, N_GROUPS), 0.01),
        'moe_w_expert': nrm((DEPTH, D_MODEL, N_GROUPS * EXPERTS_PER_GROUP), D_MODEL ** -0.5),
        'moe_b_expert': nrm((DEPTH, N_GROUPS * EXPERTS_PER_GROUP), 0.01),
        'moe_w1': nrm((DEPTH, N_GROUPS, EXPERTS_PER_GROUP, D_MODEL, D_EXPERT), D_MODEL ** -0.5),
        'moe_w3': nrm((DEPTH, N_GROUPS, EXPERTS_PER_GROUP, D_MODEL, D_EXPERT), D_MODEL ** -0.5),
        'moe_w2': nrm((DEPTH, N_GROUPS, EXPERTS_PER_GROUP, D_EXPERT, D_MODEL), D_EXPERT ** -0.5),
        'final_norm_g': 1.0 + nrm((D_MODEL,), 0.01),
    }

def reference(x, norm1_g, w_in, attn_sink, lru_conv_w, lru_conv_b, lru_w_r, lru_b_r,
              lru_w_i, lru_b_i, lru_lambda, ssm_a_re, ssm_a_im, ssm_log_step, ssm_b_re,
              ssm_b_im, ssm_c_re, ssm_c_im, ssm_d, ssm_w_glu, ssm_b_glu, w_branch, w_out,
              norm2_g, moe_w_group, moe_b_group, moe_w_expert, moe_b_expert, moe_w1,
              moe_w3, moe_w2, final_norm_g):
    for i in range(DEPTH):
        hn = rms_norm(x, norm1_g[i])
        x = x + hybrid_mixer(hn, w_in[i], attn_sink[i], lru_conv_w[i], lru_conv_b[i],
                             lru_w_r[i], lru_b_r[i], lru_w_i[i], lru_b_i[i], lru_lambda[i],
                             ssm_a_re[i], ssm_a_im[i], ssm_log_step[i], ssm_b_re[i], ssm_b_im[i],
                             ssm_c_re[i], ssm_c_im[i], ssm_d[i], ssm_w_glu[i], ssm_b_glu[i],
                             w_branch[i], w_out[i]).astype(x.dtype)
        hn = rms_norm(x, norm2_g[i])
        x = x + hier_moe(hn, moe_w_group[i], moe_b_group[i], moe_w_expert[i], moe_b_expert[i],
                         moe_w1[i], moe_w3[i], moe_w2[i])
    return rms_norm(x, final_norm_g)


_drawn_inputs = setup_inputs


def setup_inputs(seed=0):
    import zlib

    import numpy as np

    out = dict(_drawn_inputs(seed))
    spreads = {}
    factors = {'norm1_g': 4.017,
     'attn_sink': 64.0,
     'lru_b_r': 8.0,
     'lru_b_i': 8.0,
     'ssm_a_re': 64.0,
     'ssm_b_im': 2.703,
     'ssm_b_glu': 21.779,
     'norm2_g': 3.533,
     'moe_b_group': 3.57,
     'moe_b_expert': 8.0,
     'final_norm_g': 33.579,
     'ssm_c_re': 5.092}
    for name, (base, spread) in spreads.items():
        noise = np.random.default_rng([zlib.crc32(name.encode()), seed]).standard_normal(out[name].shape)
        drawn = base * np.exp(spread * noise) if base else spread * noise
        out[name] = __import__('jax').numpy.asarray(drawn.astype(out[name].dtype))
    for name, factor in factors.items():
        out[name] = (out[name] * factor).astype(out[name].dtype)
    return out
```

```python
import numpy as np
import concourse.bass as bass
from concourse import mybir
from contextlib import ExitStack

T, D = 512, 1024
P = 128
NT, KT = T // P, D // P
NQ, NKV, HD = 8, 2, 64
GQ = NQ // NKV
BW = D // 2
CT = BW // P
NBR = 3
COL_K, COL_V = BW, BW + NKV * HD
COL_XR = BW + 2 * NKV * HD
COL_GR, COL_U = COL_XR + BW, COL_XR + 2 * BW
COL_GATE = COL_XR + 3 * BW
CONV = 4
LB = 64
LRU_C = 8.0
G, C, N = 32, 16, 64
L = 8
NC = T // L
GP = G // 2
E, FE, NGRP = 16, 256, 4
SLAB = 2048
ROUND = E * P
MAXR = T // P
EPS = 1e-6
NEG = -1e30
SCALE = HD ** -0.5

K_ID, K_DIST, K_TRI, K_ONE, K_E128, K_REV, K_DLT, K_END = 0, 128, 512, 640, 768, 784, 800, 816

R_G1, R_CW, R_CB, R_BR, R_BI, R_LAM, R_BG, R_END = 0, 8, 24, 28, 36, 44, 52, 60


def constants():
    c = np.zeros((P, K_END), np.float32)
    p = np.arange(P)
    c[:, K_ID:K_ID + P] = np.eye(P)
    rel = p[:, None] - np.arange(3 * P)[None, :] + P
    c[:, K_DIST:K_DIST + 3 * P] = np.where(np.abs(rel) <= P, -np.abs(rel), NEG * 256.0)
    c[:, K_TRI:K_TRI + P] = p[:, None] < p[None, :]
    c[:, K_ONE:K_ONE + P] = 1.0
    c[:, K_E128:K_E128 + E] = np.arange(E) * P
    c[:, K_REV:K_REV + E] = E - np.arange(E)
    c[:, K_DLT:K_DLT + C] = (p[:, None] % C) == np.arange(C)[None, :]
    token = p[:, None, None] + P * np.arange(NT)[None, None, :] + 0 * np.arange(2)[None, :, None]
    ids = np.stack([token, 2 * token + np.arange(2)[None, :, None]], axis=-1).astype(np.int32)
    return c, ids



class Ring:

    def __init__(self, size):
        self.size, self.jobs = size, []

    def add(self, key, by):
        self.jobs.append((key, by))

    def index(self, key):
        return next(n for n, (k, _) in enumerate(self.jobs) if k == key)

    def emptied(self, n):
        by = self.jobs[n][1]
        return by, sum(1 for _, b in self.jobs[:n + 1] if b == by)


def key_blocks(nb):
    lo, hi = max(0, nb - 1), min(NT - 1, nb + 1)
    return lo, hi - lo + 1


def plan():
    big, tp, sc = Ring(4), Ring(2), Ring(2)
    tp.add("prm", "a")
    tp.add("s5p", "v")
    for k in range(KT):
        tp.add(("x", k), "av"[k % 2])
    for n in range(CT):
        big.add(("u", n), "a")
    for n in range(CT):
        big.add(("xr", n), "a")
    big.add("k", "a")
    big.add("v", "a")
    for r in range(2):
        tp.add(("c", r), "v")
    for ct in range(CT):
        for half in range(2):
            tp.add(("x2", ct, half), "a")
        tp.add(("U", ct), "v")
    for ct in range(CT):
        for j in range(2):
            big.add(("gr" if ct < 2 else "q", 2 * (ct % 2) + j), "a")
        for w in range(2):
            for d in range(2):
                big.add(("lru", ct, w, d), "a")
    for i in range(GQ):
        sc.add(("s", 0, i), "v")
    for d in range(KT):
        for i in range(GQ if d + 1 < KT else 0):
            sc.add(("s", d + 1, i), "v")
        for k in range(key_blocks(d // 2)[1]):
            tp.add(("p", d, k), "av"[k % 2])
        big.add(("g", 1, d), "a")
        big.add(("pv", d), "v")
        big.add(("p", 1, d), "v")
    for d in range(KT):
        if d % 2 == 0:
            for g4 in range(4):
                tp.add(("w", 2 * d + g4), "a")
        big.add(("g", 0, d), "a")
        big.add(("p", 0, d), "v")
        sc.add(("st", d), "v")
    for d in range(KT):
        big.add(("g", 2, d), "a")
        if d == 4:
            sc.add(("kf", 0), "v")
            sc.add(("kb", 0), "v")
    for ct in range(CT):
        for h in range(2):
            big.add(("y1", ct, h), "a")
        if ct + 1 < CT:
            sc.add(("kf", ct + 1), "v")
            sc.add(("kb", ct + 1), "v")
        tp.add(("y2", ct, 0), "v")
        tp.add(("y2", ct, 1), "v")
        tp.add(("y3", ct), "a")
    for n in range(CT):
        big.add(("z1", n), "a")
        big.add(("z0", n), "v")
    for d in range(KT):
        big.add(("p", 2, d), "v")
    for t in range(NT):
        for h in range(2):
            big.add(("wo", t, h), "v")
    for t in range(NT):
        for h in range(2):
            tp.add(("h2", t, h), "av"[h])
    sc.add("logits", "v")
    sc.add("rank", "v")
    return big, tp, sc


def hybrid_block(nc, x, norm1_g, w_in, attn_sink, conv_w, conv_b, w_r, b_r, w_i, b_i, lam,
                 a_re, a_im, log_step, b_re, b_im, c_re, c_im, d_skip, w_glu, b_glu, w_branch,
                 w_out, norm2_g, w_group, b_group, w_expert, b_expert, w1, w3, w2, final_g,
                 consts, token_ids, out, probe=None):
    f32, i32 = mybir.dt.float32, mybir.dt.int32
    ALU, ACT, AX = mybir.AluOpType, mybir.ActivationFunctionType, mybir.AxisListType
    MUL, ADD, SUB, MAX = ALU.mult, ALU.add, ALU.subtract, ALU.max
    BIG, TP, SC = plan()

    ctx = ExitStack()
    with ctx:
        def sb(name, shape, dt=f32):
            return ctx.enter_context(nc.sbuf_tensor(name, shape, dt))

        def sem(name):
            return ctx.enter_context(nc.semaphore(name))

        def bc(ap, axis, n):
            a = ap.unsqueeze(axis)
            shape = list(a.shape)
            shape[axis] = n
            return a.broadcast_to(shape)

        NSLOT = MAXR * ROUND
        slot_table = nc.dram_tensor("slot_table", [NSLOT + 2 * P, 2], i32, kind="Internal").ap()
        hn2_rows = nc.dram_tensor("hn2_rows", [T, D], f32, kind="Internal").ap()
        pair_rows = nc.dram_tensor("pair_rows", [2 * T, D], f32, kind="Internal").ap()

        WR, HS = 8, SLAB // 2
        cst = sb("cst", [P, K_END])
        tok = sb("tok", [P, 2, NT, 2], i32)
        prm = sb("prm", [P, R_END])
        hn = sb("hn", [P, KT * T])
        wring = sb("wring", [P, WR, HS])
        xtok = sb("xtok", [P, NT * D])
        mix = sb("mix", [P, NT * D])
        act = sb("act", [P, NBR * CT * T])
        xrp = sb("xrp", [P, CT * (T + CONV - 1)])
        xc = sb("xc", [P, CT * T])
        r1 = sb("r1", [P, 6 * SLAB])
        X = sb("X", [P, 4 * GP * (NC + 1)])
        U = sb("U", [P, G * NC])
        bb = sb("bb", [P, 4, GP, C])
        cc = sb("cc", [P, 2, GP, C])
        pw = sb("pw", [P, 2, L + 1, 2 * GP])
        aa = sb("aa", [P, 2, 4, GP])
        sm = sb("sm", [P, 96])
        lt = sb("lt", [P, 4, 8])
        dskip = sb("dskip", [2 * C, GP])
        dd = sb("dd", [2 * C, GP, C])
        slot_i = sb("slot_i", [P, 2, NT], i32)
        idx = sb("idx", [P, 4, 2], i32)
        ntot = sb("ntot", [1, 1], i32)

        ident = cst[:, K_ID:K_ID + P]
        hnv = hn[:, :].rearrange("p (k t) -> p k t", k=KT)
        xt = xtok[:, :].rearrange("p (t d) -> p t d", t=NT)
        xs = mix[:, :].rearrange("p (t d) -> p t d", t=NT)
        mixed = mix[:, :].rearrange("p (k t) -> p k t", k=KT)
        actv = act[:, :].rearrange("p (b c t) -> p b c t", b=NBR, c=CT)
        uT = actv[:, 2]
        xrv = xrp[:, :].rearrange("p (c t) -> p c t", c=CT)
        xcv = xc[:, :].rearrange("p (c t) -> p c t", c=CT)
        Xv = X[:, :].rearrange("p (d g s) -> p d g s", d=4, g=GP)
        Xd = X[:, :].rearrange("p (d r g s) -> p d r g s", d=2, r=2, g=GP)
        Uv = U[:, :].rearrange("p (g k) -> p g k", g=G)
        wri = mix[:, 0:1024].rearrange("p (w d c j) -> p w d c j", w=2, d=2, c=CT)
        btmp = mix[:, 1024:2048].rearrange("p (a g c) -> p a g c", a=2, g=2 * GP)
        bin_ = mix[:, 2048:3072].rearrange("p (r g c) -> p r g c", r=2, g=2 * GP)
        crow = mix[:, 3072:4096].rearrange("p (r t h n) -> p r t h n", r=2, t=CT, h=2)
        l_r, l_i, l_v, l_a = [xtok[:, i * 1024:(i + 1) * 1024].rearrange("p (d t) -> p d t", d=2)
                              for i in range(4)]
        l_q = r1[:, 10752:11776].rearrange("p (d t) -> p d t", d=2)
        wn = xtok[:, 0:2048].rearrange("p (d g m) -> p d g m", d=4, g=4)
        tmpA, tmpB = xtok[:, 2048:2560], xtok[:, 2560:3072]
        sgate = xtok[:, :].rearrange("p (k t) -> p k t", k=KT)
        qT = r1[:, 0:2048].rearrange("p (a t) -> p a t", a=GQ)
        kT = r1[:, 2048:2560]
        vS = r1[:, 2560:3072].rearrange("p (a t) -> p a t", a=NT)
        btab = r1[:, 3072:6144].rearrange("p (h k) -> p h k", h=NQ)
        pr = r1[:, 6144:9216].rearrange("p (b h k) -> p b h k", b=2, h=GQ)
        x2 = r1[0:NC, 6144:7168].rearrange("p (g j c) -> p g j c", g=8, j=L)
        pT = r1[:, 9216:10752].rearrange("p (k q) -> p k q", k=3)
        prows = r1[0:R_END, 9216:9216 + P]
        srows = r1[0:96, 9344:9344 + P]
        lstep = r1[0:96, 9472:9474]
        s5p = r1[:, 9474:9570]
        cs = r1[:, 9570:9634].rearrange("p (i g) -> p i g", i=2)
        s5t = r1[:, 11776:12288].rearrange("p (i g) -> p i g", i=16)
        wt = r1[:, 0:2048].rearrange("p (b d n) -> p b d n", b=4, d=4)
        cp = r1[:, 2048:6656].rearrange("p (b d g m) -> p b d g m", b=2, d=4, g=4)
        tmpC, tmpD = r1[:, 6656:7232], r1[:, 7232:7808]
        kx = r1[0:2 * C, 7808:8768].rearrange("p (g m) -> p g m", g=4)
        mm = r1[:, 8768:9792].rearrange("p (g m) -> p g m", g=8)
        y1 = r1[:, 9792:10304].rearrange("p (g k) -> p g k", g=8)
        y2 = r1[0:NC, 10304:11328].rearrange("p (j g c) -> p j g c", j=L, g=8)
        sct = r1[:, 11328:11456].rearrange("p (i d g) -> p i d g", i=2, d=4)
        gbuf = xrp[:, 0:1024].rearrange("p (b t) -> p b t", b=2)
        bbd = xrp[:, 1024:1536].rearrange("p (d g h c) -> p d g h c", d=4, g=4, h=2)
        g2b, fgb = X[:, 0:1024], X[:, 1024:2048]
        wge = X[:, 2048:2208].rearrange("p (k c) -> p k c", k=KT)
        bge = X[:, 2208:2228]
        blank = X[:, 2240:2368].bitcast(i32).rearrange("p (n c) -> p n c", c=2)
        h2 = hn[:, :].rearrange("p (t d) -> p t d", t=NT)
        h2T = mixed
        xg = act[:, 0:2048].rearrange("p (b d) -> p b d", b=2)
        xgT = act[:, 2048:4096].rearrange("p (b k s) -> p b k s", b=2, k=KT)
        sg = act[:, 4096:4608].rearrange("p (b f) -> p b f", b=2)
        hh = act[:, 4608:5120].rearrange("p (b f) -> p b f", b=2)
        hT = act[:, 5120:5632].rearrange("p (b k s) -> p b k s", b=2, k=2)
        yb = U[:, :].rearrange("p (b d) -> p b d", b=2)
        ssq, rstd = sm[:, 0:4], sm[:, 4:8]
        sink = sm[:, 8:16]
        cl = sm[:, 16:24]
        am, anm, aes, asum, ard = [sm[:, 24 + 8 * i:32 + 8 * i].rearrange("p (b h) -> p b h", b=2)
                                   for i in range(5)]
        ssq2, rstd2, ssq3, rstd3 = [sm[:, 64 + 4 * i:68 + 4 * i] for i in range(4)]
        rt = [xc[:, 64 * i:64 * i + 64].rearrange("p (t e) -> p t e", t=NT) for i in range(12)]
        rs = [xc[:, 768 + 4 * i:772 + 4 * i] for i in range(16)]
        rg = [xc[:, 832 + 16 * i:848 + 16 * i].rearrange("p (t e) -> p t e", t=NT) for i in range(8)]

        banks = {"big": [ctx.enter_context(nc.psum_tensor(f"big{i}", [P, 512], f32)) for i in range(4)],
                 "tp": [ctx.enter_context(nc.psum_tensor(f"tp{i}", [P, 512], f32)) for i in range(2)],
                 "sc": [ctx.enter_context(nc.psum_tensor(f"sc{i}", [P, 512], f32)) for i in range(2)]}
        rings = {"big": BIG, "tp": TP, "sc": SC}
        full = {r: sem(f"{r}_full") for r in rings}
        free = {(r, by): sem(f"{r}_emptied_{by}") for r in rings for by in "av"}

        cst_in, prow_in, srow_in, x_in = sem("cst_in"), sem("prow_in"), sem("srow_in"), sem("x_in")
        early_in, lru_w_in, late_in = sem("early_in"), sem("lru_w_in"), sem("late_in")
        slab_in = [sem(f"slab_in{i}") for i in range(WR)]
        dve_step, act_step, pool_step = sem("dve_step"), sem("act_step"), sem("pool_step")
        squares, mean_ready, root_ready, xs_ready = sem("squares"), sem("mean_ready"), sem("root_ready"), sem("xs_ready")
        step_exp, srows_ready, s5_arg, s5_act, s5_tab = sem("step_exp"), sem("srows_ready"), sem("s5_arg"), sem("s5_act"), sem("s5_tab")
        cl_arg, cl_exp, cl_ready = sem("cl_arg"), sem("cl_exp"), sem("cl_ready")
        pad_zero, x_zero, dskip_in = sem("pad_zero"), sem("x_zero"), sem("dskip_in")
        conv_done, btab_ready = sem("conv_done"), sem("btab_ready")
        lru_ta, lru_q, lru_s, lru_out = sem("lru_ta"), sem("lru_q"), sem("lru_s"), sem("lru_out")
        s_max, s_exp, s_prob, pv_done = sem("s_max"), sem("s_exp"), sem("s_prob"), sem("pv_done")
        gate_used = sem("gate_used")
        yg_in = [sem(f"yg_in{t}") for t in range(NT)]
        wn_ready, wn_used, scan_mul, scan_add, scan_done = sem("wn_ready"), sem("wn_used"), sem("scan_mul"), sem("scan_add"), sem("scan_done")
        bbd_zero, bbd_ready, cp_ready, kx_ready, mm_in = sem("bbd_zero"), sem("bbd_ready"), sem("cp_ready"), sem("kx_ready"), sem("mm_in")
        glu_ready, x_again, x1_sq, x1_root, h2_ready, h2_out = sem("glu_ready"), sem("x_again"), sem("x1_sq"), sem("x1_root"), sem("h2_ready"), sem("h2_out")
        pool_pass = sem("pool_pass")
        zero_ready, slot_zero, w_arg, w_exp = sem("zero_ready"), sem("slot_zero"), sem("w_arg"), sem("w_exp")
        mask_ready, n_ready, slots_ready, slot_out = sem("mask_ready"), sem("n_ready"), sem("slots_ready"), sem("slot_out")
        ew_in = [sem(f"ew_in{i}") for i in range(6)]
        w13_used, w2_used, idx_in, xg_in = sem("w13_used"), sem("w2_used"), sem("idx_in"), [sem("xg_in0"), sem("xg_in1")]
        xg_turned, xgT_a, xgT_v, hid_full, silu_done, hh_ready = sem("xg_turned"), sem("xgT_a"), sem("xgT_v"), sem("hid_full"), sem("silu_done"), sem("hh_ready")
        hT_full, hT_ready, y_full, yb_a, yb_v = sem("hT_full"), sem("hT_ready"), sem("y_full"), sem("yb_a"), sem("yb_v")
        rows_out = [sem("rows_out0"), sem("rows_out1")]
        acc_ready, out_sq, out_root, out_ready, out_in = sem("acc_ready"), sem("out_sq"), sem("out_root"), sem("out_ready"), sem("out_in")

        w_in_v = w_in.rearrange("(k p) c -> p k c", p=P)
        w_glu_v = w_glu.rearrange("(k p) c -> p k c", p=P)
        w_out_v = w_out.rearrange("(k p) c -> p k c", p=P)
        slabs = []

        def in_slab(key, col):
            slabs.append((key, [(lambda w: w.rearrange("p (k c) -> p k c", k=KT), w_in_v[:, :, col:col + P])]))

        def q_slab(i):
            slabs.append((("q", i), [
                (lambda w, h=h: w.rearrange("p (k h c) -> p k h c", k=KT, h=2)[:, :, h, :],
                 w_in_v[:, :, (h * GQ + i) * HD:(h * GQ + i + 1) * HD]) for h in range(2)]))

        def branch_slab(b, n):
            cols = slice(n * 256, n * 256 + 256)
            if b:
                parts = [(lambda w: w.rearrange("p (k c) -> p k c", k=CT),
                          w_branch[b].rearrange("(k p) c -> p k c", p=P)[:, :, cols])]
            else:
                parts = [(lambda w, h=h: w[h * HD:(h + 1) * HD].rearrange("p (k c) -> p k c", k=CT),
                          w_branch[0, h * GQ * HD:(h + 1) * GQ * HD].rearrange("(k p) c -> p k c", p=HD)[:, :, cols])
                         for h in range(2)]
            slabs.append((("p", b, n), parts))

        for n in range(CT):
            in_slab(("u", n), COL_U + P * n)
        for n in range(CT):
            in_slab(("xr", n), COL_XR + P * n)
        in_slab("k", COL_K)
        in_slab("v", COL_V)
        for n in range(CT):
            in_slab(("gr", n), COL_GR + P * n)
        for n in range(CT):
            q_slab(n)
        for b in (1, 0):
            for d in range(KT):
                in_slab(("g", b, d), COL_GATE + b * D + P * d)
                if d % 2 == 0:
                    branch_slab(b, d // 2)
        for d in range(KT):
            in_slab(("g", 2, d), COL_GATE + 2 * D + P * d)
        for n in range(CT):
            slabs.append((("z", n), [(lambda w, h=h: w.rearrange("p (k h c) -> p k h c", k=CT, h=2)[:, :, h, :],
                                      w_glu_v[:, :, h * BW + P * n:h * BW + P * n + P]) for h in range(2)]))
        for n in range(4):
            branch_slab(2, n)
        for h in range(2):
            for n in range(4):
                slabs.append((("wo", h, n), [(lambda w: w.rearrange("p (k c) -> p k c", k=2),
                                              w_out_v[:, 2 * n:2 * n + 2, h * 512:h * 512 + 512])]))
        slab_at = {key: n for n, (key, _) in enumerate(slabs)}

        def slab_count(n):
            return 16 * sum(len(slabs[m][1]) for m in range(n % WR, n + 1, WR))

        def pe_bank(eng, ring, key):
            r = rings[ring]
            n = r.index(key)
            if n >= r.size:
                by, count = r.emptied(n - r.size)
                eng.wait_ge(free[ring, by], count)
            return banks[ring][n % r.size]

        def full_bank(eng, ring, key):
            r = rings[ring]
            n = r.index(key)
            eng.wait_ge(full[ring], n + 1)
            return banks[ring][n % r.size]

        def emptied(ring, key):
            by, count = rings[ring].emptied(rings[ring].index(key))
            return free[ring, by], count

        def slab_last_job(key):
            if key[0] == "p":
                return BIG.index(("p", key[1], 2 * key[2] + 1))
            if key[0] == "wo":
                return BIG.index(("wo", NT - 1, key[1]))
            if key[0] == "z":
                return BIG.index(("z0", key[1]))
            return BIG.index(key)

        block = ctx.enter_context(nc.Block())

        @block.sync
        def _(sp):
            for t in range(NT):
                sp.dma_start(xt[:, t, :], x[t * P:(t + 1) * P, :]).then_inc(x_in, 16)
            for n, (key, parts) in enumerate(slabs):
                if n >= WR:
                    sp.wait_ge(full["big"], slab_last_job(slabs[n - WR][0]) + 1)
                for shape, src in parts:
                    sp.dma_start(shape(wring[:, n % WR, :]), src).then_inc(slab_in[n % WR], 16)

            def expert_weights(e, h):
                for j, w in enumerate((w1, w3, w2)):
                    k = KT if j < 2 else 2
                    dst = r1[:, (3 * h + j) * SLAB:(3 * h + j + 1) * SLAB].rearrange("p (k f) -> p k f", k=k)
                    src = w[bass.ds(e, 1)].rearrange("o (k p) f -> p (o k) f", p=P)
                    sp.dma_start(dst, src).then_inc(ew_in[3 * h + j], 16)

            sp.wait_ge(gate_used, NBR * KT)
            for t in range(NT):
                sp.dma_start(xt[:, t, :], x[t * P:(t + 1) * P, :]).then_inc(x_again, 16)
            sp.wait_ge(full["tp"], TP.index(("y3", CT - 1)) + 1)
            for h in range(2):
                expert_weights(h, h)
            for t in range(NT):
                sp.wait_ge(h2_ready, t + 1)
                sp.dma_start(hn2_rows[t * P:(t + 1) * P, :], h2[:, t, :]).then_inc(h2_out, 16)
            sp.wait_ge(n_ready, 1)
            rest = sp.value_load(ntot[0:1, 0:1], min_val=E - 4, max_val=MAXR * E - 4)
            with sp.Fori(2, rest + 4, 2) as g:
                for h in range(2):
                    sp.wait_ge(hid_full, g + (h - 1))
                    sp.wait_ge(y_full, g + (h - 1))
                    expert_weights((g + h) % E, h)
            sp.wait_ge(rows_out[0], rest * 8 + 32)
            sp.wait_ge(rows_out[1], rest * 8 + 32)
            sp.wait_ge(n_ready, 1)
            pairs = pair_rows.rearrange("(t p c) d -> t p c d", p=P, c=2)
            for t in range(NT):
                for c in range(2):
                    sp.dma_start((hn, mix)[c][:, t * D:(t + 1) * D], pairs[t, :, c, :]).then_inc(yg_in[t], 16)
            for t in range(NT):
                sp.wait_ge(out_ready, t + 1)
                sp.dma_start(out[t * P:(t + 1) * P, :], xt[:, t, :]).then_inc(out_in, 16)
            sp.wait_ge(out_in, 16 * NT)

        @block.gpsimd
        def _(pool):
            steps = [0]

            def link(ins):
                steps[0] += 1
                ins.then_inc(pool_step, 1)
                pool.wait_ge(pool_step, steps[0])

            nc.gpsimd.memset(xrv[:, :, 0:2], 0.0).then_inc(pad_zero, 1)
            nc.gpsimd.memset(xrv[:, :, T + 2:T + 3], 0.0).then_inc(pad_zero, 1)
            nc.gpsimd.memset(Xv[:, :, :, 0:1], 0.0).then_inc(x_zero, 1)
            pool.wait_ge(cst_in, 32)
            for h in range(NQ):
                nc.gpsimd.tensor_scalar(btab[:, h, :], cst[:, K_DIST:K_DIST + 3 * P],
                                        float(2.0 ** (-8.0 * (h + 1) / NQ)), None, MUL).then_inc(btab_ready, 1)
            pool.wait_ge(s5_tab, 1)
            pool.wait_ge(lru_out, CT)
            for ct in range(CT):
                if ct:
                    pool.wait_ge(full["tp"], TP.index(("w", 4 * ct - 1)) + 1)
                tv = [t.rearrange("p (g j c) -> p g j c", g=4, j=L) for t in (tmpA, tmpB)]
                for d in range(2):
                    cols = slice(d * GP + 4 * ct, d * GP + 4 * ct + 4)

                    def power(r):
                        rows = pw[:, r, L - 1::-1, cols] if d == 0 else pw[:, r, 0:L, cols]
                        return bc(rows.rearrange("p j g -> p g j"), 3, C)

                    def b_of(r):
                        return bc(bb[:, 2 * d + r, 4 * ct:4 * ct + 4, :], 2, L)

                    dst = [wn[:, 2 * d + r].rearrange("p g (j c) -> p g j c", j=L) for r in range(2)]
                    link(nc.gpsimd.tensor_tensor(tv[0], power(0), b_of(0), MUL))
                    link(nc.gpsimd.tensor_tensor(tv[1], power(1), b_of(1), MUL))
                    link(nc.gpsimd.tensor_tensor(dst[0], tv[0], tv[1], SUB))
                    link(nc.gpsimd.tensor_tensor(tv[0], power(0), b_of(1), MUL))
                    link(nc.gpsimd.tensor_tensor(tv[1], power(1), b_of(0), MUL))
                    nc.gpsimd.tensor_tensor(dst[1], tv[0], tv[1], ADD).then_inc(wn_ready, 1)
                    pool.wait_ge(wn_ready, 2 * ct + d + 1)
            pool.wait_ge(*emptied("sc", ("st", KT - 1)))
            with pool.Fori(1, NC - 1, 2) as s0:
                for h in range(2):
                    s = s0 + h
                    now = Xv[:, :, :, bass.ds(s, 1)].rearrange("p d g s -> p d (g s)")
                    nxt = Xv[:, :, :, bass.ds(s + 1, 1)].rearrange("p d g s -> p d (g s)")
                    nxtd = Xd[:, :, :, :, bass.ds(s + 1, 1)].rearrange("p d r g s -> p d r (g s)")
                    swapped = sct[:, 1].rearrange("p (d r) g -> p d r g", d=2)[:, :, ::-1, :]
                    nc.gpsimd.tensor_tensor(sct[:, 0], aa[:, 0], now, MUL).then_inc(scan_mul, 1)
                    nc.gpsimd.tensor_tensor(sct[:, 1], aa[:, 1], now, MUL).then_inc(scan_mul, 1)
                    pool.wait_ge(scan_mul, s * 2 - 1)
                    pool.sem_inc(pool_pass, 1)
                    nc.gpsimd.tensor_tensor(nxt, nxt, sct[:, 0], ADD).then_inc(scan_add, 1)
                    pool.wait_ge(scan_mul, s * 2)
                    pool.wait_ge(scan_add, s * 2 - 1)
                    pool.sem_inc(pool_pass, 1)
                    nc.gpsimd.tensor_tensor(nxtd, nxtd, swapped, ADD).then_inc(scan_add, 1)
                    pool.wait_ge(scan_add, s * 2)
                    pool.sem_inc(pool_pass, 1)
            pool.wait_ge(full["tp"], TP.index(("y3", CT - 1)) + 1)
            pool.dma_start(g2b, norm2_g.partition_broadcast(P)).then_inc(late_in, 16)
            pool.dma_start(fgb, final_g.partition_broadcast(P)).then_inc(late_in, 16)
            pool.dma_start(wge[:, :, 0:NGRP], w_group.rearrange("(k p) c -> p k c", p=P)).then_inc(late_in, 16)
            pool.dma_start(wge[:, :, NGRP:NGRP + E], w_expert.rearrange("(k p) c -> p k c", p=P)).then_inc(late_in, 16)
            pool.dma_start(bge[:, 0:NGRP], b_group.partition_broadcast(P)).then_inc(late_in, 16)
            pool.dma_start(bge[:, NGRP:NGRP + E], b_expert.partition_broadcast(P)).then_inc(late_in, 16)
            nc.gpsimd.memset(blank[:, :, 0:1], 0).then_inc(zero_ready, 1)
            nc.gpsimd.memset(blank[:, :, 1:2], 2 * T).then_inc(zero_ready, 1)
            pool.wait_ge(zero_ready, 2)
            pool.dma_start(slot_table[0:NSLOT].rearrange("(p n) c -> p n c", p=P), blank).then_inc(slot_zero, 16)
            pool.wait_ge(slot_zero, 16)
            pool.wait_ge(slots_ready, 2)
            for c in range(2):
                for t in range(NT):
                    pool.indirect_dma_start(slot_table, bass.IndirectOffsetOnAxis(ap=slot_i[:, c, t:t + 1], axis=0),
                                            tok[:, c, t, :], None).then_inc(slot_out, 16)
            pool.wait_ge(slot_out, 16 * 2 * NT)
            pool.wait_ge(h2_out, 16 * NT)
            pool.wait_ge(n_ready, 1)
            rest = pool.value_load(ntot[0:1, 0:1], min_val=E - 4, max_val=MAXR * E - 4)

            def gather(i, h, b):
                pool.dma_start(idx[:, b, :], slot_table[bass.ds(i * P, P), :]).then_inc(idx_in, 16)
                pool.wait_ge(idx_in, i * 16 + 16)
                pool.sem_inc(pool_pass, 1)
                pool.indirect_dma_start(xg[:, h, :], None, hn2_rows,
                                        bass.IndirectOffsetOnAxis(ap=idx[:, b, 0:1], axis=0)).then_inc(xg_in[h], 16)

            def scatter(i, h, b):
                pool.wait_ge(yb_a, i + 1)
                pool.wait_ge(yb_v, i + 1)
                pool.sem_inc(pool_pass, 1)
                pool.indirect_dma_start(pair_rows, bass.IndirectOffsetOnAxis(ap=idx[:, b, 1:2], axis=0), yb[:, h, :], None,
                                        bounds_check=2 * T - 1, oob_is_err=False).then_inc(rows_out[h], 16)

            gather(0, 0, 0)
            gather(1, 1, 1)
            with pool.Fori(0, rest, 4) as g:
                for j in range(4):
                    pool.wait_ge(xg_turned, g + (j + 1))
                    gather(g + (j + 2), j % 2, (j + 2) % 4)
                    scatter(g + j, j % 2, j)
            for j in range(4):
                if j < 2:
                    pool.wait_ge(xg_turned, rest + (j + 1))
                    gather(rest + (j + 2), j % 2, (j + 2) % 4)
                scatter(rest + j, j % 2, j)

        @block.tensor
        def _(pe):
            mmul = nc.tensor.matmul

            def turn(dst, src, n=P):
                return nc.tensor.transpose(dst, src, cst[0:n, K_ID:K_ID + n])

            def weights(key):
                n = slab_at[key]
                pe.wait_ge(slab_in[n % WR], slab_count(n))
                return wring[:, n % WR, :]

            def channels(key, w, rhs, ks, bank=None):
                bank = pe_bank(pe, "big", key)
                for k in range(ks):
                    ins = mmul(bank[:, :], w[:, k, :], rhs[:, k, :], start=(k == 0), stop=(k == ks - 1))
                ins.then_inc(full["big"], 1)

            def project(key):
                channels(key, weights(key).rearrange("p (k c) -> p k c", k=KT), hnv, KT)

            def branch(b, d):
                w = weights(("p", b, d // 2)).rearrange("p (k c) -> p k c", k=CT)
                channels(("p", b, d), w[:, :, (d % 2) * P:(d % 2 + 1) * P], actv[:, b], CT)

            pe.wait_ge(cst_in, 32)
            pe.wait_ge(prow_in, 16 * 8)
            turn(pe_bank(pe, "tp", "prm")[:, 0:R_END], prows[:, :], R_END).then_inc(full["tp"], 1)
            pe.wait_ge(srow_in, 16 * 3)
            pe.wait_ge(srows_ready, 1)
            turn(pe_bank(pe, "tp", "s5p")[:, 0:96], srows[:, :], 96).then_inc(full["tp"], 1)
            pe.wait_ge(xs_ready, NT)
            for k in range(KT):
                bank = pe_bank(pe, "tp", ("x", k))
                for t in range(NT):
                    ins = turn(bank[:, t * P:(t + 1) * P], xs[:, t, k * P:(k + 1) * P])
                ins.then_inc(full["tp"], 1)
            pe.wait_ge(*emptied("tp", ("x", KT - 2)))
            pe.wait_ge(*emptied("tp", ("x", KT - 1)))
            for n in range(CT):
                project(("u", n))
            for n in range(CT):
                project(("xr", n))
            project("k")
            w = weights("v").rearrange("p (k c) -> p k c", k=KT)
            bank = pe_bank(pe, "big", "v")
            for t in range(NT):
                for k in range(KT):
                    ins = mmul(bank[:, t * P:(t + 1) * P], hnv[:, k, t * P:(t + 1) * P], w[:, k, :],
                               start=(k == 0), stop=(k == KT - 1))
            ins.then_inc(full["big"], 1)
            pe.wait_ge(early_in, 16 * 8)
            for r in range(2):
                bank = pe_bank(pe, "tp", ("c", r))
                for q in range(CT):
                    ins = turn(bank[:, q * P:(q + 1) * P], crow[:, r, q].rearrange("p h n -> p (h n)"))
                ins.then_inc(full["tp"], 1)
            pe.wait_ge(*emptied("big", ("u", CT - 1)))
            for ct in range(CT):
                for half in range(2):
                    bank = pe_bank(pe, "tp", ("x2", ct, half))
                    for j in range(4):
                        ins = turn(bank[0:NC, j * P:(j + 1) * P], uT[:, ct, half * 4 + j::L])
                    ins.then_inc(full["tp"], 1)
                for half in range(2):
                    pe.wait_ge(*emptied("tp", ("x2", ct, half)))
                bank = pe_bank(pe, "tp", ("U", ct))
                for g in range(8):
                    ins = turn(bank[:, g * NC:(g + 1) * NC], x2[:, g].rearrange("p j c -> p (j c)"), NC)
                ins.then_inc(full["tp"], 1)
            pe.wait_ge(lru_w_in, 16 * 8)
            for ct in range(CT):
                for j in range(2):
                    project(("gr" if ct < 2 else "q", 2 * (ct % 2) + j))
                pe.wait_ge(conv_done, ct + 1)
                for w in range(2):
                    for d in range(2):
                        bank = pe_bank(pe, "big", ("lru", ct, w, d))
                        for h in range(2):
                            rows = slice(h * LB, (h + 1) * LB)
                            ins = mmul(bank[rows, :], wri[rows, w, d, ct, :], xcv[rows, ct, :], start=True, stop=True)
                        ins.then_inc(full["big"], 1)

            def scores(u):
                nb, h = u // 2, u % 2
                lo, n = key_blocks(nb)
                rows = slice(h * HD, (h + 1) * HD)
                for i in range(GQ):
                    bank = pe_bank(pe, "sc", ("s", u, i))
                    mmul(bank[:, 0:n * P], qT[rows, i, nb * P:(nb + 1) * P], kT[rows, lo * P:(lo + n) * P],
                         start=True, stop=True).then_inc(full["sc"], 1)

            pe.wait_ge(*emptied("big", ("q", CT - 1)))
            scores(0)
            for d in range(KT):
                if d + 1 < KT:
                    scores(d + 1)
                nb, h = d // 2, d % 2
                lo, n = key_blocks(nb)
                pe.wait_ge(s_prob, d + 1)
                for k in range(n):
                    bank = pe_bank(pe, "tp", ("p", d, k))
                    for i in range(GQ):
                        ins = turn(bank[:, i * P:(i + 1) * P], pr[:, d % 2, i, k * P:(k + 1) * P])
                    ins.then_inc(full["tp"], 1)
                project(("g", 1, d))
                bank = pe_bank(pe, "big", ("pv", d))
                for k in range(n):
                    pe.wait_ge(*emptied("tp", ("p", d, k)))
                    ins = mmul(bank[h * HD:(h + 1) * HD, :], vS[:, lo + k, h * HD:(h + 1) * HD], pT[:, k, :],
                               start=(k == 0), stop=(k == n - 1))
                ins.then_inc(full["big"], 1)
                pe.wait_ge(lru_out, CT)
                branch(1, d)
            pe.wait_ge(*emptied("big", ("pv", KT - 1)))
            for d in range(KT):
                if d % 2 == 0:
                    pe.wait_ge(wn_ready, d + 2)
                    for g4 in range(4):
                        bank = pe_bank(pe, "tp", ("w", 2 * d + g4))
                        for q in range(4):
                            ins = turn(bank[:, q * P:(q + 1) * P], wn[:, q, g4, :])
                        ins.then_inc(full["tp"], 1)
                project(("g", 0, d))
                bank = pe_bank(pe, "sc", ("st", d))
                for h in range(2):
                    g4 = 2 * (d % 2) + h
                    pe.wait_ge(*emptied("tp", ("w", 4 * (d // 2) + g4)))
                    for q in range(4):
                        for g2 in range(2):
                            g = 4 * d + 2 * h + g2
                            rhs = Uv[:, g, :] if q < 2 else Uv[:, g, ::-1]
                            ins = mmul(bank[g2 * N:(g2 + 1) * N, (q * 2 + h) * NC:(q * 2 + h + 1) * NC],
                                       wt[:, g4, q, g2 * N:(g2 + 1) * N], rhs, start=True, stop=True)
                ins.then_inc(full["sc"], 1)
                branch(0, d)

            def kernel_of(ct):
                pe.wait_ge(cp_ready, 2 * ct + 2)
                pe.wait_ge(bbd_ready, 2 * ct + 2)
                for name, d, off in (("kf", 0, 0), ("kb", 1, C)):
                    bank = pe_bank(pe, "sc", (name, ct))
                    for g4 in range(4):
                        for r in range(2):
                            ins = mmul(bank[0:2 * C, g4 * P:(g4 + 1) * P],
                                       bbd[:, 2 * d + r, g4].rearrange("p h c -> p (h c)"),
                                       cp[:, ct % 2, 2 * d + r, g4, off:off + P], start=(r == 0), stop=(r == 1))
                    ins.then_inc(full["sc"], 1)

            for d in range(KT):
                project(("g", 2, d))
                if d == 4:
                    kernel_of(0)
            pe.wait_ge(scan_add, 2 * (NC - 2))
            for ct in range(CT):
                pe.wait_ge(mm_in, 16 * 2 * L * (ct + 1))
                for g in (0, 2, 4, 6, 1, 3, 5, 7):
                    if g < 2:
                        bank = pe_bank(pe, "big", ("y1", ct, g))
                    dst = bank[:, (g // 2) * NC:(g // 2 + 1) * NC]
                    rows = slice((g % 2) * N, (g % 2 + 1) * N)
                    gp = 4 * ct + g // 2
                    mmul(dst, mm[:, g, :], Uv[:, 8 * ct + g, :], start=True, stop=False)
                    for q in range(4):
                        off = C if q < 2 else 0
                        st = Xv[rows, q, gp, 0:NC] if q < 2 else Xv[rows, q, gp, NC - 1::-1]
                        ins = mmul(dst, cp[rows, ct % 2, q, g // 2, off:off + P], st, start=False, stop=(q == 3))
                    if g >= 6:
                        ins.then_inc(full["big"], 1)
                if ct + 1 < CT:
                    kernel_of(ct + 1)
                pe.wait_ge(*emptied("big", ("y1", ct, 1)))
                for half in range(2):
                    bank = pe_bank(pe, "tp", ("y2", ct, half))
                    for g in range(4):
                        ins = turn(bank[0:NC, g * P:(g + 1) * P], y1[:, 4 * half + g, :])
                    ins.then_inc(full["tp"], 1)
                for half in range(2):
                    pe.wait_ge(*emptied("tp", ("y2", ct, half)))
                bank = pe_bank(pe, "tp", ("y3", ct))
                for j in range(L):
                    ins = turn(bank[:, j * NC:(j + 1) * NC], y2[:, j].rearrange("p g c -> p (g c)"), NC)
                ins.then_inc(full["tp"], 1)
            pe.wait_ge(*emptied("tp", ("y3", CT - 1)))
            for n in range(CT):
                w = weights(("z", n)).rearrange("p (k h c) -> p k h c", k=CT, h=2)
                channels(("z1", n), w[:, :, 1, :], xcv, CT)
                channels(("z0", n), w[:, :, 0, :], xcv, CT)
            pe.wait_ge(glu_ready, CT)
            for d in range(KT):
                branch(2, d)
            pe.wait_ge(gate_used, NBR * KT)
            for t in range(NT):
                for h in range(2):
                    bank = pe_bank(pe, "big", ("wo", t, h))
                    for k in range(KT):
                        w = weights(("wo", h, k // 2)).rearrange("p (k c) -> p k c", k=2)
                        ins = mmul(bank[:, :], mixed[:, k, t * P:(t + 1) * P], w[:, k % 2, :],
                                   start=(k == 0), stop=(k == KT - 1))
                    ins.then_inc(full["big"], 1)
            pe.wait_ge(late_in, 16 * 6)
            lb = pe_bank(pe, "sc", "logits")
            for t in range(NT):
                pe.wait_ge(h2_ready, t + 1)
                for half in range(2):
                    bank = pe_bank(pe, "tp", ("h2", t, half))
                    for k in range(4):
                        ins = turn(bank[:, k * P:(k + 1) * P], h2[:, t, (4 * half + k) * P:(4 * half + k + 1) * P])
                    ins.then_inc(full["tp"], 1)
                for half in range(2):
                    pe.wait_ge(*emptied("tp", ("h2", t, half)))
                for k in range(KT):
                    ins = mmul(lb[:, t * (NGRP + E):(t + 1) * (NGRP + E)], h2T[:, k, t * P:(t + 1) * P], wge[:, k, :],
                               start=(k == 0), stop=(k == KT - 1))
            ins.then_inc(full["sc"], 1)
            rb = pe_bank(pe, "sc", "rank")
            pe.wait_ge(mask_ready, 1)
            for t in range(NT + 1):
                for i in range(min(t + 1, NT)):
                    m = K_TRI if i == t else K_ONE
                    ins = mmul(rb[:, t * E:(t + 1) * E], cst[:, m:m + P], rt[7][:, i, :],
                               start=(i == 0), stop=(i == min(t, NT - 1)))
            ins.then_inc(full["sc"], 1)

            pe.wait_ge(n_ready, 1)
            rest = pe.value_load(ntot[0:1, 0:1], min_val=E - 4, max_val=MAXR * E - 4)

            def turn_rows(i, h, first):
                pe.wait_ge(xg_in[h], (i + (2 - h)) * 8)
                if not first:
                    pe.wait_ge(xgT_a, i)
                    pe.wait_ge(xgT_v, i)
                for k in range(KT):
                    ins = turn(banks["tp"][k // 4][:, (k % 4) * P:(k % 4 + 1) * P], xg[:, h, k * P:(k + 1) * P])
                ins.then_inc(xg_turned, 1)

            def hidden(i, h, first):
                pe.wait_ge(ew_in[3 * h], (i + (2 - h)) * 8)
                pe.wait_ge(ew_in[3 * h + 1], (i + (2 - h)) * 8)
                pe.wait_ge(xgT_a, i + 1)
                pe.wait_ge(xgT_v, i + 1)
                if not first:
                    pe.wait_ge(hh_ready, i)
                w = r1[:, 3 * h * SLAB:(3 * h + 2) * SLAB].rearrange("p (w k f) -> p k w f", w=2, k=KT)
                for k in range(KT):
                    ins = mmul(banks["sc"][0][:, :].rearrange("p (w f) -> p w f", w=2), xgT[:, h, k, :], w[:, k],
                               start=(k == 0), stop=(k == KT - 1))
                ins.then_inc(hid_full, 1)

            def outputs(i, h, second):
                pe.wait_ge(hh_ready, i + 1)
                for k in range(2):
                    ins = turn(banks["sc"][1][:, k * P:(k + 1) * P], hh[:, h, k * P:(k + 1) * P])
                ins.then_inc(hT_full, 1)
                pe.wait_ge(ew_in[3 * h + 2], (i + (2 - h)) * 8)
                pe.wait_ge(hT_ready, i + 1)
                if not second:
                    pe.wait_ge(yb_a, i - 1)
                    pe.wait_ge(yb_v, i - 1)
                w = r1[:, (3 * h + 2) * SLAB:(3 * h + 3) * SLAB].rearrange("p (k f) -> p k f", k=2)
                for q in range(2):
                    for k in range(2):
                        ins = mmul(banks["big"][2 * h + q][:, :], hT[:, h, k, :], w[:, k, q * 512:(q + 1) * 512],
                                   start=(k == 0), stop=(k == 1))
                ins.then_inc(y_full, 1)

            turn_rows(0, 0, True)
            hidden(0, 0, True)
            turn_rows(1, 1, False)
            outputs(0, 0, True)
            hidden(1, 1, False)
            turn_rows(2, 0, False)
            outputs(1, 1, True)
            hidden(2, 0, False)
            with pe.Fori(3, rest + 3, 2) as g:
                for i, h in ((g, 1), (g + 1, 0)):
                    turn_rows(i, h, False)
                    outputs(i - 1, 1 - h, False)
                    hidden(i, h, False)
            turn_rows(rest + 3, 1, False)
            outputs(rest + 2, 0, False)
            hidden(rest + 3, 1, False)
            outputs(rest + 3, 1, False)

        @block.scalar
        def _(act_e):
            steps = [0]
            fn = nc.scalar.activation

            def link(ins):
                steps[0] += 1
                ins.then_inc(act_step, 1)
                act_e.wait_ge(act_step, steps[0])

            def emptying(ring, ins):
                ins.then_inc(free[ring, "a"], 1)

            load = act_e.dma_start
            load(cst[:, :], consts).then_inc(cst_in, 16)
            load(tok[:, :], token_ids).then_inc(cst_in, 16)
            load(lstep[64:96, :], log_step.rearrange("d (g h) -> (d g) h", h=2)).then_inc(srow_in, 16)
            load(srows[0:32, :], a_re.rearrange("d (g h) n -> (d g) (h n)", h=2)).then_inc(srow_in, 16)
            load(srows[32:64, :], a_im.rearrange("d (g h) n -> (d g) (h n)", h=2)).then_inc(srow_in, 16)
            for row, rows, src in ((R_G1, KT, norm1_g.rearrange("(r p) -> r p", p=P)),
                                   (R_CW, CONV * CT, conv_w.rearrange("w (r p) -> (w r) p", p=P)),
                                   (R_CB, CT, conv_b.rearrange("(r p) -> r p", p=P)),
                                   (R_BR, 2 * CT, b_r.rearrange("d (r p) -> (d r) p", p=P)),
                                   (R_BI, 2 * CT, b_i.rearrange("d (r p) -> (d r) p", p=P)),
                                   (R_LAM, 2 * CT, lam.rearrange("d (r p) -> (d r) p", p=P)),
                                   (R_BG, 2 * CT, b_glu.rearrange("(r p) -> r p", p=P))):
                load(prows[row:row + rows, :], src).then_inc(prow_in, 16)
            load(sink, attn_sink.partition_broadcast(P)).then_inc(prow_in, 16)
            load(dskip[:, :], d_skip.rearrange("(g q) -> q g", q=2 * C), allow_slow_non_contiguous=True).then_inc(dskip_in, 16)
            for t in range(NT):
                act_e.wait_ge(x_in, 16 * NT)
                fn(hn[:, t * D:(t + 1) * D], xt[:, t, :], ACT.Square, accum_out=ssq[:, t:t + 1]).then_inc(squares, 1)
            act_e.wait_ge(mean_ready, 1)
            fn(rstd, ssq, ACT.Sqrt).then_inc(root_ready, 1)
            act_e.wait_ge(srow_in, 16 * 3)
            fn(lstep[64:96, :], lstep[64:96, :], ACT.Exp).then_inc(step_exp, 1)
            bank = full_bank(act_e, "tp", "prm")
            emptying("tp", fn(prm[:, :], bank[:, 0:R_END], ACT.Copy))
            act_e.wait_ge(free["tp", "a"], 1)
            for k in range(0, KT, 2):
                bank = full_bank(act_e, "tp", ("x", k))
                emptying("tp", fn(hnv[:, k, :], bank[:, :], ACT.Identity, scale=prm[:, R_G1 + k:R_G1 + k + 1]))
            act_e.wait_ge(full["tp"], TP.index(("x", KT - 1)) + 1)
            for w, src in enumerate((w_r, w_i)):
                for h in range(2):
                    for d in range(2):
                        load(wri[h * LB:(h + 1) * LB, w, d],
                             src[d].rearrange("(c h) i j -> h i c j", h=2)[h]).then_inc(lru_w_in, 16)
            for r, src in enumerate((b_re, b_im)):
                for d in range(2):
                    load(bin_[:, r, d * GP:(d + 1) * GP, :],
                         src[d].rearrange("(g h) n c -> (h n) g c", h=2)).then_inc(early_in, 16)
            for r, src in enumerate((c_re, c_im)):
                for h in range(2):
                    load(crow[:, r, :, h, :], src.rearrange("(t g) c n -> (g c) t n", t=CT)).then_inc(early_in, 16)
            act_e.wait_ge(cl_arg, 1)
            fn(lt[:, 1, :], lt[:, 0, :], ACT.Exp).then_inc(cl_exp, 1)
            act_e.wait_ge(s5_arg, 1)
            fn(s5t[:, 1, :], s5t[:, 0, :], ACT.Exp).then_inc(s5_act, 1)
            act_e.wait_ge(s5_arg, 2)
            fn(cs[:, :, :], s5t[:, 2:4, :], ACT.Sin).then_inc(s5_act, 1)
            for n in range(CT):
                bank = full_bank(act_e, "big", ("u", n))
                emptying("big", fn(uT[:, n, :], bank[:, :], ACT.Copy))
            for n in range(CT):
                bank = full_bank(act_e, "big", ("xr", n))
                emptying("big", fn(xrv[:, n, 2:T + 2], bank[:, :], ACT.Copy))
            bank = full_bank(act_e, "big", "k")
            emptying("big", fn(kT, bank[:, :], ACT.Copy))
            bank = full_bank(act_e, "big", "v")
            emptying("big", fn(vS.rearrange("p t c -> p (t c)"), bank[:, :], ACT.Copy))
            for ct in range(CT):
                for half in range(2):
                    if ct:
                        act_e.wait_ge(full["tp"], TP.index(("U", ct - 1)) + 1)
                    bank = full_bank(act_e, "tp", ("x2", ct, half))
                    emptying("tp", fn(x2[:, :, half * 4:half * 4 + 4, :].rearrange("p g j c -> p j g c"),
                                      bank[0:NC, :].rearrange("p (j g c) -> p j g c", j=4, g=8), ACT.Copy))
            act_e.wait_ge(cl_ready, 1)
            for ct in range(CT):
                for j in range(2):
                    n = 2 * (ct % 2) + j
                    if ct < 2:
                        bank = full_bank(act_e, "big", ("gr", n))
                        emptying("big", fn(actv[:, 1, n, :], bank[:, :], ACT.Gelu_apprx_tanh))
                    else:
                        bank = full_bank(act_e, "big", ("q", n))
                        emptying("big", fn(qT[:, n, :], bank[:, :], ACT.Copy, scale=SCALE))
                if ct:
                    act_e.wait_ge(lru_out, ct)
                else:
                    act_e.wait_ge(xs_ready, NT)
                for w, dst, row in ((0, l_r, R_BR), (1, l_i, R_BI)):
                    for d in range(2):
                        bank = full_bank(act_e, "big", ("lru", ct, w, d))
                        col = row + d * CT + ct
                        emptying("big", fn(dst[:, d, :], bank[:, :], ACT.Sigmoid, bias=prm[:, col:col + 1]))
                act_e.wait_ge(*emptied("big", ("lru", ct, 0, 1)))
                for f, dst in ((ACT.Tanh, l_v), (ACT.Exp, l_a)):
                    for d in range(2):
                        fn(dst[:, d, :], l_r[:, d, :], f, scale=cl[:, d * CT + ct:d * CT + ct + 1]).then_inc(lru_ta, 1)
                act_e.wait_ge(lru_q, ct + 1)
                fn(l_q[:, :, :], l_v[:, :, :], ACT.Sqrt).then_inc(lru_s, 1)

            def softmax_exp(u):
                n = key_blocks(u // 2)[1]
                b = u % 2
                act_e.wait_ge(s_max, u + 1)
                for i in range(GQ):
                    fn(pr[:, b, i, 0:n * P], pr[:, b, i, 0:n * P], ACT.Exp, bias=anm[:, b, i:i + 1],
                       accum_out=asum[:, b, i:i + 1])
                fn(aes[:, b, :], aes[:, b, :], ACT.Exp).then_inc(s_exp, 1)

            def gate(b, d):
                n = gate_n[0]
                gate_n[0] += 1
                bank = full_bank(act_e, "big", ("g", b, d))
                if b == 2:
                    dst = sgate[:, d, :]
                else:
                    if n >= 2:
                        act_e.wait_ge(gate_used, n - 1)
                    dst = gbuf[:, n % 2, :]
                emptying("big", fn(dst, bank[:, :], ACT.Sigmoid))

            gate_n = [0]
            act_e.wait_ge(conv_done, CT)
            softmax_exp(0)
            for d in range(KT):
                if d + 1 < KT:
                    softmax_exp(d + 1)
                for k in range(0, key_blocks(d // 2)[1], 2):
                    if d:
                        act_e.wait_ge(full["big"], BIG.index(("pv", d - 1)) + 1)
                    bank = full_bank(act_e, "tp", ("p", d, k))
                    emptying("tp", fn(pT[:, k, :], bank[:, :], ACT.Copy))
                gate(1, d)
            for d in range(KT):
                if d % 2 == 0:
                    if d:
                        act_e.wait_ge(full["sc"], SC.index(("st", d - 1)) + 1)
                    for g4 in range(4):
                        bank = full_bank(act_e, "tp", ("w", 2 * d + g4))
                        emptying("tp", fn(wt[:, g4].rearrange("p d n -> p (d n)"), bank[:, :], ACT.Copy))
                gate(0, d)
            for d in range(KT):
                gate(2, d)
            for ct in range(CT):
                act_e.wait_ge(kx_ready, ct + 1)
                if ct:
                    act_e.wait_ge(full["big"], BIG.index(("y1", ct - 1, 1)) + 1)
                for j in range(L):
                    for h in range(2):
                        load(mm[j * C:(j + 1) * C].rearrange("p (g h) m -> p g h m", h=2)[:, :, h, :],
                             kx[h * C:(h + 1) * C, :, (L - 1 - j) * C:(L - 1 - j) * C + P]).then_inc(mm_in, 16)
                for h in range(2):
                    bank = full_bank(act_e, "big", ("y1", ct, h))
                    if ct:
                        act_e.wait_ge(full["tp"], TP.index(("y2", ct - 1, 1)) + 1)
                    emptying("big", fn(y1.rearrange("p (g h) k -> p g h k", h=2)[:, :, h, :],
                                       bank[:, 0:4 * NC].rearrange("p (g k) -> p g k", g=4), ACT.Copy))
                bank = full_bank(act_e, "tp", ("y3", ct))
                emptying("tp", fn(xcv[:, ct, :].rearrange("p (k j) -> p j k", j=L),
                                  bank[:, :].rearrange("p (j k) -> p j k", j=L), ACT.Gelu_apprx_tanh))
            for n in range(CT):
                bank = full_bank(act_e, "big", ("z1", n))
                if n == 0:
                    act_e.wait_ge(gate_used, 2 * KT)
                if n >= 2:
                    act_e.wait_ge(glu_ready, n - 1)
                emptying("big", fn(gbuf[:, n % 2, :], bank[:, :], ACT.Sigmoid, bias=prm[:, R_BG + CT + n:R_BG + CT + n + 1]))
            act_e.wait_ge(full["big"], BIG.index(("p", 2, KT - 1)) + 1)
            for t in range(NT):
                act_e.wait_ge(*emptied("big", ("wo", t, 1)))
                fn(act[:, t * D:(t + 1) * D], xt[:, t, :], ACT.Square, accum_out=ssq2[:, t:t + 1]).then_inc(x1_sq, 1)
                act_e.wait_ge(mean_ready, 2 + t)
                fn(rstd2[:, t:t + 1], ssq2[:, t:t + 1], ACT.Sqrt).then_inc(x1_root, 1)
            for t in range(NT):
                bank = full_bank(act_e, "tp", ("h2", t, 0))
                emptying("tp", fn(h2T[:, 0:4, t * P:(t + 1) * P], bank[:, :].rearrange("p (k s) -> p k s", k=4), ACT.Copy))
            act_e.wait_ge(w_arg, 1)
            fn(rg[3], rg[2], ACT.Exp).then_inc(w_exp, 1)
            act_e.wait_ge(w_arg, 2)
            fn(rs[8], rs[7], ACT.Exp).then_inc(w_exp, 1)

            act_e.wait_ge(n_ready, 1)
            rest = act_e.value_load(ntot[0:1, 0:1], min_val=E - 4, max_val=MAXR * E - 4)

            def rows_in(i, h, second):
                act_e.wait_ge(xg_turned, i + 1)
                if not second:
                    act_e.wait_ge(hid_full, i - 1)
                fn(xgT[:, h, 0:4, :], banks["tp"][0][:, :].rearrange("p (k s) -> p k s", k=4), ACT.Copy).then_inc(xgT_a, 1)

            def silu(i, h, second):
                act_e.wait_ge(hid_full, i + 1)
                if not second:
                    act_e.wait_ge(hh_ready, i - 1)
                fn(sg[:, h, :], banks["sc"][0][:, 0:FE], ACT.Silu).then_inc(silu_done, 1)

            def rows_done(i, h):
                act_e.wait_ge(y_full, i + 1)
                act_e.wait_ge(rows_out[h], (i - h) * 8)
                fn(yb[:, h, 0:512], banks["big"][2 * h][:, :], ACT.Copy).then_inc(yb_a, 1)

            act_e.wait_ge(full["sc"], SC.index("rank") + 1)
            rows_in(0, 0, True)
            silu(0, 0, True)
            rows_in(1, 1, True)
            rows_done(0, 0)
            silu(1, 1, True)
            rows_in(2, 0, False)
            rows_done(1, 1)
            silu(2, 0, False)
            with act_e.Fori(3, rest + 3, 2) as g:
                for i, h in ((g, 1), (g + 1, 0)):
                    rows_in(i, h, False)
                    rows_done(i - 1, 1 - h)
                    silu(i, h, False)
            rows_in(rest + 3, 1, False)
            rows_done(rest + 2, 0)
            silu(rest + 3, 1, False)
            rows_done(rest + 3, 1)
            for t in range(NT):
                act_e.wait_ge(acc_ready, t + 1)
                fn(act[:, t * D:(t + 1) * D], xt[:, t, :], ACT.Square, accum_out=ssq3[:, t:t + 1]).then_inc(out_sq, 1)
                act_e.wait_ge(mean_ready, 2 + NT + t)
                fn(rstd3[:, t:t + 1], ssq3[:, t:t + 1], ACT.Sqrt).then_inc(out_root, 1)

        @block.vector
        def _(dve):
            steps = [0]
            tt, ts, stt = nc.vector.tensor_tensor, nc.vector.tensor_scalar, nc.vector.scalar_tensor_tensor

            def link(ins):
                steps[0] += 1
                ins.then_inc(dve_step, 1)
                dve.wait_ge(dve_step, steps[0])

            def emptying(ring, ins):
                ins.then_inc(free[ring, "v"], 1)

            dve.wait_ge(squares, NT)
            ts(ssq, ssq, 1.0 / D, EPS, MUL, ADD).then_inc(mean_ready, 1)
            dve.wait_ge(root_ready, 1)
            link(nc.vector.reciprocal(rstd, rstd))
            for t in range(NT):
                ts(xs[:, t, :], xt[:, t, :], rstd[:, t:t + 1], None, MUL).then_inc(xs_ready, 1)
            dve.wait_ge(step_exp, 1)
            nc.vector.tensor_copy(srows[64:96, :].rearrange("p (h n) -> p h n", h=2), bc(lstep[64:96, :], 2, N)).then_inc(srows_ready, 1)
            bank = full_bank(dve, "tp", "s5p")
            emptying("tp", nc.vector.tensor_copy(s5p[:, :], bank[:, 0:96]))
            dve.wait_ge(*emptied("tp", "prm"))
            for k in range(1, KT, 2):
                bank = full_bank(dve, "tp", ("x", k))
                emptying("tp", ts(hnv[:, k, :], bank[:, :], prm[:, R_G1 + k:R_G1 + k + 1], None, MUL))
            lm = prm[:, R_LAM:R_LAM + 2 * CT]
            stt(lt[:, 0, :], lm, -1.0, lm, MUL, ALU.min).then_inc(cl_arg, 1)
            dve.wait_ge(cl_exp, 1)
            link(ts(lt[:, 2, :], lt[:, 1, :], 2.0, None, ADD))
            link(nc.vector.reciprocal(lt[:, 2, :], lt[:, 2, :]))
            link(tt(lt[:, 0, :], lt[:, 1, :], lt[:, 2, :], MUL))
            link(tt(lt[:, 1, :], lt[:, 0, :], lt[:, 0, :], MUL))
            link(ts(lt[:, 2, :], lt[:, 1, :], 1.0 / 15, None, MUL))
            for m in (13, 11, 9, 7, 5, 3):
                link(stt(lt[:, 2, :], lt[:, 2, :], 1.0 / m, lt[:, 1, :], ADD, MUL))
            link(stt(lt[:, 2, :], lt[:, 2, :], 1.0, lt[:, 0, :], ADD, MUL))
            link(ts(lt[:, 3, :], lm, -1.0, 0.0, MUL, MAX))
            link(stt(lt[:, 3, :], lt[:, 2, :], 2.0, lt[:, 3, :], MUL, ADD))
            ts(cl, lt[:, 3, :], -LRU_C, None, MUL).then_inc(cl_ready, 1)
            ar, ai, st = s5p[:, 0:32], s5p[:, 32:64], s5p[:, 64:96]
            q = [s5t[:, i, :] for i in range(16)]
            dve.wait_ge(*emptied("tp", "s5p"))
            tt(q[0], ar, st, MUL).then_inc(s5_arg, 1)
            link(tt(q[4], ai, st, MUL))
            big = 1.5 * 2.0 ** 23
            link(ts(q[5], q[4], 1.0 / (2 * np.pi), big, MUL, ADD))
            link(ts(q[5], q[5], -big, None, ADD))
            c1 = 6.28125
            c2 = float(np.float32(np.round((2 * np.pi - c1) * 2.0 ** 20) / 2.0 ** 20))
            for c in (c1, c2, 2 * np.pi - c1 - c2):
                link(stt(q[4], q[5], -c, q[4], MUL, ADD))
            link(ts(q[3], q[4], 3.1415925, -3.1415925, ALU.min, MAX))
            link(stt(q[2], q[3], -1.0, q[3], MUL, ALU.min))
            ts(q[2], q[2], float(np.pi / 2), None, ADD).then_inc(s5_arg, 1)
            dve.wait_ge(s5_act, 2)
            link(tt(pw[:, 0, 1, :], q[1], cs[:, 0, :], MUL))
            link(tt(pw[:, 1, 1, :], q[1], cs[:, 1, :], MUL))
            link(nc.vector.memset(pw[:, 0, 0, :], 1.0))
            link(nc.vector.memset(pw[:, 1, 0, :], 0.0))
            nr, ni = q[5], pw[:, 1, 1, :]
            link(ts(nr, pw[:, 0, 1, :], -1.0, None, ADD))
            link(tt(q[6], ar, ar, MUL))
            link(tt(q[7], ai, ai, MUL))
            link(tt(q[6], q[6], q[7], ADD))
            link(nc.vector.reciprocal(q[6], q[6]))
            link(tt(q[7], nr, ar, MUL))
            link(tt(q[8], ni, ai, MUL))
            link(tt(q[7], q[7], q[8], ADD))
            link(tt(q[7], q[7], q[6], MUL))
            link(tt(q[8], ni, ar, MUL))
            link(tt(q[9], nr, ai, MUL))
            link(tt(q[8], q[8], q[9], SUB))
            link(tt(q[8], q[8], q[6], MUL))
            dve.wait_ge(early_in, 16 * 8)
            sr, si = bc(q[7], 2, C), bc(q[8], 2, C)
            bbv = bb[:, :, :, :].rearrange("p (d r) g c -> p d r g c", d=2)
            bt = [btmp[:, a].rearrange("p (d g) c -> p d g c", d=2) for a in range(2)]
            for r, (x0, x1, op) in enumerate(((0, 1, SUB), (1, 0, ADD))):
                link(tt(btmp[:, 0], sr, bin_[:, x0], MUL))
                link(tt(btmp[:, 1], si, bin_[:, x1], MUL))
                link(tt(bbv[:, :, r], bt[0], bt[1], op))
            for lo, n, by in ((1, 1, 1), (1, 2, 2), (1, 4, 4)):
                xr_, xi_ = pw[:, 0, lo:lo + n, :], pw[:, 1, lo:lo + n, :]
                yr_, yi_ = bc(pw[:, 0, by, :], 1, n), bc(pw[:, 1, by, :], 1, n)
                dst = slice(lo + by, lo + by + n)
                ta = s5t[:, 8:8 + n, :]
                tb = s5t[:, 12:12 + n, :]
                link(tt(ta, xr_, yr_, MUL))
                link(tt(tb, xi_, yi_, MUL))
                link(tt(pw[:, 0, dst, :], ta, tb, SUB))
                link(tt(ta, xr_, yi_, MUL))
                link(tt(tb, xi_, yr_, MUL))
                link(tt(pw[:, 1, dst, :], ta, tb, ADD))
            for d in range(2):
                cols = slice(d * GP, (d + 1) * GP)
                link(nc.vector.tensor_copy(aa[:, 0, 2 * d, :], pw[:, 0, L, cols]))
                link(nc.vector.tensor_copy(aa[:, 0, 2 * d + 1, :], pw[:, 0, L, cols]))
                link(nc.vector.tensor_copy(aa[:, 1, 2 * d, :], pw[:, 1, L, cols]))
                link(ts(aa[:, 1, 2 * d + 1, :], pw[:, 1, L, cols], -1.0, None, MUL))
            dve.wait_ge(dskip_in, 16)
            tt(dd[:, :, :], bc(dskip[:, :], 2, C), bc(cst[0:2 * C, K_DLT:K_DLT + C], 1, GP), MUL).then_inc(s5_tab, 1)
            for r in range(2):
                bank = full_bank(dve, "tp", ("c", r))
                for h in range(2):
                    rows = slice(h * N, (h + 1) * N)
                    src = bank[rows, :].rearrange("p (g h c) -> p g h c", h=2, c=C)[:, :, h, :]
                    ins = nc.vector.tensor_copy(cc[rows, r], src)
                emptying("tp", ins)
            dve.wait_ge(pad_zero, 2)
            for ct in range(CT):
                dve.wait_ge(*emptied("big", ("xr", ct)))
                w = [prm[:, R_CW + i * CT + ct:R_CW + i * CT + ct + 1] for i in range(CONV)]
                link(ts(xcv[:, ct, :], xrv[:, ct, 0:T], w[0], prm[:, R_CB + ct:R_CB + ct + 1], MUL, ADD))
                for i in range(1, CONV - 1):
                    link(stt(xcv[:, ct, :], xrv[:, ct, i:i + T], w[i], xcv[:, ct, :], MUL, ADD))
                stt(xcv[:, ct, :], xrv[:, ct, 3:3 + T], w[3], xcv[:, ct, :], MUL, ADD).then_inc(conv_done, 1)
            for ct in range(CT):
                bank = full_bank(dve, "tp", ("U", ct))
                emptying("tp", nc.vector.tensor_copy(Uv[:, 8 * ct:8 * ct + 8, :].rearrange("p g k -> p (g k)"), bank[:, :]))
            dve.wait_ge(conv_done, CT)
            for ct in range(CT):
                dve.wait_ge(*emptied("big", ("lru", ct, 1, 1)))
                tt(l_i[:, :, :], l_i[:, :, :], bc(xcv[:, ct, :], 1, 2), MUL)
                dve.wait_ge(lru_ta, 4 * ct + 2)
                link(ts(l_q[:, :, :], l_v[:, :, :], -1.0, 1.0, MUL, ADD))
                link(nc.vector.reciprocal(l_q[:, :, :], l_q[:, :, :]))
                stt(l_v[:, :, :], l_v[:, :, :], -2.0, l_q[:, :, :], MUL, MUL).then_inc(lru_q, 1)
                dve.wait_ge(lru_s, ct + 1)
                dve.wait_ge(lru_ta, 4 * ct + 4)
                link(tt(l_i[:, :, :], l_i[:, :, :], l_q[:, :, :], MUL))
                nc.vector.tensor_tensor_scan(l_v[:, 0, :], l_a[:, 0, :], l_i[:, 0, :], 0.0, MUL, ADD)
                link(nc.vector.tensor_tensor_scan(l_v[:, 1, ::-1], l_a[:, 1, ::-1], l_i[:, 1, ::-1], 0.0, MUL, ADD))
                link(tt(l_v[:, 0, :], l_v[:, 0, :], l_v[:, 1, :], ADD))
                dve.wait_ge(*emptied("big", ("gr", ct)))
                tt(actv[:, 1, ct, :], actv[:, 1, ct, :], l_v[:, 0, :], MUL).then_inc(lru_out, 1)

            dve.wait_ge(btab_ready, NQ)
            dve.wait_ge(prow_in, 16 * 8)

            def softmax_max(u):
                nb, hk = u // 2, u % 2
                lo, n = key_blocks(nb)
                off = (lo - nb + 1) * P
                b = u % 2
                for i in range(GQ):
                    bank = full_bank(dve, "sc", ("s", u, i))
                    h = hk * GQ + i
                    if i == 0 and u >= 2:
                        dve.wait_ge(full["tp"], TP.index(("p", u - 2, key_blocks((u - 2) // 2)[1] - 1)) + 1)
                    emptying("sc", nc.vector.tensor_tensor_reduce(
                        out=pr[:, b, i, 0:n * P], in0=bank[:, 0:n * P], in1=btab[:, h, off:off + n * P], scale=1.0,
                        scalar=sink[:, h:h + 1], op0=ADD, op1=MAX, accum_out=am[:, b, i:i + 1]))
                dve.wait_ge(*emptied("sc", ("s", u, GQ - 1)))
                ts(anm[:, b, :], am[:, b, :], -1.0, None, MUL)
                tt(aes[:, b, :], sink[:, hk * GQ:(hk + 1) * GQ], am[:, b, :], SUB).then_inc(s_max, 1)

            def softmax_scale(u):
                n = key_blocks(u // 2)[1]
                b = u % 2
                dve.wait_ge(s_exp, u + 1)
                link(tt(ard[:, b, :], asum[:, b, :], aes[:, b, :], ADD))
                link(nc.vector.reciprocal(ard[:, b, :], ard[:, b, :]))
                for i in range(GQ):
                    ins = ts(pr[:, b, i, 0:n * P], pr[:, b, i, 0:n * P], ard[:, b, i:i + 1], None, MUL)
                ins.then_inc(s_prob, 1)

            gate_n = [0]

            def gated(b, d):
                bank = full_bank(dve, "big", ("p", b, d))
                dve.wait_ge(*emptied("big", ("g", b, d)))
                g = sgate[:, d, :] if b == 2 else gbuf[:, gate_n[0] % 2, :]
                gate_n[0] += 1
                if b == 1:
                    emptying("big", tt(mixed[:, d, :], bank[:, :], g, MUL))
                    dve.wait_ge(*emptied("big", ("p", b, d)))
                    dve.nop().then_inc(gate_used, 1)
                else:
                    emptying("big", tt(g, bank[:, :], g, MUL))
                    dve.wait_ge(*emptied("big", ("p", b, d)))
                    tt(mixed[:, d, :], mixed[:, d, :], g, ADD).then_inc(gate_used, 1)

            softmax_max(0)
            softmax_scale(0)
            for d in range(KT):
                if d + 1 < KT:
                    softmax_max(d + 1)
                for k in range(1, key_blocks(d // 2)[1], 2):
                    if d:
                        dve.wait_ge(full["big"], BIG.index(("pv", d - 1)) + 1)
                    bank = full_bank(dve, "tp", ("p", d, k))
                    emptying("tp", nc.vector.tensor_copy(pT[:, k, :], bank[:, :]))
                if d + 1 < KT:
                    softmax_scale(d + 1)
                rows = slice((d % 2) * HD, (d % 2 + 1) * HD)
                bank = full_bank(dve, "big", ("pv", d))
                emptying("big", nc.vector.tensor_copy(actv[rows, 0, :, (d // 2) * P:(d // 2 + 1) * P],
                                                      bank[rows, :].rearrange("p (i q) -> p i q", i=GQ)))
                gated(1, d)
            dve.wait_ge(x_zero, 1)
            for d in range(KT):
                bank = full_bank(dve, "sc", ("st", d))
                emptying("sc", nc.vector.tensor_copy(Xv[:, :, 2 * d:2 * d + 2, 1:NC + 1],
                                                     bank[:, :].rearrange("p (q g k) -> p q g k", q=4, g=2)))
                gated(0, d)

            def c_powers(ct):
                b = ct % 2
                if ct >= 2:
                    dve.wait_ge(full["big"], BIG.index(("y1", ct - 2, 1)) + 1)
                tv = [t.rearrange("p (g j c) -> p g j c", g=4, j=L + 1) for t in (tmpC, tmpD)]
                for d in range(2):
                    cols = slice(d * GP + 4 * ct, d * GP + 4 * ct + 4)

                    def power(r):
                        rows = pw[:, r, 0:L + 1, cols] if d == 0 else pw[:, r, L::-1, cols]
                        return bc(rows.rearrange("p j g -> p g j"), 3, C)

                    def c_of(r):
                        return bc(cc[:, r, 4 * ct:4 * ct + 4, :], 2, L + 1)

                    link(tt(tv[0], power(0), c_of(0), MUL))
                    link(tt(tv[1], power(1), c_of(1), MUL))
                    link(tt(cp[:, b, 2 * d].rearrange("p g m -> p (g m)"), tmpC, tmpD, SUB))
                    link(tt(tv[0], power(0), c_of(1), MUL))
                    link(tt(tv[1], power(1), c_of(0), MUL))
                    stt(cp[:, b, 2 * d + 1].rearrange("p g m -> p (g m)"), tmpC, -1.0, tmpD, MUL, SUB).then_inc(cp_ready, 1)
                    dve.wait_ge(cp_ready, 2 * ct + d + 1)
                if ct:
                    dve.wait_ge(full["sc"], SC.index(("kb", ct - 1)) + 1)
                for h in range(2):
                    rows = slice(h * N, (h + 1) * N)
                    nc.vector.tensor_copy(bbd[rows, :, :, h, :], bb[rows, :, 4 * ct:4 * ct + 4, :]).then_inc(bbd_ready, 1)

            def lag_kernels(ct):
                kf = full_bank(dve, "sc", ("kf", ct))[0:2 * C, :].rearrange("p (g m) -> p g m", g=4)
                kb = full_bank(dve, "sc", ("kb", ct))[0:2 * C, :].rearrange("p (g m) -> p g m", g=4)
                if ct:
                    dve.wait_ge(mm_in, 16 * 2 * L * ct)
                link(nc.vector.tensor_copy(kx[:, :, (L - 1) * C:], kf))
                emptying("sc", tt(kx[:, :, (L - 1) * C:L * C], kx[:, :, (L - 1) * C:L * C], kb[:, :, (L - 1) * C:], ADD))
                emptying("sc", nc.vector.tensor_copy(kx[:, :, 0:(L - 1) * C], kb[:, :, 0:(L - 1) * C]))
                dve.wait_ge(*emptied("sc", ("kb", ct)))
                tt(kx[:, :, (L - 1) * C:L * C], kx[:, :, (L - 1) * C:L * C], dd[:, 4 * ct:4 * ct + 4, :], ADD).then_inc(kx_ready, 1)

            link(nc.vector.memset(xrp[:, 1024:1536], 0.0))
            c_powers(0)
            lag_kernels(0)
            c_powers(1)
            for ct in range(CT):
                if ct + 1 < CT:
                    lag_kernels(ct + 1)
                for half in range(2):
                    if ct and half == 0:
                        dve.wait_ge(full["tp"], TP.index(("y3", ct - 1)) + 1)
                    bank = full_bank(dve, "tp", ("y2", ct, half))
                    emptying("tp", nc.vector.tensor_copy(
                        y2[:, :, 4 * half:4 * half + 4, :].rearrange("p j g c -> p g j c"),
                        bank[0:NC, :].rearrange("p (g j c) -> p g j c", g=4, j=L)))
                if ct + 2 < CT:
                    c_powers(ct + 2)
            for n in range(CT):
                bank = full_bank(dve, "big", ("z0", n))
                dve.wait_ge(*emptied("big", ("z1", n)))
                col = prm[:, R_BG + n:R_BG + n + 1]
                ins = stt(actv[:, 2, n, :], bank[:, :], col, gbuf[:, n % 2, :], ADD, MUL)
                emptying("big", ins)
                dve.wait_ge(*emptied("big", ("z0", n)))
                dve.nop().then_inc(glu_ready, 1)
            for d in range(KT):
                gated(2, d)
            dve.wait_ge(x_again, 16 * NT)
            dve.wait_ge(late_in, 16 * 6)
            for t in range(NT):
                for h in range(2):
                    bank = full_bank(dve, "big", ("wo", t, h))
                    half = xt[:, t, h * 512:(h + 1) * 512]
                    emptying("big", tt(half, bank[:, :], half, ADD))
                dve.wait_ge(x1_sq, t + 1)
                ts(ssq2[:, t:t + 1], ssq2[:, t:t + 1], 1.0 / D, EPS, MUL, ADD).then_inc(mean_ready, 1)
                dve.wait_ge(x1_root, t + 1)
                link(nc.vector.reciprocal(rstd2[:, t:t + 1], rstd2[:, t:t + 1]))
                stt(h2[:, t, :], xt[:, t, :], rstd2[:, t:t + 1], g2b, MUL, MUL).then_inc(h2_ready, 1)
            for t in range(NT):
                if t == 0:
                    dve.wait_ge(full["big"], BIG.index(("wo", NT - 1, 1)) + 1)
                bank = full_bank(dve, "tp", ("h2", t, 1))
                emptying("tp", nc.vector.tensor_copy(h2T[:, 4:8, t * P:(t + 1) * P], bank[:, :].rearrange("p (k s) -> p k s", k=4)))
            lg = xc[:, 960:1040].rearrange("p (t c) -> p t c", t=NT)
            bank = full_bank(dve, "sc", "logits")
            emptying("sc", tt(lg, bank[:, 0:NT * (NGRP + E)].rearrange("p (t c) -> p t c", t=NT), bc(bge, 1, NT), ADD))
            dve.wait_ge(*emptied("sc", "logits"))
            lgg, lge = lg[:, :, 0:NGRP], lg[:, :, NGRP:]

            def top(mask, values, peak, score, rank, n):
                link(nc.vector.tensor_reduce(peak, values, AX.X, MAX))
                link(tt(score, values, bc(peak, 2, n), ALU.is_equal))
                link(tt(score, score, bc(cst[:, K_REV:K_REV + n], 1, NT), MUL))
                link(nc.vector.tensor_reduce(rank, score, AX.X, MAX))
                link(tt(mask, score, bc(rank, 2, n), ALU.is_equal))

            top(rg[1], lgg, rs[0], rg[0], rs[1], NGRP)
            tt(rg[2], lgg, bc(rs[0], 2, NGRP), SUB).then_inc(w_arg, 1)
            link(ts(rg[4], rg[1], -NEG, NEG, MUL, ADD))
            g4 = "p t (g e) -> p t g e"
            link(tt(rt[1].rearrange(g4, g=NGRP), lge.rearrange(g4, g=NGRP), bc(rg[1], 3, 4), MUL))
            link(tt(rt[1].rearrange(g4, g=NGRP), rt[1].rearrange(g4, g=NGRP), bc(rg[4], 3, 4), ADD))
            top(rt[3], rt[1], rs[2], rt[2], rs[3], E)
            link(stt(rt[4], rt[3], 2 * NEG, rt[1], MUL, ADD))
            top(rt[5], rt[4], rs[4], rt[2], rs[5], E)
            tt(rs[7], rs[4], rs[2], SUB).then_inc(w_arg, 1)
            tt(rt[7], rt[3], rt[5], ADD).then_inc(mask_ready, 1)
            dve.wait_ge(w_exp, 2)
            link(nc.vector.tensor_reduce(rs[9], rg[3], AX.X, ADD))
            link(ts(rs[10], rs[8], 1.0, None, ADD))
            link(tt(rs[10], rs[10], rs[9], MUL))
            link(nc.vector.reciprocal(rs[11], rs[10]))
            link(tt(rs[12], rs[11], rs[8], MUL))
            bank = full_bank(dve, "sc", "rank")
            link(nc.vector.tensor_copy(rt[8], bank[:, 0:NT * E].rearrange("p (t e) -> p t e", t=NT)))
            cnt = rs[13][0:1, 0:1]
            rounds = rs[14][0:1, 0:1]
            part = rs[15][0:1, 0:1]
            emptying("sc", nc.vector.tensor_reduce(cnt, bank[0:1, NT * E:(NT + 1) * E], AX.X, MAX))
            dve.wait_ge(*emptied("sc", "rank"))
            link(ts(rounds, cnt, P + 0.5, 1.0, ALU.is_gt, ADD))
            link(ts(rt[9], rt[8], P - 0.5, float(ROUND - P), ALU.is_gt, MUL))
            for r in range(2, MAXR):
                link(ts(part, cnt, r * P + 0.5, None, ALU.is_gt))
                link(tt(rounds, rounds, part, ADD))
                link(ts(rt[10], rt[8], r * P - 0.5, float(ROUND - P), ALU.is_gt, MUL))
                link(tt(rt[9], rt[9], rt[10], ADD))
            link(ts(rounds, rounds, float(E), -4.0, MUL, ADD))
            nc.vector.tensor_copy(ntot[0:1, 0:1], rounds).then_inc(n_ready, 1)
            link(tt(rt[8], rt[8], rt[9], ADD))
            link(tt(rt[8], rt[8], bc(cst[:, K_E128:K_E128 + E], 1, NT), ADD))
            for c, mask in enumerate((rt[3], rt[5])):
                link(tt(rt[10], rt[8], mask, MUL))
                link(nc.vector.tensor_reduce(rs[5], rt[10], AX.X, ADD))
                nc.vector.tensor_copy(slot_i[:, c, :], rs[5]).then_inc(slots_ready, 1)
                dve.wait_ge(slots_ready, c + 1)

            rest = dve.value_load(ntot[0:1, 0:1], min_val=E - 4, max_val=MAXR * E - 4)

            def rows_in(i, h, second):
                dve.wait_ge(xg_turned, i + 1)
                if not second:
                    dve.wait_ge(hid_full, i - 1)
                nc.vector.tensor_copy(xgT[:, h, 4:8, :], banks["tp"][1][:, :].rearrange("p (k s) -> p k s", k=4)).then_inc(xgT_v, 1)

            def gated_hidden(i, h):
                dve.wait_ge(silu_done, i + 1)
                tt(hh[:, h, :], banks["sc"][0][:, FE:2 * FE], sg[:, h, :], MUL).then_inc(hh_ready, 1)

            def hidden_turned(i, h):
                dve.wait_ge(hT_full, i + 1)
                nc.vector.tensor_copy(hT[:, h].rearrange("p k s -> p (k s)"), banks["sc"][1][:, 0:2 * P]).then_inc(hT_ready, 1)

            def rows_done(i, h):
                dve.wait_ge(y_full, i + 1)
                dve.wait_ge(rows_out[h], (i - h) * 8)
                nc.vector.tensor_copy(yb[:, h, 512:1024], banks["big"][2 * h + 1][:, :]).then_inc(yb_v, 1)

            rows_in(0, 0, True)
            gated_hidden(0, 0)
            rows_in(1, 1, True)
            hidden_turned(0, 0)
            rows_done(0, 0)
            gated_hidden(1, 1)
            rows_in(2, 0, False)
            hidden_turned(1, 1)
            rows_done(1, 1)
            gated_hidden(2, 0)
            with dve.Fori(3, rest + 3, 2) as g:
                for i, h in ((g, 1), (g + 1, 0)):
                    rows_in(i, h, False)
                    hidden_turned(i - 1, 1 - h)
                    rows_done(i - 1, 1 - h)
                    gated_hidden(i, h)
            rows_in(rest + 3, 1, False)
            hidden_turned(rest + 2, 0)
            rows_done(rest + 2, 0)
            gated_hidden(rest + 3, 1)
            hidden_turned(rest + 3, 1)
            rows_done(rest + 3, 1)
            for t in range(NT):
                dve.wait_ge(yg_in[t], 32)
                for c in range(2):
                    src = (hn, mix)[c][:, t * D:(t + 1) * D]
                    ins = stt(xt[:, t, :], src, rs[11 + c][:, t:t + 1], xt[:, t, :], MUL, ADD)
                    if c:
                        ins.then_inc(acc_ready, 1)
                    else:
                        link(ins)
                dve.wait_ge(out_sq, t + 1)
                ts(ssq3[:, t:t + 1], ssq3[:, t:t + 1], 1.0 / D, EPS, MUL, ADD).then_inc(mean_ready, 1)
                dve.wait_ge(out_root, t + 1)
                link(nc.vector.reciprocal(rstd3[:, t:t + 1], rstd3[:, t:t + 1]))
                stt(xt[:, t, :], xt[:, t, :], rstd3[:, t:t + 1], fgb, MUL, MUL).then_inc(out_ready, 1)


_LAYERED = ["norm1_g", "w_in", "attn_sink", "lru_conv_w", "lru_conv_b", "lru_w_r", "lru_b_r", "lru_w_i", "lru_b_i",
            "lru_lambda", "ssm_a_re", "ssm_a_im", "ssm_log_step", "ssm_b_re", "ssm_b_im", "ssm_c_re", "ssm_c_im",
            "ssm_d", "ssm_w_glu", "ssm_b_glu", "w_branch", "w_out", "norm2_g", "moe_w_group", "moe_b_group",
            "moe_w_expert", "moe_b_expert", "moe_w1", "moe_w3", "moe_w2"]


def kernel(**inputs):
    import concourse.bacc as bacc
    from concourse.bass_utils import run_bass_kernel_spmd

    arrays = {"x": inputs["x"][0]}
    for name in _LAYERED:
        a = np.asarray(inputs[name])[0]
        if name.startswith("moe_w") and a.ndim == 4:
            a = a.reshape((E,) + a.shape[2:])
        arrays[name] = a
    arrays["final_norm_g"] = inputs["final_norm_g"]
    arrays["consts"], arrays["token_ids"] = constants()

    nc = bacc.Bacc("TRN2", target_bir_lowering=False, num_devices=1)
    ins, args = {}, []
    for name, a in arrays.items():
        a = np.ascontiguousarray(a)
        ins[f"in_{name}"] = a
        args.append(nc.dram_tensor(f"in_{name}", a.shape, mybir.dt.from_np(a.dtype), kind="ExternalInput").ap())
    args.append(nc.dram_tensor("out_0", (T, D), mybir.dt.float32, kind="ExternalOutput").ap())
    hybrid_block(nc, *args)
    r = run_bass_kernel_spmd(nc, [ins], core_ids=[0])
    return r.results[0]["out_0"].reshape(1, T, D)
```

```python
import numpy as np
import concourse.bass as bass
from concourse import mybir
from contextlib import ExitStack

T, D = 512, 1024
P = 128
NT, KT = T // P, D // P
NQ, NKV, HD = 8, 2, 64
GQ = NQ // NKV
BW = D // 2
CT = BW // P
NBR = 3
COL_K, COL_V = BW, BW + NKV * HD
COL_XR = BW + 2 * NKV * HD
COL_GR, COL_U = COL_XR + BW, COL_XR + 2 * BW
COL_GATE = COL_XR + 3 * BW
CONV = 4
LB = 64
LRU_C = 8.0
G, C, N = 32, 16, 64
L = 8
NC = T // L
GP = G // 2
E, FE, NGRP = 16, 256, 4
SLAB = 2048
ROUND = E * P
MAXR = T // P
EPS = 1e-6
NEG = -1e30
SCALE = HD ** -0.5

K_ID, K_DIST, K_TRI, K_ONE, K_E128, K_REV, K_DLT, K_END = 0, 128, 512, 640, 768, 784, 800, 816

R_G1, R_CW, R_CB, R_BR, R_BI, R_LAM, R_BG, R_END = 0, 8, 24, 28, 36, 44, 52, 60


def constants():
    c = np.zeros((P, K_END), np.float32)
    p = np.arange(P)
    c[:, K_ID:K_ID + P] = np.eye(P)
    rel = p[:, None] - np.arange(3 * P)[None, :] + P
    c[:, K_DIST:K_DIST + 3 * P] = np.where(np.abs(rel) <= P, -np.abs(rel), NEG * 256.0)
    c[:, K_TRI:K_TRI + P] = p[:, None] < p[None, :]
    c[:, K_ONE:K_ONE + P] = 1.0
    c[:, K_E128:K_E128 + E] = np.arange(E) * P
    c[:, K_REV:K_REV + E] = E - np.arange(E)
    c[:, K_DLT:K_DLT + C] = (p[:, None] % C) == np.arange(C)[None, :]
    token = p[:, None, None] + P * np.arange(NT)[None, None, :] + 0 * np.arange(2)[None, :, None]
    ids = np.stack([token, 2 * token + np.arange(2)[None, :, None]], axis=-1).astype(np.int32)
    return c, ids



class Ring:

    def __init__(self, size):
        self.size, self.jobs = size, []

    def add(self, key, by):
        self.jobs.append((key, by))

    def index(self, key):
        return next(n for n, (k, _) in enumerate(self.jobs) if k == key)

    def emptied(self, n):
        by = self.jobs[n][1]
        return by, sum(1 for _, b in self.jobs[:n + 1] if b == by)


def key_blocks(nb):
    lo, hi = max(0, nb - 1), min(NT - 1, nb + 1)
    return lo, hi - lo + 1


SSM_STEPS = {
    (0, 1): [("K", 0)], (0, 2): [("M", 0)], (0, 3): [("K", 1)], (0, 4): [("M", 1), ("Y1", 0)], (0, 5): [("Y2", 0)],
    (0, 6): [("Y3", 0)], (0, 7): [("K", 2), ("Y1", 1)],
    (2, 0): [("M", 2), ("Y2", 1)], (2, 1): [("Y3", 1)], (2, 2): [("K", 3), ("Y1", 2)], (2, 3): [("M", 3), ("Y2", 2)],
    (2, 4): [("Y3", 2)], (2, 5): [("Y1", 3)], (2, 6): [("Y2", 3)], (2, 7): [("Y3", 3)],
}
C_POWERS = {(0, 0): 0, (0, 2): 1, (0, 6): 2, (2, 1): 3}


def gates_order():
    order = [("u", n) for n in range(CT)] + [("xr", n) for n in range(CT)] + ["k", "v"]
    order += [("gr", n) for n in range(CT)] + [("q", n) for n in range(CT)]
    return order + [("g", b, d) for b in (1, 0, 2) for d in range(KT)]


def plan():
    big, tp, sc = Ring(4), Ring(2), Ring(2)
    tp.add("prm", "a")
    tp.add("s5p", "v")
    for k in range(KT):
        tp.add(("x", k), "v")
    for n in range(CT):
        big.add(("u", n), "a")
    for n in range(CT):
        big.add(("xr", n), "a")
    big.add("k", "a")
    big.add("v", "a")
    for r in range(2):
        tp.add(("c", r), "v")
    for ct in range(CT):
        for half in range(2):
            tp.add(("x2", ct, half), "a")
        tp.add(("U", ct), "v")
    for ct in range(CT):
        for j in range(2):
            big.add(("gr" if ct < 2 else "q", 2 * (ct % 2) + j), "a")
        for g4 in range(4):
            tp.add(("w", ct, g4), "a")
        for h in range(2):
            sc.add(("st", 2 * ct + h), "v")
        for w in range(2):
            for d in range(2):
                big.add(("lru", ct, w, d), "a")
    for i in range(GQ):
        sc.add(("s", 0, i), "v")
    for d in range(KT):
        for i in range(GQ if d + 1 < KT else 0):
            sc.add(("s", d + 1, i), "v")
        for k in range(key_blocks(d // 2)[1]):
            tp.add(("p", d, k), "av"[k % 2])
        big.add(("g", 1, d), "a")
        big.add(("pv", d), "v")
        big.add(("p", 1, d), "v")
    for b in (0, 2):
        for d in range(KT):
            big.add(("g", b, d), "a")
            if b == 0:
                big.add(("p", 0, d), "v")
            for step, ct in SSM_STEPS.get((b, d), []):
                if step == "K":
                    sc.add(("kf", ct), "v")
                    sc.add(("kb", ct), "v")
                if step == "Y1":
                    for h in range(2):
                        big.add(("y1", ct, h), "a")
                if step == "Y2":
                    tp.add(("y2", ct, 0), "v")
                    tp.add(("y2", ct, 1), "v")
                if step == "Y3":
                    tp.add(("y3", ct), "a")
    for n in range(CT):
        big.add(("z1", n), "a")
        big.add(("z0", n), "v")
    for d in range(KT):
        big.add(("p", 2, d), "v")
    for t in range(NT):
        for h in range(2):
            big.add(("wo", t, h), "v")
    for t in range(NT):
        for h in range(2):
            tp.add(("h2", t, h), "av"[h])
    sc.add("logits", "v")
    sc.add("rank", "v")
    return big, tp, sc


def hybrid_block(nc, x, norm1_g, w_in, attn_sink, conv_w, conv_b, w_r, b_r, w_i, b_i, lam,
                 a_re, a_im, log_step, b_re, b_im, c_re, c_im, d_skip, w_glu, b_glu, w_branch,
                 w_out, norm2_g, w_group, b_group, w_expert, b_expert, w1, w3, w2, final_g,
                 consts, token_ids, out, probe=None):
    f32, i32, f32r = mybir.dt.float32, mybir.dt.int32, mybir.dt.float32r
    ALU, ACT, AX = mybir.AluOpType, mybir.ActivationFunctionType, mybir.AxisListType
    MUL, ADD, SUB, MAX = ALU.mult, ALU.add, ALU.subtract, ALU.max
    BIG, TP, SC = plan()
    ORDER = gates_order()
    POOL_SPLITS = 12

    ctx = ExitStack()
    with ctx:
        def sb(name, shape, dt=f32):
            return ctx.enter_context(nc.sbuf_tensor(name, shape, dt))

        def sem(name):
            return ctx.enter_context(nc.semaphore(name))

        def bc(ap, axis, n):
            a = ap.unsqueeze(axis)
            shape = list(a.shape)
            shape[axis] = n
            return a.broadcast_to(shape)

        NSLOT = MAXR * ROUND
        slot_table = nc.dram_tensor("slot_table", [NSLOT + 2 * P, 2], i32, kind="Internal").ap()
        hn2_rows = nc.dram_tensor("hn2_rows", [T, D], f32, kind="Internal").ap()
        pair_rows = nc.dram_tensor("pair_rows", [2 * T, D], f32, kind="Internal").ap()

        HS = SLAB // 2
        WR, WP, WL = 2, 2, 8
        cst = sb("cst", [P, K_END])
        tok = sb("tok", [P, 2, NT, 2], i32)
        prm = sb("prm", [P, R_END])
        with ExitStack() as early:
            hnh = early.enter_context(nc.sbuf_tensor("hnh", [P, KT, T], f32r))
            hnl = early.enter_context(nc.sbuf_tensor("hnl", [P, KT, T], f32r))
            wplain = early.enter_context(nc.sbuf_tensor("wplain", [P, WP, HS], f32))
            wraw = early.enter_context(nc.sbuf_tensor("wraw", [P, WR, HS], f32))
            wh = early.enter_context(nc.sbuf_tensor("wh", [P, 2, HS], f32r))
            wl = early.enter_context(nc.sbuf_tensor("wl", [P, 2, HS], f32r))
        xres = sb("xres", [P, NT, D])
        h2 = sb("h2", [P, NT, D])
        wlate = sb("wlate", [P, WL, HS])
        mix = sb("mix", [P, NT * D])
        act = sb("act", [P, 2 * CT * T])
        late = sb("late", [P, 2176])
        xrp = sb("xrp", [P, CT * (T + CONV - 1)])
        xc = sb("xc", [P, CT * T])
        r1 = sb("r1", [P, 6 * SLAB])
        X = sb("X", [P, 4 * GP * (NC + 1)])
        U = sb("U", [P, G * NC])
        bb = sb("bb", [P, 4, GP, C])
        cc = sb("cc", [P, 2, GP, C])
        pw = sb("pw", [P, 2, L + 1, 2 * GP])
        aa = sb("aa", [P, 2, 4, GP])
        sm = sb("sm", [P, 96])
        lt = sb("lt", [P, 4, 8])
        dskip = sb("dskip", [2 * C, GP])
        dd = sb("dd", [2 * C, GP, C])
        slot_i = sb("slot_i", [P, 2, NT], i32)
        idx = sb("idx", [P, 4, 2], i32)
        ntot = sb("ntot", [1, 1], i32)

        ident = cst[:, K_ID:K_ID + P]
        xt = r1[:, 0:4096].rearrange("p (t d) -> p t d", t=NT)
        xs = r1[:, 4096:8192].rearrange("p (t d) -> p t d", t=NT)
        mixed = mix[:, :].rearrange("p (k t) -> p k t", k=KT)
        oatt, olru = [act[:, i * 2048:(i + 1) * 2048].rearrange("p (c t) -> p c t", c=CT) for i in range(2)]
        ossm = U[:, :].rearrange("p (c t) -> p c t", c=CT)
        branch_in = (oatt, olru, ossm)
        uT = olru
        xrv = xrp[:, :].rearrange("p (c t) -> p c t", c=CT)
        xcv = xc[:, :].rearrange("p (c t) -> p c t", c=CT)
        Xv = X[:, :].rearrange("p (d g s) -> p d g s", d=4, g=GP)
        Xd = X[:, :].rearrange("p (d r g s) -> p d r g s", d=2, r=2, g=GP)
        Uv = U[:, :].rearrange("p (g k) -> p g k", g=G)
        wri = mix[:, 0:1024].rearrange("p (w d c j) -> p w d c j", w=2, d=2, c=CT)
        btmp = mix[:, 1024:2048].rearrange("p (a g c) -> p a g c", a=2, g=2 * GP)
        bin_ = mix[:, 2048:3072].rearrange("p (r g c) -> p r g c", r=2, g=2 * GP)
        crow = mix[:, 3072:4096].rearrange("p (r t h n) -> p r t h n", r=2, t=CT, h=2)
        l_r, l_i, l_v, l_a, l_q = [r1[:, 6144 + i * 1024:7168 + i * 1024].rearrange("p (d t) -> p d t", d=2)
                                   for i in range(5)]
        wn = r1[:, 3072:5120].rearrange("p (d g m) -> p d g m", d=4, g=4)
        tmpA, tmpB = r1[:, 5120:5632], r1[:, 5632:6144]
        wt = late[:, 0:2048].rearrange("p (b d n) -> p b d n", b=4, d=4)
        sgate = act[:, :].rearrange("p (k t) -> p k t", k=KT)
        qT = r1[:, 0:2048].rearrange("p (a t) -> p a t", a=GQ)
        kT = r1[:, 2048:2560]
        vS = r1[:, 2560:3072].rearrange("p (a t) -> p a t", a=NT)
        btab = r1[:, 3072:6144].rearrange("p (h k) -> p h k", h=NQ)
        pr = r1[:, 6144:9216].rearrange("p (b h k) -> p b h k", b=2, h=GQ)
        x2 = r1[0:NC, 6144:7168].rearrange("p (g j c) -> p g j c", g=8, j=L)
        pT = r1[:, 9216:10752].rearrange("p (k q) -> p k q", k=3)
        prows = r1[0:R_END, 11264:11264 + P]
        srows = r1[0:96, 11392:11392 + P]
        lstep = r1[0:96, 11520:11522]
        s5p = r1[:, 11522:11618]
        cs = r1[:, 11618:11682].rearrange("p (i g) -> p i g", i=2)
        s5t = r1[:, 11776:12288].rearrange("p (i g) -> p i g", i=16)
        cp = r1[:, 0:4608].rearrange("p (b d g m) -> p b d g m", b=2, d=4, g=4)
        tmpC, tmpD = r1[:, 4608:5184], r1[:, 5184:5760]
        kx = r1[0:2 * C, 5760:6720].rearrange("p (g m) -> p g m", g=4)
        y1 = r1[:, 6720:7232].rearrange("p (g k) -> p g k", g=8)
        y2 = r1[0:NC, 7232:8256].rearrange("p (j g c) -> p j g c", j=L, g=8)
        mms = [(late[:, 0:1024], late[:, 1024:2048], r1[:, 8256:9280], r1[:, 9280:10304])[i]
               .rearrange("p (g m) -> p g m", g=8) for i in range(CT)]
        sct = late[:, 2048:2176].rearrange("p (i d g) -> p i d g", i=2, d=4)
        gbuf = xrp[:, 0:1024].rearrange("p (b t) -> p b t", b=2)
        bbd = xrp[:, 1024:1536].rearrange("p (d g h c) -> p d g h c", d=4, g=4, h=2)
        g2b, fgb = X[:, 0:1024], X[:, 1024:2048]
        wge = X[:, 2048:2208].rearrange("p (k c) -> p k c", k=KT)
        bge = X[:, 2208:2228]
        blank = X[:, 2240:2368].bitcast(i32).rearrange("p (n c) -> p n c", c=2)
        h2T = mixed
        pair = (h2, mix[:, :].rearrange("p (t d) -> p t d", t=NT))
        xg = act[:, 0:2048].rearrange("p (b d) -> p b d", b=2)
        xgT = act[:, 2048:4096].rearrange("p (b k s) -> p b k s", b=2, k=KT)
        sg = late[:, 0:512].rearrange("p (b f) -> p b f", b=2)
        hh = late[:, 512:1024].rearrange("p (b f) -> p b f", b=2)
        hT = late[:, 1024:1536].rearrange("p (b k s) -> p b k s", b=2, k=2)
        yb = U[:, :].rearrange("p (b d) -> p b d", b=2)
        ssq, rstd = sm[:, 0:4], sm[:, 4:8]
        sink = sm[:, 8:16]
        cl = sm[:, 16:24]
        am, anm, aes, asum, ard = [sm[:, 24 + 8 * i:32 + 8 * i].rearrange("p (b h) -> p b h", b=2)
                                   for i in range(5)]
        ssq2, rstd2, ssq3, rstd3 = [sm[:, 64 + 4 * i:68 + 4 * i] for i in range(4)]
        rt = [xc[:, 64 * i:64 * i + 64].rearrange("p (t e) -> p t e", t=NT) for i in range(12)]
        rs = [xc[:, 768 + 4 * i:772 + 4 * i] for i in range(16)]
        rg = [xc[:, 832 + 16 * i:848 + 16 * i].rearrange("p (t e) -> p t e", t=NT) for i in range(8)]

        banks = {"big": [ctx.enter_context(nc.psum_tensor(f"big{i}", [P, 512], f32)) for i in range(4)],
                 "tp": [ctx.enter_context(nc.psum_tensor(f"tp{i}", [P, 512], f32)) for i in range(2)],
                 "sc": [ctx.enter_context(nc.psum_tensor(f"sc{i}", [P, 512], f32)) for i in range(2)]}
        rings = {"big": BIG, "tp": TP, "sc": SC}
        full = {r: sem(f"{r}_full") for r in rings}
        free = {(r, by): sem(f"{r}_emptied_{by}") for r in rings for by in "av"}

        cst_in, prow_in, srow_in, x_in = sem("cst_in"), sem("prow_in"), sem("srow_in"), sem("x_in")
        early_in, lru_w_in, late_in = sem("early_in"), sem("lru_w_in"), sem("late_in")
        raw_in, plain_in, last_in = ([sem(f"{name}_in{i}") for i in range(n)]
                                     for name, n in (("raw", WR), ("plain", WP), ("last", WL)))
        x_hi = sem("x_hi")
        hi_ready, lo_pool, lo_dve = sem("hi_ready"), sem("lo_pool"), sem("lo_dve")
        dve_step, act_step, pool_step = sem("dve_step"), sem("act_step"), sem("pool_step")
        squares, mean_ready, root_ready, xs_ready = sem("squares"), sem("mean_ready"), sem("root_ready"), sem("xs_ready")
        step_exp, srows_ready, s5_arg, s5_act, s5_tab = sem("step_exp"), sem("srows_ready"), sem("s5_arg"), sem("s5_act"), sem("s5_tab")
        cl_arg, cl_exp, cl_ready = sem("cl_arg"), sem("cl_exp"), sem("cl_ready")
        pad_zero, x_zero, dskip_in = sem("pad_zero"), sem("x_zero"), sem("dskip_in")
        conv_done, btab_ready = sem("conv_done"), sem("btab_ready")
        lru_ta, lru_q, lru_s, lru_out = sem("lru_ta"), sem("lru_q"), sem("lru_s"), sem("lru_out")
        s_max, s_exp, s_prob, pv_done = sem("s_max"), sem("s_exp"), sem("s_prob"), sem("pv_done")
        gate_used = sem("gate_used")
        yg_in = [sem(f"yg_in{t}") for t in range(NT)]
        wn_ready, scan_mul, scan_add = sem("wn_ready"), sem("scan_mul"), sem("scan_add")
        bbd_zero, bbd_ready, cp_ready, kx_ready, mm_in = sem("bbd_zero"), sem("bbd_ready"), sem("cp_ready"), sem("kx_ready"), sem("mm_in")
        glu_ready, x_again, x1_sq, x1_root, h2_ready, h2_out = sem("glu_ready"), sem("x_again"), sem("x1_sq"), sem("x1_root"), sem("h2_ready"), sem("h2_out")
        pool_pass = sem("pool_pass")
        zero_ready, slot_zero, w_arg, w_exp = sem("zero_ready"), sem("slot_zero"), sem("w_arg"), sem("w_exp")
        mask_ready, n_ready, slots_ready, slot_out = sem("mask_ready"), sem("n_ready"), sem("slots_ready"), sem("slot_out")
        ew_in = [sem(f"ew_in{i}") for i in range(6)]
        w13_used, w2_used, idx_in, xg_in = sem("w13_used"), sem("w2_used"), sem("idx_in"), [sem("xg_in0"), sem("xg_in1")]
        xg_turned, xgT_a, xgT_v, hid_full, silu_done, hh_ready = sem("xg_turned"), sem("xgT_a"), sem("xgT_v"), sem("hid_full"), sem("silu_done"), sem("hh_ready")
        hT_full, hT_ready, y_full, yb_a, yb_v = sem("hT_full"), sem("hT_ready"), sem("y_full"), sem("yb_a"), sem("yb_v")
        rows_out = [sem("rows_out0"), sem("rows_out1")]
        acc_ready, out_sq, out_root, out_ready, out_in = sem("acc_ready"), sem("out_sq"), sem("out_root"), sem("out_ready"), sem("out_in")

        w_in_v = w_in.rearrange("(k p) c -> p k c", p=P)
        w_glu_v = w_glu.rearrange("(k p) c -> p k c", p=P)
        w_out_v = w_out.rearrange("(k p) c -> p k c", p=P)
        raw_slabs, plain_slabs, last_slabs = [], [], []

        def in_slab(key, col):
            raw_slabs.append((key, [(lambda w: w.rearrange("p (k c) -> p k c", k=KT), w_in_v[:, :, col:col + P])]))

        def q_slab(i):
            raw_slabs.append((("q", i), [
                (lambda w, h=h: w.rearrange("p (k h c) -> p k h c", k=KT, h=2)[:, :, h, :],
                 w_in_v[:, :, (h * GQ + i) * HD:(h * GQ + i + 1) * HD]) for h in range(2)]))

        def branch_slab(slabs, b, n):
            cols = slice(n * 256, n * 256 + 256)
            if b:
                parts = [(lambda w: w.rearrange("p (k c) -> p k c", k=CT),
                          w_branch[b].rearrange("(k p) c -> p k c", p=P)[:, :, cols])]
            else:
                parts = [(lambda w, h=h: w[h * HD:(h + 1) * HD].rearrange("p (k c) -> p k c", k=CT),
                          w_branch[0, h * GQ * HD:(h + 1) * GQ * HD].rearrange("(k p) c -> p k c", p=HD)[:, :, cols])
                         for h in range(2)]
            slabs.append((("p", b, n), parts))

        column = {"u": COL_U, "xr": COL_XR, "gr": COL_GR, "k": COL_K, "v": COL_V}
        for key in ORDER:
            if key[0] == "q":
                q_slab(key[1])
            elif key[0] == "g":
                in_slab(key, COL_GATE + key[1] * D + P * key[2])
            else:
                in_slab(key, column[key] if key in column else column[key[0]] + P * key[1])
        for b in (1, 0):
            for n in range(4):
                branch_slab(plain_slabs, b, n)
        for n in range(CT):
            last_slabs.append((("z", n), [(lambda w, h=h: w.rearrange("p (k h c) -> p k h c", k=CT, h=2)[:, :, h, :],
                                           w_glu_v[:, :, h * BW + P * n:h * BW + P * n + P]) for h in range(2)]))
        for n in range(4):
            branch_slab(last_slabs, 2, n)
        for h in range(2):
            for n in range(4):
                last_slabs.append((("wo", h, n), [(lambda w: w.rearrange("p (k c) -> p k c", k=2),
                                                   w_out_v[:, 2 * n:2 * n + 2, h * 512:h * 512 + 512])]))

        def slab_count(slabs, n, slots):
            return 16 * sum(len(slabs[m][1]) for m in range(n % slots, n + 1, slots))

        def index_of(slabs, key):
            return next(n for n, (k, _) in enumerate(slabs) if k == key)

        def lo_done(m):
            return (lo_pool, m + 1) if m < POOL_SPLITS else (lo_dve, m - POOL_SPLITS + 1)

        def split_lo(eng, tensor_tensor, m):
            eng.wait_ge(hi_ready, m + 1)
            tensor_tensor(wl[:, m % 2, :], wraw[:, m % WR, :], wh[:, m % 2, :].bitcast(f32), SUB).then_inc(lo_done(m)[0], 1)

        def pe_bank(eng, ring, key):
            r = rings[ring]
            n = r.index(key)
            if n >= r.size:
                by, count = r.emptied(n - r.size)
                eng.wait_ge(free[ring, by], count)
            return banks[ring][n % r.size]

        def full_bank(eng, ring, key):
            r = rings[ring]
            n = r.index(key)
            eng.wait_ge(full[ring], n + 1)
            return banks[ring][n % r.size]

        def emptied(ring, key):
            by, count = rings[ring].emptied(rings[ring].index(key))
            return free[ring, by], count

        def slab_last_job(key):
            if key[0] == "p":
                return BIG.index(("p", key[1], 2 * key[2] + 1))
            if key[0] == "wo":
                return BIG.index(("wo", NT - 1, key[1]))
            if key[0] == "z":
                return BIG.index(("z0", key[1]))
            return BIG.index(key)

        block = ctx.enter_context(nc.Block())

        @block.sync
        def _(sp):
            for t in range(NT):
                sp.dma_start(xt[:, t, :], x[t * P:(t + 1) * P, :]).then_inc(x_in, 16)

            def load_slab(slabs, n, slots, ring, done):
                for shape, src in slabs[n][1]:
                    sp.dma_start(shape(ring[:, n % slots, :]), src).then_inc(done[n % slots], 16)

            def load_plain(n):
                if n >= WP:
                    sp.wait_ge(full["big"], slab_last_job(plain_slabs[n - WP][0]) + 1)
                load_slab(plain_slabs, n, WP, wplain, plain_in)

            for m, key in enumerate(ORDER):
                if m >= WR:
                    sp.wait_ge(*lo_done(m - WR))
                load_slab(raw_slabs, m, WR, wraw, raw_in)
                if key[0] == "g" and key[1] != 2 and key[2] % 2 == 0:
                    load_plain((4 if key[1] == 0 else 0) + key[2] // 2)
            for n in range(len(last_slabs)):
                if n < WL:
                    if n == 0:
                        sp.wait_ge(full["big"], BIG.index(("p", 0, KT - 1)) + 1)
                    if n == WP:
                        sp.wait_ge(full["big"], BIG.index(("g", 2, KT - 1)) + 1)
                else:
                    sp.wait_ge(full["big"], slab_last_job(last_slabs[n - WL][0]) + 1)
                load_slab(last_slabs, n, WL, wlate, last_in)
                if n == WL - 1:
                    for t in range(NT):
                        sp.dma_start(xres[:, t, :], x[t * P:(t + 1) * P, :]).then_inc(x_again, 16)

            def expert_weights(e, h):
                for j, w in enumerate((w1, w3, w2)):
                    k = KT if j < 2 else 2
                    dst = r1[:, (3 * h + j) * SLAB:(3 * h + j + 1) * SLAB].rearrange("p (k f) -> p k f", k=k)
                    src = w[bass.ds(e, 1)].rearrange("o (k p) f -> p (o k) f", p=P)
                    sp.dma_start(dst, src).then_inc(ew_in[3 * h + j], 16)

            sp.wait_ge(full["tp"], TP.index(("y3", CT - 1)) + 1)
            for h in range(2):
                expert_weights(h, h)
            for t in range(NT):
                sp.wait_ge(h2_ready, t + 1)
                sp.dma_start(hn2_rows[t * P:(t + 1) * P, :], h2[:, t, :]).then_inc(h2_out, 16)
            sp.wait_ge(n_ready, 1)
            rest = sp.value_load(ntot[0:1, 0:1], min_val=E - 4, max_val=MAXR * E - 4)
            with sp.Fori(2, rest + 4, 2) as g:
                for h in range(2):
                    sp.wait_ge(hid_full, g + (h - 1))
                    sp.wait_ge(y_full, g + (h - 1))
                    expert_weights((g + h) % E, h)
            sp.wait_ge(rows_out[0], rest * 8 + 32)
            sp.wait_ge(rows_out[1], rest * 8 + 32)
            sp.wait_ge(n_ready, 1)
            pairs = pair_rows.rearrange("(t p c) d -> t p c d", p=P, c=2)
            for t in range(NT):
                for c in range(2):
                    sp.dma_start(pair[c][:, t, :], pairs[t, :, c, :]).then_inc(yg_in[t], 16)
            for t in range(NT):
                sp.wait_ge(out_ready, t + 1)
                sp.dma_start(out[t * P:(t + 1) * P, :], xres[:, t, :]).then_inc(out_in, 16)
            sp.wait_ge(out_in, 16 * NT)

        @block.gpsimd
        def _(pool):
            steps = [0]

            def link(ins):
                steps[0] += 1
                ins.then_inc(pool_step, 1)
                pool.wait_ge(pool_step, steps[0])

            nc.gpsimd.memset(xrv[:, :, 0:2], 0.0).then_inc(pad_zero, 1)
            nc.gpsimd.memset(xrv[:, :, T + 2:T + 3], 0.0).then_inc(pad_zero, 1)
            nc.gpsimd.memset(Xv[:, :, :, 0:1], 0.0).then_inc(x_zero, 1)
            for m in range(POOL_SPLITS):
                split_lo(pool, nc.gpsimd.tensor_tensor, m)
            pool.wait_ge(s5_tab, 1)
            for ct in range(CT):
                if ct:
                    pool.wait_ge(full["tp"], TP.index(("w", ct - 1, 3)) + 1)
                tv = [t.rearrange("p (g j c) -> p g j c", g=4, j=L) for t in (tmpA, tmpB)]
                for d in range(2):
                    cols = slice(d * GP + 4 * ct, d * GP + 4 * ct + 4)

                    def power(r):
                        rows = pw[:, r, L - 1::-1, cols] if d == 0 else pw[:, r, 0:L, cols]
                        return bc(rows.rearrange("p j g -> p g j"), 3, C)

                    def b_of(r):
                        return bc(bb[:, 2 * d + r, 4 * ct:4 * ct + 4, :], 2, L)

                    dst = [wn[:, 2 * d + r].rearrange("p g (j c) -> p g j c", j=L) for r in range(2)]
                    link(nc.gpsimd.tensor_tensor(tv[0], power(0), b_of(0), MUL))
                    link(nc.gpsimd.tensor_tensor(tv[1], power(1), b_of(1), MUL))
                    link(nc.gpsimd.tensor_tensor(dst[0], tv[0], tv[1], SUB))
                    link(nc.gpsimd.tensor_tensor(tv[0], power(0), b_of(1), MUL))
                    link(nc.gpsimd.tensor_tensor(tv[1], power(1), b_of(0), MUL))
                    nc.gpsimd.tensor_tensor(dst[1], tv[0], tv[1], ADD).then_inc(wn_ready, 1)
                    pool.wait_ge(wn_ready, 2 * ct + d + 1)
            pool.wait_ge(full["tp"], TP.index(("w", CT - 1, 3)) + 1)
            pool.wait_ge(cst_in, 32)
            for h in range(NQ):
                nc.gpsimd.tensor_scalar(btab[:, h, :], cst[:, K_DIST:K_DIST + 3 * P],
                                        float(2.0 ** (-8.0 * (h + 1) / NQ)), None, MUL).then_inc(btab_ready, 1)
            pool.wait_ge(*emptied("sc", ("st", KT - 1)))
            with pool.Fori(1, NC - 1, 2) as s0:
                for h in range(2):
                    s = s0 + h
                    now = Xv[:, :, :, bass.ds(s, 1)].rearrange("p d g s -> p d (g s)")
                    nxt = Xv[:, :, :, bass.ds(s + 1, 1)].rearrange("p d g s -> p d (g s)")
                    nxtd = Xd[:, :, :, :, bass.ds(s + 1, 1)].rearrange("p d r g s -> p d r (g s)")
                    swapped = sct[:, 1].rearrange("p (d r) g -> p d r g", d=2)[:, :, ::-1, :]
                    nc.gpsimd.tensor_tensor(sct[:, 0], aa[:, 0], now, MUL).then_inc(scan_mul, 1)
                    nc.gpsimd.tensor_tensor(sct[:, 1], aa[:, 1], now, MUL).then_inc(scan_mul, 1)
                    pool.wait_ge(scan_mul, s * 2 - 1)
                    pool.sem_inc(pool_pass, 1)
                    nc.gpsimd.tensor_tensor(nxt, nxt, sct[:, 0], ADD).then_inc(scan_add, 1)
                    pool.wait_ge(scan_mul, s * 2)
                    pool.wait_ge(scan_add, s * 2 - 1)
                    pool.sem_inc(pool_pass, 1)
                    nc.gpsimd.tensor_tensor(nxtd, nxtd, swapped, ADD).then_inc(scan_add, 1)
                    pool.wait_ge(scan_add, s * 2)
                    pool.sem_inc(pool_pass, 1)
            pool.wait_ge(full["tp"], TP.index(("y3", CT - 1)) + 1)
            pool.dma_start(g2b, norm2_g.partition_broadcast(P)).then_inc(late_in, 16)
            pool.dma_start(fgb, final_g.partition_broadcast(P)).then_inc(late_in, 16)
            pool.dma_start(wge[:, :, 0:NGRP], w_group.rearrange("(k p) c -> p k c", p=P)).then_inc(late_in, 16)
            pool.dma_start(wge[:, :, NGRP:NGRP + E], w_expert.rearrange("(k p) c -> p k c", p=P)).then_inc(late_in, 16)
            pool.dma_start(bge[:, 0:NGRP], b_group.partition_broadcast(P)).then_inc(late_in, 16)
            pool.dma_start(bge[:, NGRP:NGRP + E], b_expert.partition_broadcast(P)).then_inc(late_in, 16)
            nc.gpsimd.memset(blank[:, :, 0:1], 0).then_inc(zero_ready, 1)
            nc.gpsimd.memset(blank[:, :, 1:2], 2 * T).then_inc(zero_ready, 1)
            pool.wait_ge(zero_ready, 2)
            pool.dma_start(slot_table[0:NSLOT].rearrange("(p n) c -> p n c", p=P), blank).then_inc(slot_zero, 16)
            pool.wait_ge(slot_zero, 16)
            pool.wait_ge(slots_ready, 2)
            for c in range(2):
                for t in range(NT):
                    pool.indirect_dma_start(slot_table, bass.IndirectOffsetOnAxis(ap=slot_i[:, c, t:t + 1], axis=0),
                                            tok[:, c, t, :], None).then_inc(slot_out, 16)
            pool.wait_ge(slot_out, 16 * 2 * NT)
            pool.wait_ge(h2_out, 16 * NT)
            pool.wait_ge(n_ready, 1)
            rest = pool.value_load(ntot[0:1, 0:1], min_val=E - 4, max_val=MAXR * E - 4)

            def gather(i, h, b):
                pool.dma_start(idx[:, b, :], slot_table[bass.ds(i * P, P), :]).then_inc(idx_in, 16)
                pool.wait_ge(idx_in, i * 16 + 16)
                pool.sem_inc(pool_pass, 1)
                pool.indirect_dma_start(xg[:, h, :], None, hn2_rows,
                                        bass.IndirectOffsetOnAxis(ap=idx[:, b, 0:1], axis=0)).then_inc(xg_in[h], 16)

            def scatter(i, h, b):
                pool.wait_ge(yb_a, i + 1)
                pool.wait_ge(yb_v, i + 1)
                pool.sem_inc(pool_pass, 1)
                pool.indirect_dma_start(pair_rows, bass.IndirectOffsetOnAxis(ap=idx[:, b, 1:2], axis=0), yb[:, h, :], None,
                                        bounds_check=2 * T - 1, oob_is_err=False).then_inc(rows_out[h], 16)

            gather(0, 0, 0)
            gather(1, 1, 1)
            with pool.Fori(0, rest, 4) as g:
                for j in range(4):
                    pool.wait_ge(xg_turned, g + (j + 1))
                    gather(g + (j + 2), j % 2, (j + 2) % 4)
                    scatter(g + j, j % 2, j)
            for j in range(4):
                if j < 2:
                    pool.wait_ge(xg_turned, rest + (j + 1))
                    gather(rest + (j + 2), j % 2, (j + 2) % 4)
                scatter(rest + j, j % 2, j)

        @block.tensor
        def _(pe):
            mmul = nc.tensor.matmul

            def turn(dst, src, n=P):
                return nc.tensor.transpose(dst, src, cst[0:n, K_ID:K_ID + n])

            def plain_weights(key):
                slabs, slots, ring, done = ((last_slabs, WL, wlate, last_in) if key[0] != "p" or key[1] == 2 else
                                            (plain_slabs, WP, wplain, plain_in))
                n = index_of(slabs, key)
                pe.wait_ge(done[n % slots], slab_count(slabs, n, slots))
                return ring[:, n % slots, :]

            def split_weights(key):
                m = ORDER.index(key)
                pe.wait_ge(*lo_done(m))
                return [w[:, m % 2, :].rearrange("p (k c) -> p k c", k=KT) for w in (wh, wl)]

            def channels(key, w, rhs, ks):
                bank = pe_bank(pe, "big", key)
                for k in range(ks):
                    ins = mmul(bank[:, :], w[:, k, :], rhs[:, k, :], start=(k == 0), stop=(k == ks - 1))
                ins.then_inc(full["big"], 1)

            def project(key):
                w = split_weights(key)
                bank = pe_bank(pe, "big", key)
                for k in range(KT):
                    mmul(bank[:, :], w[0][:, k, :], hnh[:, k, :], start=(k == 0), stop=False)
                    mmul(bank[:, :], w[0][:, k, :], hnl[:, k, :], start=False, stop=False)
                    ins = mmul(bank[:, :], w[1][:, k, :], hnh[:, k, :], start=False, stop=(k == KT - 1))
                ins.then_inc(full["big"], 1)

            def branch(b, d):
                w = plain_weights(("p", b, d // 2)).rearrange("p (k c) -> p k c", k=CT)
                channels(("p", b, d), w[:, :, (d % 2) * P:(d % 2 + 1) * P], branch_in[b], CT)

            pe.wait_ge(cst_in, 32)
            pe.wait_ge(prow_in, 16 * 8)
            turn(pe_bank(pe, "tp", "prm")[:, 0:R_END], prows[:, :], R_END).then_inc(full["tp"], 1)
            pe.wait_ge(srow_in, 16 * 3)
            pe.wait_ge(srows_ready, 1)
            turn(pe_bank(pe, "tp", "s5p")[:, 0:96], srows[:, :], 96).then_inc(full["tp"], 1)
            pe.wait_ge(xs_ready, NT)
            for k in range(KT):
                bank = pe_bank(pe, "tp", ("x", k))
                for t in range(NT):
                    ins = turn(bank[:, t * P:(t + 1) * P], xs[:, t, k * P:(k + 1) * P])
                ins.then_inc(full["tp"], 1)
            pe.wait_ge(*emptied("tp", ("x", KT - 1)))
            for n in range(CT):
                project(("u", n))
            for n in range(CT):
                project(("xr", n))
            project("k")
            w = split_weights("v")
            bank = pe_bank(pe, "big", "v")
            for t in range(NT):
                rows = slice(t * P, (t + 1) * P)
                for k in range(KT):
                    mmul(bank[:, rows], hnh[:, k, rows], w[0][:, k, :], start=(k == 0), stop=False)
                    mmul(bank[:, rows], hnh[:, k, rows], w[1][:, k, :], start=False, stop=False)
                    ins = mmul(bank[:, rows], hnl[:, k, rows], w[0][:, k, :], start=False, stop=(k == KT - 1))
            ins.then_inc(full["big"], 1)
            pe.wait_ge(early_in, 16 * 8)
            for r in range(2):
                bank = pe_bank(pe, "tp", ("c", r))
                for q in range(CT):
                    ins = turn(bank[:, q * P:(q + 1) * P], crow[:, r, q].rearrange("p h n -> p (h n)"))
                ins.then_inc(full["tp"], 1)
            pe.wait_ge(*emptied("big", ("u", CT - 1)))
            for ct in range(CT):
                for half in range(2):
                    bank = pe_bank(pe, "tp", ("x2", ct, half))
                    for j in range(4):
                        ins = turn(bank[0:NC, j * P:(j + 1) * P], uT[:, ct, half * 4 + j::L])
                    ins.then_inc(full["tp"], 1)
                for half in range(2):
                    pe.wait_ge(*emptied("tp", ("x2", ct, half)))
                bank = pe_bank(pe, "tp", ("U", ct))
                for g in range(8):
                    ins = turn(bank[:, g * NC:(g + 1) * NC], x2[:, g].rearrange("p j c -> p (j c)"), NC)
                ins.then_inc(full["tp"], 1)
            pe.wait_ge(lru_w_in, 16 * 8)
            for ct in range(CT):
                for j in range(2):
                    project(("gr" if ct < 2 else "q", 2 * (ct % 2) + j))
                pe.wait_ge(wn_ready, 2 * ct + 2)
                for g4 in range(4):
                    bank = pe_bank(pe, "tp", ("w", ct, g4))
                    for q in range(4):
                        ins = turn(bank[:, q * P:(q + 1) * P], wn[:, q, g4, :])
                    ins.then_inc(full["tp"], 1)
                pe.wait_ge(*emptied("tp", ("U", CT - 1)))
                for d in (2 * ct, 2 * ct + 1):
                    bank = pe_bank(pe, "sc", ("st", d))
                    for h in range(2):
                        g4 = 2 * (d % 2) + h
                        pe.wait_ge(*emptied("tp", ("w", ct, g4)))
                        for q in range(4):
                            for g2 in range(2):
                                g = 4 * d + 2 * h + g2
                                rhs = Uv[:, g, :] if q < 2 else Uv[:, g, ::-1]
                                ins = mmul(bank[g2 * N:(g2 + 1) * N, (q * 2 + h) * NC:(q * 2 + h + 1) * NC],
                                           wt[:, g4, q, g2 * N:(g2 + 1) * N], rhs, start=True, stop=True)
                    ins.then_inc(full["sc"], 1)
                pe.wait_ge(conv_done, ct + 1)
                for w in range(2):
                    for d in range(2):
                        bank = pe_bank(pe, "big", ("lru", ct, w, d))
                        for h in range(2):
                            rows = slice(h * LB, (h + 1) * LB)
                            ins = mmul(bank[rows, :], wri[rows, w, d, ct, :], xcv[rows, ct, :], start=True, stop=True)
                        ins.then_inc(full["big"], 1)

            def scores(u):
                nb, h = u // 2, u % 2
                lo, n = key_blocks(nb)
                rows = slice(h * HD, (h + 1) * HD)
                for i in range(GQ):
                    bank = pe_bank(pe, "sc", ("s", u, i))
                    mmul(bank[:, 0:n * P], qT[rows, i, nb * P:(nb + 1) * P], kT[rows, lo * P:(lo + n) * P],
                         start=True, stop=True).then_inc(full["sc"], 1)

            pe.wait_ge(*emptied("big", ("q", CT - 1)))
            scores(0)
            for d in range(KT):
                if d + 1 < KT:
                    scores(d + 1)
                nb, h = d // 2, d % 2
                lo, n = key_blocks(nb)
                pe.wait_ge(s_prob, d + 1)
                for k in range(n):
                    bank = pe_bank(pe, "tp", ("p", d, k))
                    for i in range(GQ):
                        ins = turn(bank[:, i * P:(i + 1) * P], pr[:, d % 2, i, k * P:(k + 1) * P])
                    ins.then_inc(full["tp"], 1)
                project(("g", 1, d))
                bank = pe_bank(pe, "big", ("pv", d))
                for k in range(n):
                    pe.wait_ge(*emptied("tp", ("p", d, k)))
                    ins = mmul(bank[h * HD:(h + 1) * HD, :], vS[:, lo + k, h * HD:(h + 1) * HD], pT[:, k, :],
                               start=(k == 0), stop=(k == n - 1))
                ins.then_inc(full["big"], 1)
                pe.wait_ge(lru_out, CT)
                branch(1, d)
            def ssm_kernels(ct):
                pe.wait_ge(cp_ready, 2 * ct + 2)
                pe.wait_ge(bbd_ready, 2 * ct + 2)
                for name, d, off in (("kf", 0, 0), ("kb", 1, C)):
                    bank = pe_bank(pe, "sc", (name, ct))
                    for g4 in range(4):
                        for r in range(2):
                            ins = mmul(bank[0:2 * C, g4 * P:(g4 + 1) * P],
                                       bbd[:, 2 * d + r, g4].rearrange("p h c -> p (h c)"),
                                       cp[:, ct % 2, 2 * d + r, g4, off:off + P], start=(r == 0), stop=(r == 1))
                    ins.then_inc(full["sc"], 1)

            def ssm_products(ct):
                if ct == 0:
                    pe.wait_ge(scan_add, 2 * (NC - 2))
                pe.wait_ge(mm_in, 16 * 2 * L * (ct + 1))
                for g in (0, 2, 4, 6, 1, 3, 5, 7):
                    if g < 2:
                        bank = pe_bank(pe, "big", ("y1", ct, g))
                    dst = bank[:, (g // 2) * NC:(g // 2 + 1) * NC]
                    rows = slice((g % 2) * N, (g % 2 + 1) * N)
                    gp = 4 * ct + g // 2
                    mmul(dst, mms[ct][:, g, :], Uv[:, 8 * ct + g, :], start=True, stop=False)
                    for q in range(4):
                        off = C if q < 2 else 0
                        st = Xv[rows, q, gp, 0:NC] if q < 2 else Xv[rows, q, gp, NC - 1::-1]
                        ins = mmul(dst, cp[rows, ct % 2, q, g // 2, off:off + P], st, start=False, stop=(q == 3))
                    if g >= 6:
                        ins.then_inc(full["big"], 1)

            def ssm_to_chunks(ct):
                pe.wait_ge(*emptied("big", ("y1", ct, 1)))
                for half in range(2):
                    bank = pe_bank(pe, "tp", ("y2", ct, half))
                    for g in range(4):
                        ins = turn(bank[0:NC, g * P:(g + 1) * P], y1[:, 4 * half + g, :])
                    ins.then_inc(full["tp"], 1)

            def ssm_to_channels(ct):
                for half in range(2):
                    pe.wait_ge(*emptied("tp", ("y2", ct, half)))
                bank = pe_bank(pe, "tp", ("y3", ct))
                for j in range(L):
                    ins = turn(bank[:, j * NC:(j + 1) * NC], y2[:, j].rearrange("p g c -> p (g c)"), NC)
                ins.then_inc(full["tp"], 1)

            steps = {"K": ssm_kernels, "Y1": ssm_products, "Y2": ssm_to_chunks, "Y3": ssm_to_channels}
            pe.wait_ge(*emptied("big", ("pv", KT - 1)))
            for b in (0, 2):
                for d in range(KT):
                    project(("g", b, d))
                    if b == 0:
                        branch(0, d)
                    for step, ct in SSM_STEPS.get((b, d), []):
                        if step in steps:
                            steps[step](ct)
            pe.wait_ge(*emptied("tp", ("y3", CT - 1)))
            for n in range(CT):
                w = plain_weights(("z", n)).rearrange("p (k h c) -> p k h c", k=CT, h=2)
                channels(("z1", n), w[:, :, 1, :], xcv, CT)
                channels(("z0", n), w[:, :, 0, :], xcv, CT)
            pe.wait_ge(glu_ready, CT)
            for d in range(KT):
                branch(2, d)
            pe.wait_ge(gate_used, NBR * KT)
            for t in range(NT):
                for h in range(2):
                    bank = pe_bank(pe, "big", ("wo", t, h))
                    for k in range(KT):
                        w = plain_weights(("wo", h, k // 2)).rearrange("p (k c) -> p k c", k=2)
                        ins = mmul(bank[:, :], mixed[:, k, t * P:(t + 1) * P], w[:, k % 2, :],
                                   start=(k == 0), stop=(k == KT - 1))
                    ins.then_inc(full["big"], 1)
            pe.wait_ge(late_in, 16 * 6)
            lb = pe_bank(pe, "sc", "logits")
            for t in range(NT):
                pe.wait_ge(h2_ready, t + 1)
                for half in range(2):
                    bank = pe_bank(pe, "tp", ("h2", t, half))
                    for k in range(4):
                        ins = turn(bank[:, k * P:(k + 1) * P], h2[:, t, (4 * half + k) * P:(4 * half + k + 1) * P])
                    ins.then_inc(full["tp"], 1)
                for half in range(2):
                    pe.wait_ge(*emptied("tp", ("h2", t, half)))
                for k in range(KT):
                    ins = mmul(lb[:, t * (NGRP + E):(t + 1) * (NGRP + E)], h2T[:, k, t * P:(t + 1) * P], wge[:, k, :],
                               start=(k == 0), stop=(k == KT - 1))
            ins.then_inc(full["sc"], 1)
            rb = pe_bank(pe, "sc", "rank")
            pe.wait_ge(mask_ready, 1)
            for t in range(NT + 1):
                for i in range(min(t + 1, NT)):
                    m = K_TRI if i == t else K_ONE
                    ins = mmul(rb[:, t * E:(t + 1) * E], cst[:, m:m + P], rt[7][:, i, :],
                               start=(i == 0), stop=(i == min(t, NT - 1)))
            ins.then_inc(full["sc"], 1)

            pe.wait_ge(n_ready, 1)
            rest = pe.value_load(ntot[0:1, 0:1], min_val=E - 4, max_val=MAXR * E - 4)

            def turn_rows(i, h, first):
                pe.wait_ge(xg_in[h], (i + (2 - h)) * 8)
                if not first:
                    pe.wait_ge(xgT_a, i)
                    pe.wait_ge(xgT_v, i)
                for k in range(KT):
                    ins = turn(banks["tp"][k // 4][:, (k % 4) * P:(k % 4 + 1) * P], xg[:, h, k * P:(k + 1) * P])
                ins.then_inc(xg_turned, 1)

            def hidden(i, h, first):
                pe.wait_ge(ew_in[3 * h], (i + (2 - h)) * 8)
                pe.wait_ge(ew_in[3 * h + 1], (i + (2 - h)) * 8)
                pe.wait_ge(xgT_a, i + 1)
                pe.wait_ge(xgT_v, i + 1)
                if not first:
                    pe.wait_ge(hh_ready, i)
                w = r1[:, 3 * h * SLAB:(3 * h + 2) * SLAB].rearrange("p (w k f) -> p k w f", w=2, k=KT)
                for k in range(KT):
                    ins = mmul(banks["sc"][0][:, :].rearrange("p (w f) -> p w f", w=2), xgT[:, h, k, :], w[:, k],
                               start=(k == 0), stop=(k == KT - 1))
                ins.then_inc(hid_full, 1)

            def outputs(i, h, second):
                pe.wait_ge(hh_ready, i + 1)
                for k in range(2):
                    ins = turn(banks["sc"][1][:, k * P:(k + 1) * P], hh[:, h, k * P:(k + 1) * P])
                ins.then_inc(hT_full, 1)
                pe.wait_ge(ew_in[3 * h + 2], (i + (2 - h)) * 8)
                pe.wait_ge(hT_ready, i + 1)
                if not second:
                    pe.wait_ge(yb_a, i - 1)
                    pe.wait_ge(yb_v, i - 1)
                w = r1[:, (3 * h + 2) * SLAB:(3 * h + 3) * SLAB].rearrange("p (k f) -> p k f", k=2)
                for q in range(2):
                    for k in range(2):
                        ins = mmul(banks["big"][2 * h + q][:, :], hT[:, h, k, :], w[:, k, q * 512:(q + 1) * 512],
                                   start=(k == 0), stop=(k == 1))
                ins.then_inc(y_full, 1)

            turn_rows(0, 0, True)
            hidden(0, 0, True)
            turn_rows(1, 1, False)
            outputs(0, 0, True)
            hidden(1, 1, False)
            turn_rows(2, 0, False)
            outputs(1, 1, True)
            hidden(2, 0, False)
            with pe.Fori(3, rest + 3, 2) as g:
                for i, h in ((g, 1), (g + 1, 0)):
                    turn_rows(i, h, False)
                    outputs(i - 1, 1 - h, False)
                    hidden(i, h, False)
            turn_rows(rest + 3, 1, False)
            outputs(rest + 2, 0, False)
            hidden(rest + 3, 1, False)
            outputs(rest + 3, 1, False)

        @block.scalar
        def _(act_e):
            steps = [0]
            fn = nc.scalar.activation

            def link(ins):
                steps[0] += 1
                ins.then_inc(act_step, 1)
                act_e.wait_ge(act_step, steps[0])

            def emptying(ring, ins):
                ins.then_inc(free[ring, "a"], 1)

            load = act_e.dma_start
            load(cst[:, :], consts).then_inc(cst_in, 16)
            load(tok[:, :], token_ids).then_inc(cst_in, 16)
            load(lstep[64:96, :], log_step.rearrange("d (g h) -> (d g) h", h=2)).then_inc(srow_in, 16)
            load(srows[0:32, :], a_re.rearrange("d (g h) n -> (d g) (h n)", h=2)).then_inc(srow_in, 16)
            load(srows[32:64, :], a_im.rearrange("d (g h) n -> (d g) (h n)", h=2)).then_inc(srow_in, 16)
            for row, rows, src in ((R_G1, KT, norm1_g.rearrange("(r p) -> r p", p=P)),
                                   (R_CW, CONV * CT, conv_w.rearrange("w (r p) -> (w r) p", p=P)),
                                   (R_CB, CT, conv_b.rearrange("(r p) -> r p", p=P)),
                                   (R_BR, 2 * CT, b_r.rearrange("d (r p) -> (d r) p", p=P)),
                                   (R_BI, 2 * CT, b_i.rearrange("d (r p) -> (d r) p", p=P)),
                                   (R_LAM, 2 * CT, lam.rearrange("d (r p) -> (d r) p", p=P)),
                                   (R_BG, 2 * CT, b_glu.rearrange("(r p) -> r p", p=P))):
                load(prows[row:row + rows, :], src).then_inc(prow_in, 16)
            load(sink, attn_sink.partition_broadcast(P)).then_inc(prow_in, 16)
            load(dskip[:, :], d_skip.rearrange("(g q) -> q g", q=2 * C), allow_slow_non_contiguous=True).then_inc(dskip_in, 16)
            for w, src in enumerate((w_r, w_i)):
                for h in range(2):
                    for d in range(2):
                        load(wri[h * LB:(h + 1) * LB, w, d],
                             src[d].rearrange("(c h) i j -> h i c j", h=2)[h]).then_inc(lru_w_in, 16)
            for r, src in enumerate((b_re, b_im)):
                for d in range(2):
                    load(bin_[:, r, d * GP:(d + 1) * GP, :],
                         src[d].rearrange("(g h) n c -> (h n) g c", h=2)).then_inc(early_in, 16)
            for r, src in enumerate((c_re, c_im)):
                for h in range(2):
                    load(crow[:, r, :, h, :], src.rearrange("(t g) c n -> (g c) t n", t=CT)).then_inc(early_in, 16)
            for t in range(NT):
                act_e.wait_ge(x_in, 16 * NT)
                fn(act[:, t * D:(t + 1) * D], xt[:, t, :], ACT.Square, accum_out=ssq[:, t:t + 1]).then_inc(squares, 1)
            act_e.wait_ge(mean_ready, 1)
            fn(rstd, ssq, ACT.Sqrt).then_inc(root_ready, 1)
            act_e.wait_ge(srow_in, 16 * 3)
            fn(lstep[64:96, :], lstep[64:96, :], ACT.Exp).then_inc(step_exp, 1)
            bank = full_bank(act_e, "tp", "prm")
            emptying("tp", fn(prm[:, :], bank[:, 0:R_END], ACT.Copy))
            act_e.wait_ge(free["tp", "a"], 1)

            def split_hi(m):
                if m < len(ORDER):
                    act_e.wait_ge(raw_in[m % WR], slab_count(raw_slabs, m, WR))
                    fn(wh[:, m % 2, :], wraw[:, m % WR, :], ACT.Copy).then_inc(hi_ready, 1)

            def projected(key, dst, f, **more):
                bank = full_bank(act_e, "big", key)
                emptying("big", fn(dst, bank[:, :], f, **more))
                split_hi(ORDER.index(key) + 2)

            for k in range(KT):
                bank = full_bank(act_e, "tp", ("x", k))
                fn(hnh[:, k, :], bank[:, :], ACT.Identity, scale=prm[:, R_G1 + k:R_G1 + k + 1]).then_inc(x_hi, 1)
                if k < 2:
                    split_hi(k)
            act_e.wait_ge(cl_arg, 1)
            fn(lt[:, 1, :], lt[:, 0, :], ACT.Exp).then_inc(cl_exp, 1)
            act_e.wait_ge(s5_arg, 1)
            fn(s5t[:, 1, :], s5t[:, 0, :], ACT.Exp).then_inc(s5_act, 1)
            act_e.wait_ge(s5_arg, 2)
            fn(cs[:, :, :], s5t[:, 2:4, :], ACT.Sin).then_inc(s5_act, 1)
            for n in range(CT):
                projected(("u", n), uT[:, n, :], ACT.Copy)
            for n in range(CT):
                projected(("xr", n), xrv[:, n, 2:T + 2], ACT.Copy)
            projected("k", kT, ACT.Copy)
            projected("v", vS.rearrange("p t c -> p (t c)"), ACT.Copy)
            for ct in range(CT):
                for half in range(2):
                    if ct:
                        act_e.wait_ge(full["tp"], TP.index(("U", ct - 1)) + 1)
                    bank = full_bank(act_e, "tp", ("x2", ct, half))
                    emptying("tp", fn(x2[:, :, half * 4:half * 4 + 4, :].rearrange("p g j c -> p j g c"),
                                      bank[0:NC, :].rearrange("p (j g c) -> p j g c", j=4, g=8), ACT.Copy))
            act_e.wait_ge(cl_ready, 1)
            for ct in range(CT):
                for j in range(2):
                    n = 2 * (ct % 2) + j
                    if ct < 2:
                        projected(("gr", n), olru[:, n, :], ACT.Gelu_apprx_tanh)
                    else:
                        projected(("q", n), qT[:, n, :], ACT.Copy, scale=SCALE)
                if ct:
                    act_e.wait_ge(full["sc"], SC.index(("st", 2 * ct - 1)) + 1)
                for g4 in range(4):
                    bank = full_bank(act_e, "tp", ("w", ct, g4))
                    emptying("tp", fn(wt[:, g4].rearrange("p d n -> p (d n)"), bank[:, :], ACT.Copy))
                if ct:
                    act_e.wait_ge(lru_out, ct)
                for w, dst, row in ((0, l_r, R_BR), (1, l_i, R_BI)):
                    for d in range(2):
                        bank = full_bank(act_e, "big", ("lru", ct, w, d))
                        col = row + d * CT + ct
                        emptying("big", fn(dst[:, d, :], bank[:, :], ACT.Sigmoid, bias=prm[:, col:col + 1]))
                act_e.wait_ge(*emptied("big", ("lru", ct, 0, 1)))
                for f, dst in ((ACT.Tanh, l_v), (ACT.Exp, l_a)):
                    for d in range(2):
                        fn(dst[:, d, :], l_r[:, d, :], f, scale=cl[:, d * CT + ct:d * CT + ct + 1]).then_inc(lru_ta, 1)
                act_e.wait_ge(lru_q, ct + 1)
                fn(l_q[:, :, :], l_v[:, :, :], ACT.Sqrt).then_inc(lru_s, 1)

            def softmax_exp(u):
                n = key_blocks(u // 2)[1]
                b = u % 2
                act_e.wait_ge(s_max, u + 1)
                for i in range(GQ):
                    fn(pr[:, b, i, 0:n * P], pr[:, b, i, 0:n * P], ACT.Exp, bias=anm[:, b, i:i + 1],
                       accum_out=asum[:, b, i:i + 1])
                fn(aes[:, b, :], aes[:, b, :], ACT.Exp).then_inc(s_exp, 1)

            def gate(b, d):
                n = gate_n[0]
                gate_n[0] += 1
                if b == 2:
                    dst = sgate[:, d, :]
                else:
                    if n >= 2:
                        act_e.wait_ge(gate_used, n - 1)
                    dst = gbuf[:, n % 2, :]
                projected(("g", b, d), dst, ACT.Sigmoid)

            gate_n = [0]
            act_e.wait_ge(conv_done, CT)
            softmax_exp(0)
            for d in range(KT):
                if d + 1 < KT:
                    softmax_exp(d + 1)
                for k in range(0, key_blocks(d // 2)[1], 2):
                    if d:
                        act_e.wait_ge(full["big"], BIG.index(("pv", d - 1)) + 1)
                    bank = full_bank(act_e, "tp", ("p", d, k))
                    emptying("tp", fn(pT[:, k, :], bank[:, :], ACT.Copy))
                gate(1, d)
            def ssm_matrices(ct):
                act_e.wait_ge(kx_ready, ct + 1)
                for j in range(L):
                    for h in range(2):
                        load(mms[ct][j * C:(j + 1) * C].rearrange("p (g h) m -> p g h m", h=2)[:, :, h, :],
                             kx[h * C:(h + 1) * C, :, (L - 1 - j) * C:(L - 1 - j) * C + P]).then_inc(mm_in, 16)

            def ssm_products(ct):
                for h in range(2):
                    bank = full_bank(act_e, "big", ("y1", ct, h))
                    if ct:
                        act_e.wait_ge(full["tp"], TP.index(("y2", ct - 1, 1)) + 1)
                    emptying("big", fn(y1.rearrange("p (g h) k -> p g h k", h=2)[:, :, h, :],
                                       bank[:, 0:4 * NC].rearrange("p (g k) -> p g k", g=4), ACT.Copy))

            def ssm_to_channels(ct):
                bank = full_bank(act_e, "tp", ("y3", ct))
                emptying("tp", fn(xcv[:, ct, :].rearrange("p (k j) -> p j k", j=L),
                                  bank[:, :].rearrange("p (j k) -> p j k", j=L), ACT.Gelu_apprx_tanh))

            steps_of = {"M": ssm_matrices, "Y1": ssm_products, "Y3": ssm_to_channels}
            for b in (0, 2):
                for d in range(KT):
                    gate(b, d)
                    for step, ct in SSM_STEPS.get((b, d), []):
                        if step in steps_of:
                            steps_of[step](ct)
            for n in range(CT):
                bank = full_bank(act_e, "big", ("z1", n))
                if n == 0:
                    act_e.wait_ge(gate_used, 2 * KT)
                if n >= 2:
                    act_e.wait_ge(glu_ready, n - 1)
                emptying("big", fn(gbuf[:, n % 2, :], bank[:, :], ACT.Sigmoid, bias=prm[:, R_BG + CT + n:R_BG + CT + n + 1]))
            act_e.wait_ge(full["big"], BIG.index(("p", 2, KT - 1)) + 1)
            for t in range(NT):
                act_e.wait_ge(*emptied("big", ("wo", t, 1)))
                fn(act[:, t * D:(t + 1) * D], xres[:, t, :], ACT.Square, accum_out=ssq2[:, t:t + 1]).then_inc(x1_sq, 1)
                act_e.wait_ge(mean_ready, 2 + t)
                fn(rstd2[:, t:t + 1], ssq2[:, t:t + 1], ACT.Sqrt).then_inc(x1_root, 1)
            for t in range(NT):
                bank = full_bank(act_e, "tp", ("h2", t, 0))
                emptying("tp", fn(h2T[:, 0:4, t * P:(t + 1) * P], bank[:, :].rearrange("p (k s) -> p k s", k=4), ACT.Copy))
            act_e.wait_ge(w_arg, 1)
            fn(rg[3], rg[2], ACT.Exp).then_inc(w_exp, 1)
            act_e.wait_ge(w_arg, 2)
            fn(rs[8], rs[7], ACT.Exp).then_inc(w_exp, 1)

            act_e.wait_ge(n_ready, 1)
            rest = act_e.value_load(ntot[0:1, 0:1], min_val=E - 4, max_val=MAXR * E - 4)

            def rows_in(i, h, second):
                act_e.wait_ge(xg_turned, i + 1)
                if not second:
                    act_e.wait_ge(hid_full, i - 1)
                fn(xgT[:, h, 0:4, :], banks["tp"][0][:, :].rearrange("p (k s) -> p k s", k=4), ACT.Copy).then_inc(xgT_a, 1)

            def silu(i, h, second):
                act_e.wait_ge(hid_full, i + 1)
                if not second:
                    act_e.wait_ge(hh_ready, i - 1)
                fn(sg[:, h, :], banks["sc"][0][:, 0:FE], ACT.Silu).then_inc(silu_done, 1)

            def rows_done(i, h):
                act_e.wait_ge(y_full, i + 1)
                act_e.wait_ge(rows_out[h], (i - h) * 8)
                fn(yb[:, h, 0:512], banks["big"][2 * h][:, :], ACT.Copy).then_inc(yb_a, 1)

            act_e.wait_ge(full["sc"], SC.index("rank") + 1)
            rows_in(0, 0, True)
            silu(0, 0, True)
            rows_in(1, 1, True)
            rows_done(0, 0)
            silu(1, 1, True)
            rows_in(2, 0, False)
            rows_done(1, 1)
            silu(2, 0, False)
            with act_e.Fori(3, rest + 3, 2) as g:
                for i, h in ((g, 1), (g + 1, 0)):
                    rows_in(i, h, False)
                    rows_done(i - 1, 1 - h)
                    silu(i, h, False)
            rows_in(rest + 3, 1, False)
            rows_done(rest + 2, 0)
            silu(rest + 3, 1, False)
            rows_done(rest + 3, 1)
            for t in range(NT):
                act_e.wait_ge(acc_ready, t + 1)
                fn(act[:, t * D:(t + 1) * D], xres[:, t, :], ACT.Square, accum_out=ssq3[:, t:t + 1]).then_inc(out_sq, 1)
                act_e.wait_ge(mean_ready, 2 + NT + t)
                fn(rstd3[:, t:t + 1], ssq3[:, t:t + 1], ACT.Sqrt).then_inc(out_root, 1)

        @block.vector
        def _(dve):
            steps = [0]
            tt, ts, stt = nc.vector.tensor_tensor, nc.vector.tensor_scalar, nc.vector.scalar_tensor_tensor

            def link(ins):
                steps[0] += 1
                ins.then_inc(dve_step, 1)
                dve.wait_ge(dve_step, steps[0])

            def emptying(ring, ins):
                ins.then_inc(free[ring, "v"], 1)

            dve.wait_ge(squares, NT)
            ts(ssq, ssq, 1.0 / D, EPS, MUL, ADD).then_inc(mean_ready, 1)
            dve.wait_ge(root_ready, 1)
            link(nc.vector.reciprocal(rstd, rstd))
            for t in range(NT):
                ts(xs[:, t, :], xt[:, t, :], rstd[:, t:t + 1], None, MUL).then_inc(xs_ready, 1)
            dve.wait_ge(step_exp, 1)
            nc.vector.tensor_copy(srows[64:96, :].rearrange("p (h n) -> p h n", h=2), bc(lstep[64:96, :], 2, N)).then_inc(srows_ready, 1)
            bank = full_bank(dve, "tp", "s5p")
            emptying("tp", nc.vector.tensor_copy(s5p[:, :], bank[:, 0:96]))
            dve.wait_ge(*emptied("tp", "prm"))
            for k in range(KT):
                bank = full_bank(dve, "tp", ("x", k))
                dve.wait_ge(x_hi, k + 1)
                emptying("tp", stt(hnl[:, k, :], bank[:, :], prm[:, R_G1 + k:R_G1 + k + 1],
                                   hnh[:, k, :].bitcast(f32), MUL, SUB))
            lm = prm[:, R_LAM:R_LAM + 2 * CT]
            stt(lt[:, 0, :], lm, -1.0, lm, MUL, ALU.min).then_inc(cl_arg, 1)
            dve.wait_ge(cl_exp, 1)
            link(ts(lt[:, 2, :], lt[:, 1, :], 2.0, None, ADD))
            link(nc.vector.reciprocal(lt[:, 2, :], lt[:, 2, :]))
            link(tt(lt[:, 0, :], lt[:, 1, :], lt[:, 2, :], MUL))
            link(tt(lt[:, 1, :], lt[:, 0, :], lt[:, 0, :], MUL))
            link(ts(lt[:, 2, :], lt[:, 1, :], 1.0 / 15, None, MUL))
            for m in (13, 11, 9, 7, 5, 3):
                link(stt(lt[:, 2, :], lt[:, 2, :], 1.0 / m, lt[:, 1, :], ADD, MUL))
            link(stt(lt[:, 2, :], lt[:, 2, :], 1.0, lt[:, 0, :], ADD, MUL))
            link(ts(lt[:, 3, :], lm, -1.0, 0.0, MUL, MAX))
            link(stt(lt[:, 3, :], lt[:, 2, :], 2.0, lt[:, 3, :], MUL, ADD))
            ts(cl, lt[:, 3, :], -LRU_C, None, MUL).then_inc(cl_ready, 1)
            ar, ai, st = s5p[:, 0:32], s5p[:, 32:64], s5p[:, 64:96]
            q = [s5t[:, i, :] for i in range(16)]
            dve.wait_ge(*emptied("tp", "s5p"))
            tt(q[0], ar, st, MUL).then_inc(s5_arg, 1)
            link(tt(q[4], ai, st, MUL))
            big = 1.5 * 2.0 ** 23
            link(ts(q[5], q[4], 1.0 / (2 * np.pi), big, MUL, ADD))
            link(ts(q[5], q[5], -big, None, ADD))
            c1 = 6.28125
            c2 = float(np.float32(np.round((2 * np.pi - c1) * 2.0 ** 20) / 2.0 ** 20))
            for c in (c1, c2, 2 * np.pi - c1 - c2):
                link(stt(q[4], q[5], -c, q[4], MUL, ADD))
            link(ts(q[3], q[4], 3.1415925, -3.1415925, ALU.min, MAX))
            link(stt(q[2], q[3], -1.0, q[3], MUL, ALU.min))
            ts(q[2], q[2], float(np.pi / 2), None, ADD).then_inc(s5_arg, 1)
            dve.wait_ge(s5_act, 2)
            link(tt(pw[:, 0, 1, :], q[1], cs[:, 0, :], MUL))
            link(tt(pw[:, 1, 1, :], q[1], cs[:, 1, :], MUL))
            link(nc.vector.memset(pw[:, 0, 0, :], 1.0))
            link(nc.vector.memset(pw[:, 1, 0, :], 0.0))
            nr, ni = q[5], pw[:, 1, 1, :]
            link(ts(nr, pw[:, 0, 1, :], -1.0, None, ADD))
            link(tt(q[6], ar, ar, MUL))
            link(tt(q[7], ai, ai, MUL))
            link(tt(q[6], q[6], q[7], ADD))
            link(nc.vector.reciprocal(q[6], q[6]))
            link(tt(q[7], nr, ar, MUL))
            link(tt(q[8], ni, ai, MUL))
            link(tt(q[7], q[7], q[8], ADD))
            link(tt(q[7], q[7], q[6], MUL))
            link(tt(q[8], ni, ar, MUL))
            link(tt(q[9], nr, ai, MUL))
            link(tt(q[8], q[8], q[9], SUB))
            link(tt(q[8], q[8], q[6], MUL))
            dve.wait_ge(early_in, 16 * 8)
            sr, si = bc(q[7], 2, C), bc(q[8], 2, C)
            bbv = bb[:, :, :, :].rearrange("p (d r) g c -> p d r g c", d=2)
            bt = [btmp[:, a].rearrange("p (d g) c -> p d g c", d=2) for a in range(2)]
            for r, (x0, x1, op) in enumerate(((0, 1, SUB), (1, 0, ADD))):
                link(tt(btmp[:, 0], sr, bin_[:, x0], MUL))
                link(tt(btmp[:, 1], si, bin_[:, x1], MUL))
                link(tt(bbv[:, :, r], bt[0], bt[1], op))
            for lo, n, by in ((1, 1, 1), (1, 2, 2), (1, 4, 4)):
                xr_, xi_ = pw[:, 0, lo:lo + n, :], pw[:, 1, lo:lo + n, :]
                yr_, yi_ = bc(pw[:, 0, by, :], 1, n), bc(pw[:, 1, by, :], 1, n)
                dst = slice(lo + by, lo + by + n)
                ta = s5t[:, 8:8 + n, :]
                tb = s5t[:, 12:12 + n, :]
                link(tt(ta, xr_, yr_, MUL))
                link(tt(tb, xi_, yi_, MUL))
                link(tt(pw[:, 0, dst, :], ta, tb, SUB))
                link(tt(ta, xr_, yi_, MUL))
                link(tt(tb, xi_, yr_, MUL))
                link(tt(pw[:, 1, dst, :], ta, tb, ADD))
            for d in range(2):
                cols = slice(d * GP, (d + 1) * GP)
                link(nc.vector.tensor_copy(aa[:, 0, 2 * d, :], pw[:, 0, L, cols]))
                link(nc.vector.tensor_copy(aa[:, 0, 2 * d + 1, :], pw[:, 0, L, cols]))
                link(nc.vector.tensor_copy(aa[:, 1, 2 * d, :], pw[:, 1, L, cols]))
                link(ts(aa[:, 1, 2 * d + 1, :], pw[:, 1, L, cols], -1.0, None, MUL))
            dve.wait_ge(dskip_in, 16)
            tt(dd[:, :, :], bc(dskip[:, :], 2, C), bc(cst[0:2 * C, K_DLT:K_DLT + C], 1, GP), MUL).then_inc(s5_tab, 1)
            for r in range(2):
                bank = full_bank(dve, "tp", ("c", r))
                for h in range(2):
                    rows = slice(h * N, (h + 1) * N)
                    src = bank[rows, :].rearrange("p (g h c) -> p g h c", h=2, c=C)[:, :, h, :]
                    ins = nc.vector.tensor_copy(cc[rows, r], src)
                emptying("tp", ins)
            dve.wait_ge(pad_zero, 2)
            for ct in range(CT):
                dve.wait_ge(*emptied("big", ("xr", ct)))
                w = [prm[:, R_CW + i * CT + ct:R_CW + i * CT + ct + 1] for i in range(CONV)]
                link(ts(xcv[:, ct, :], xrv[:, ct, 0:T], w[0], prm[:, R_CB + ct:R_CB + ct + 1], MUL, ADD))
                for i in range(1, CONV - 1):
                    link(stt(xcv[:, ct, :], xrv[:, ct, i:i + T], w[i], xcv[:, ct, :], MUL, ADD))
                stt(xcv[:, ct, :], xrv[:, ct, 3:3 + T], w[3], xcv[:, ct, :], MUL, ADD).then_inc(conv_done, 1)
            for ct in range(CT):
                bank = full_bank(dve, "tp", ("U", ct))
                emptying("tp", nc.vector.tensor_copy(Uv[:, 8 * ct:8 * ct + 8, :].rearrange("p g k -> p (g k)"), bank[:, :]))
            def rest_of(key):
                if ORDER.index(key) + 2 < len(ORDER):
                    split_lo(dve, tt, ORDER.index(key) + 2)

            dve.wait_ge(conv_done, CT)
            dve.wait_ge(x_zero, 1)
            for ct in range(CT):
                for j in range(2):
                    rest_of(("gr" if ct < 2 else "q", 2 * (ct % 2) + j))
                for d in (2 * ct, 2 * ct + 1):
                    bank = full_bank(dve, "sc", ("st", d))
                    emptying("sc", nc.vector.tensor_copy(Xv[:, :, 2 * d:2 * d + 2, 1:NC + 1],
                                                         bank[:, :].rearrange("p (q g k) -> p q g k", q=4, g=2)))
                dve.wait_ge(*emptied("big", ("lru", ct, 1, 1)))
                tt(l_i[:, :, :], l_i[:, :, :], bc(xcv[:, ct, :], 1, 2), MUL)
                dve.wait_ge(lru_ta, 4 * ct + 2)
                link(ts(l_q[:, :, :], l_v[:, :, :], -1.0, 1.0, MUL, ADD))
                link(nc.vector.reciprocal(l_q[:, :, :], l_q[:, :, :]))
                stt(l_v[:, :, :], l_v[:, :, :], -2.0, l_q[:, :, :], MUL, MUL).then_inc(lru_q, 1)
                dve.wait_ge(lru_s, ct + 1)
                dve.wait_ge(lru_ta, 4 * ct + 4)
                link(tt(l_i[:, :, :], l_i[:, :, :], l_q[:, :, :], MUL))
                nc.vector.tensor_tensor_scan(l_v[:, 0, :], l_a[:, 0, :], l_i[:, 0, :], 0.0, MUL, ADD)
                link(nc.vector.tensor_tensor_scan(l_v[:, 1, ::-1], l_a[:, 1, ::-1], l_i[:, 1, ::-1], 0.0, MUL, ADD))
                link(tt(l_v[:, 0, :], l_v[:, 0, :], l_v[:, 1, :], ADD))
                dve.wait_ge(*emptied("big", ("gr", ct)))
                tt(olru[:, ct, :], olru[:, ct, :], l_v[:, 0, :], MUL).then_inc(lru_out, 1)

            dve.wait_ge(btab_ready, NQ)
            dve.wait_ge(prow_in, 16 * 8)

            def softmax_max(u):
                nb, hk = u // 2, u % 2
                lo, n = key_blocks(nb)
                off = (lo - nb + 1) * P
                b = u % 2
                for i in range(GQ):
                    bank = full_bank(dve, "sc", ("s", u, i))
                    h = hk * GQ + i
                    if i == 0 and u >= 2:
                        dve.wait_ge(full["tp"], TP.index(("p", u - 2, key_blocks((u - 2) // 2)[1] - 1)) + 1)
                    emptying("sc", nc.vector.tensor_tensor_reduce(
                        out=pr[:, b, i, 0:n * P], in0=bank[:, 0:n * P], in1=btab[:, h, off:off + n * P], scale=1.0,
                        scalar=sink[:, h:h + 1], op0=ADD, op1=MAX, accum_out=am[:, b, i:i + 1]))
                dve.wait_ge(*emptied("sc", ("s", u, GQ - 1)))
                ts(anm[:, b, :], am[:, b, :], -1.0, None, MUL)
                tt(aes[:, b, :], sink[:, hk * GQ:(hk + 1) * GQ], am[:, b, :], SUB).then_inc(s_max, 1)

            def softmax_scale(u):
                n = key_blocks(u // 2)[1]
                b = u % 2
                dve.wait_ge(s_exp, u + 1)
                link(tt(ard[:, b, :], asum[:, b, :], aes[:, b, :], ADD))
                link(nc.vector.reciprocal(ard[:, b, :], ard[:, b, :]))
                for i in range(GQ):
                    ins = ts(pr[:, b, i, 0:n * P], pr[:, b, i, 0:n * P], ard[:, b, i:i + 1], None, MUL)
                ins.then_inc(s_prob, 1)

            gate_n = [0]

            def gated(b, d):
                bank = full_bank(dve, "big", ("p", b, d))
                dve.wait_ge(*emptied("big", ("g", b, d)))
                g = sgate[:, d, :] if b == 2 else gbuf[:, gate_n[0] % 2, :]
                gate_n[0] += 1
                if b == 1:
                    emptying("big", tt(mixed[:, d, :], bank[:, :], g, MUL))
                    dve.wait_ge(*emptied("big", ("p", b, d)))
                    dve.nop().then_inc(gate_used, 1)
                else:
                    emptying("big", tt(g, bank[:, :], g, MUL))
                    dve.wait_ge(*emptied("big", ("p", b, d)))
                    tt(mixed[:, d, :], mixed[:, d, :], g, ADD).then_inc(gate_used, 1)

            softmax_max(0)
            softmax_scale(0)
            for d in range(KT):
                if d:
                    rest_of(("g", 1, d - 1))
                if d + 1 < KT:
                    softmax_max(d + 1)
                for k in range(1, key_blocks(d // 2)[1], 2):
                    if d:
                        dve.wait_ge(full["big"], BIG.index(("pv", d - 1)) + 1)
                    bank = full_bank(dve, "tp", ("p", d, k))
                    emptying("tp", nc.vector.tensor_copy(pT[:, k, :], bank[:, :]))
                if d + 1 < KT:
                    softmax_scale(d + 1)
                rows = slice((d % 2) * HD, (d % 2 + 1) * HD)
                bank = full_bank(dve, "big", ("pv", d))
                emptying("big", nc.vector.tensor_copy(oatt[rows, :, (d // 2) * P:(d // 2 + 1) * P],
                                                      bank[rows, :].rearrange("p (i q) -> p i q", i=GQ)))
                gated(1, d)
            def c_powers(ct):
                b = ct % 2
                if ct >= 2:
                    dve.wait_ge(full["big"], BIG.index(("y1", ct - 2, 1)) + 1)
                tv = [t.rearrange("p (g j c) -> p g j c", g=4, j=L + 1) for t in (tmpC, tmpD)]
                for d in range(2):
                    cols = slice(d * GP + 4 * ct, d * GP + 4 * ct + 4)

                    def power(r):
                        rows = pw[:, r, 0:L + 1, cols] if d == 0 else pw[:, r, L::-1, cols]
                        return bc(rows.rearrange("p j g -> p g j"), 3, C)

                    def c_of(r):
                        return bc(cc[:, r, 4 * ct:4 * ct + 4, :], 2, L + 1)

                    link(tt(tv[0], power(0), c_of(0), MUL))
                    link(tt(tv[1], power(1), c_of(1), MUL))
                    link(tt(cp[:, b, 2 * d].rearrange("p g m -> p (g m)"), tmpC, tmpD, SUB))
                    link(tt(tv[0], power(0), c_of(1), MUL))
                    link(tt(tv[1], power(1), c_of(0), MUL))
                    stt(cp[:, b, 2 * d + 1].rearrange("p g m -> p (g m)"), tmpC, -1.0, tmpD, MUL, SUB).then_inc(cp_ready, 1)
                    dve.wait_ge(cp_ready, 2 * ct + d + 1)
                if ct:
                    dve.wait_ge(full["sc"], SC.index(("kb", ct - 1)) + 1)
                for h in range(2):
                    rows = slice(h * N, (h + 1) * N)
                    nc.vector.tensor_copy(bbd[rows, :, :, h, :], bb[rows, :, 4 * ct:4 * ct + 4, :]).then_inc(bbd_ready, 1)

            def lag_kernels(ct):
                kf = full_bank(dve, "sc", ("kf", ct))[0:2 * C, :].rearrange("p (g m) -> p g m", g=4)
                kb = full_bank(dve, "sc", ("kb", ct))[0:2 * C, :].rearrange("p (g m) -> p g m", g=4)
                if ct:
                    dve.wait_ge(mm_in, 16 * 2 * L * ct)
                link(nc.vector.tensor_copy(kx[:, :, (L - 1) * C:], kf))
                emptying("sc", tt(kx[:, :, (L - 1) * C:L * C], kx[:, :, (L - 1) * C:L * C], kb[:, :, (L - 1) * C:], ADD))
                emptying("sc", nc.vector.tensor_copy(kx[:, :, 0:(L - 1) * C], kb[:, :, 0:(L - 1) * C]))
                dve.wait_ge(*emptied("sc", ("kb", ct)))
                tt(kx[:, :, (L - 1) * C:L * C], kx[:, :, (L - 1) * C:L * C], dd[:, 4 * ct:4 * ct + 4, :], ADD).then_inc(kx_ready, 1)

            def ssm_to_chunks(ct):
                for half in range(2):
                    if ct and half == 0:
                        dve.wait_ge(full["tp"], TP.index(("y3", ct - 1)) + 1)
                    bank = full_bank(dve, "tp", ("y2", ct, half))
                    emptying("tp", nc.vector.tensor_copy(
                        y2[:, :, 4 * half:4 * half + 4, :].rearrange("p j g c -> p g j c"),
                        bank[0:NC, :].rearrange("p (g j c) -> p g j c", g=4, j=L)))

            link(nc.vector.memset(xrp[:, 1024:1536], 0.0))
            last = ("g", 1, KT - 1)
            for b in (0, 2):
                for d in range(KT):
                    rest_of(last)
                    last = ("g", b, d)
                    if (b, d) in C_POWERS:
                        c_powers(C_POWERS[b, d])
                    if b == 0:
                        gated(0, d)
                    for step, ct in SSM_STEPS.get((b, d), []):
                        if step == "K":
                            lag_kernels(ct)
                        if step == "Y2":
                            ssm_to_chunks(ct)
            for n in range(CT):
                bank = full_bank(dve, "big", ("z0", n))
                dve.wait_ge(*emptied("big", ("z1", n)))
                col = prm[:, R_BG + n:R_BG + n + 1]
                ins = stt(ossm[:, n, :], bank[:, :], col, gbuf[:, n % 2, :], ADD, MUL)
                emptying("big", ins)
                dve.wait_ge(*emptied("big", ("z0", n)))
                dve.nop().then_inc(glu_ready, 1)
            for d in range(KT):
                gated(2, d)
            dve.wait_ge(x_again, 16 * NT)
            dve.wait_ge(late_in, 16 * 6)
            for t in range(NT):
                for h in range(2):
                    bank = full_bank(dve, "big", ("wo", t, h))
                    half = xres[:, t, h * 512:(h + 1) * 512]
                    emptying("big", tt(half, bank[:, :], half, ADD))
                dve.wait_ge(x1_sq, t + 1)
                ts(ssq2[:, t:t + 1], ssq2[:, t:t + 1], 1.0 / D, EPS, MUL, ADD).then_inc(mean_ready, 1)
                dve.wait_ge(x1_root, t + 1)
                link(nc.vector.reciprocal(rstd2[:, t:t + 1], rstd2[:, t:t + 1]))
                stt(h2[:, t, :], xres[:, t, :], rstd2[:, t:t + 1], g2b, MUL, MUL).then_inc(h2_ready, 1)
            for t in range(NT):
                if t == 0:
                    dve.wait_ge(full["big"], BIG.index(("wo", NT - 1, 1)) + 1)
                bank = full_bank(dve, "tp", ("h2", t, 1))
                emptying("tp", nc.vector.tensor_copy(h2T[:, 4:8, t * P:(t + 1) * P], bank[:, :].rearrange("p (k s) -> p k s", k=4)))
            lg = xc[:, 960:1040].rearrange("p (t c) -> p t c", t=NT)
            bank = full_bank(dve, "sc", "logits")
            emptying("sc", tt(lg, bank[:, 0:NT * (NGRP + E)].rearrange("p (t c) -> p t c", t=NT), bc(bge, 1, NT), ADD))
            dve.wait_ge(*emptied("sc", "logits"))
            lgg, lge = lg[:, :, 0:NGRP], lg[:, :, NGRP:]

            def top(mask, values, peak, score, rank, n):
                link(nc.vector.tensor_reduce(peak, values, AX.X, MAX))
                link(tt(score, values, bc(peak, 2, n), ALU.is_equal))
                link(tt(score, score, bc(cst[:, K_REV:K_REV + n], 1, NT), MUL))
                link(nc.vector.tensor_reduce(rank, score, AX.X, MAX))
                link(tt(mask, score, bc(rank, 2, n), ALU.is_equal))

            top(rg[1], lgg, rs[0], rg[0], rs[1], NGRP)
            tt(rg[2], lgg, bc(rs[0], 2, NGRP), SUB).then_inc(w_arg, 1)
            link(ts(rg[4], rg[1], -NEG, NEG, MUL, ADD))
            g4 = "p t (g e) -> p t g e"
            link(tt(rt[1].rearrange(g4, g=NGRP), lge.rearrange(g4, g=NGRP), bc(rg[1], 3, 4), MUL))
            link(tt(rt[1].rearrange(g4, g=NGRP), rt[1].rearrange(g4, g=NGRP), bc(rg[4], 3, 4), ADD))
            top(rt[3], rt[1], rs[2], rt[2], rs[3], E)
            link(stt(rt[4], rt[3], 2 * NEG, rt[1], MUL, ADD))
            top(rt[5], rt[4], rs[4], rt[2], rs[5], E)
            tt(rs[7], rs[4], rs[2], SUB).then_inc(w_arg, 1)
            tt(rt[7], rt[3], rt[5], ADD).then_inc(mask_ready, 1)
            dve.wait_ge(w_exp, 2)
            link(nc.vector.tensor_reduce(rs[9], rg[3], AX.X, ADD))
            link(ts(rs[10], rs[8], 1.0, None, ADD))
            link(tt(rs[10], rs[10], rs[9], MUL))
            link(nc.vector.reciprocal(rs[11], rs[10]))
            link(tt(rs[12], rs[11], rs[8], MUL))
            bank = full_bank(dve, "sc", "rank")
            link(nc.vector.tensor_copy(rt[8], bank[:, 0:NT * E].rearrange("p (t e) -> p t e", t=NT)))
            cnt = rs[13][0:1, 0:1]
            rounds = rs[14][0:1, 0:1]
            part = rs[15][0:1, 0:1]
            emptying("sc", nc.vector.tensor_reduce(cnt, bank[0:1, NT * E:(NT + 1) * E], AX.X, MAX))
            dve.wait_ge(*emptied("sc", "rank"))
            link(ts(rounds, cnt, P + 0.5, 1.0, ALU.is_gt, ADD))
            link(ts(rt[9], rt[8], P - 0.5, float(ROUND - P), ALU.is_gt, MUL))
            for r in range(2, MAXR):
                link(ts(part, cnt, r * P + 0.5, None, ALU.is_gt))
                link(tt(rounds, rounds, part, ADD))
                link(ts(rt[10], rt[8], r * P - 0.5, float(ROUND - P), ALU.is_gt, MUL))
                link(tt(rt[9], rt[9], rt[10], ADD))
            link(ts(rounds, rounds, float(E), -4.0, MUL, ADD))
            nc.vector.tensor_copy(ntot[0:1, 0:1], rounds).then_inc(n_ready, 1)
            link(tt(rt[8], rt[8], rt[9], ADD))
            link(tt(rt[8], rt[8], bc(cst[:, K_E128:K_E128 + E], 1, NT), ADD))
            for c, mask in enumerate((rt[3], rt[5])):
                link(tt(rt[10], rt[8], mask, MUL))
                link(nc.vector.tensor_reduce(rs[5], rt[10], AX.X, ADD))
                nc.vector.tensor_copy(slot_i[:, c, :], rs[5]).then_inc(slots_ready, 1)
                dve.wait_ge(slots_ready, c + 1)

            rest = dve.value_load(ntot[0:1, 0:1], min_val=E - 4, max_val=MAXR * E - 4)

            def rows_in(i, h, second):
                dve.wait_ge(xg_turned, i + 1)
                if not second:
                    dve.wait_ge(hid_full, i - 1)
                nc.vector.tensor_copy(xgT[:, h, 4:8, :], banks["tp"][1][:, :].rearrange("p (k s) -> p k s", k=4)).then_inc(xgT_v, 1)

            def gated_hidden(i, h):
                dve.wait_ge(silu_done, i + 1)
                tt(hh[:, h, :], banks["sc"][0][:, FE:2 * FE], sg[:, h, :], MUL).then_inc(hh_ready, 1)

            def hidden_turned(i, h):
                dve.wait_ge(hT_full, i + 1)
                nc.vector.tensor_copy(hT[:, h].rearrange("p k s -> p (k s)"), banks["sc"][1][:, 0:2 * P]).then_inc(hT_ready, 1)

            def rows_done(i, h):
                dve.wait_ge(y_full, i + 1)
                dve.wait_ge(rows_out[h], (i - h) * 8)
                nc.vector.tensor_copy(yb[:, h, 512:1024], banks["big"][2 * h + 1][:, :]).then_inc(yb_v, 1)

            rows_in(0, 0, True)
            gated_hidden(0, 0)
            rows_in(1, 1, True)
            hidden_turned(0, 0)
            rows_done(0, 0)
            gated_hidden(1, 1)
            rows_in(2, 0, False)
            hidden_turned(1, 1)
            rows_done(1, 1)
            gated_hidden(2, 0)
            with dve.Fori(3, rest + 3, 2) as g:
                for i, h in ((g, 1), (g + 1, 0)):
                    rows_in(i, h, False)
                    hidden_turned(i - 1, 1 - h)
                    rows_done(i - 1, 1 - h)
                    gated_hidden(i, h)
            rows_in(rest + 3, 1, False)
            hidden_turned(rest + 2, 0)
            rows_done(rest + 2, 0)
            gated_hidden(rest + 3, 1)
            hidden_turned(rest + 3, 1)
            rows_done(rest + 3, 1)
            for t in range(NT):
                dve.wait_ge(yg_in[t], 32)
                for c in range(2):
                    src = pair[c][:, t, :]
                    ins = stt(xres[:, t, :], src, rs[11 + c][:, t:t + 1], xres[:, t, :], MUL, ADD)
                    if c:
                        ins.then_inc(acc_ready, 1)
                    else:
                        link(ins)
                dve.wait_ge(out_sq, t + 1)
                ts(ssq3[:, t:t + 1], ssq3[:, t:t + 1], 1.0 / D, EPS, MUL, ADD).then_inc(mean_ready, 1)
                dve.wait_ge(out_root, t + 1)
                link(nc.vector.reciprocal(rstd3[:, t:t + 1], rstd3[:, t:t + 1]))
                stt(xres[:, t, :], xres[:, t, :], rstd3[:, t:t + 1], fgb, MUL, MUL).then_inc(out_ready, 1)


_LAYERED = ["norm1_g", "w_in", "attn_sink", "lru_conv_w", "lru_conv_b", "lru_w_r", "lru_b_r", "lru_w_i", "lru_b_i",
            "lru_lambda", "ssm_a_re", "ssm_a_im", "ssm_log_step", "ssm_b_re", "ssm_b_im", "ssm_c_re", "ssm_c_im",
            "ssm_d", "ssm_w_glu", "ssm_b_glu", "w_branch", "w_out", "norm2_g", "moe_w_group", "moe_b_group",
            "moe_w_expert", "moe_b_expert", "moe_w1", "moe_w3", "moe_w2"]


def kernel(**inputs):
    import concourse.bacc as bacc
    from concourse.bass_utils import run_bass_kernel_spmd

    arrays = {"x": inputs["x"][0]}
    for name in _LAYERED:
        a = np.asarray(inputs[name])[0]
        if name.startswith("moe_w") and a.ndim == 4:
            a = a.reshape((E,) + a.shape[2:])
        arrays[name] = a
    arrays["final_norm_g"] = inputs["final_norm_g"]
    arrays["consts"], arrays["token_ids"] = constants()

    nc = bacc.Bacc("TRN2", target_bir_lowering=False, num_devices=1)
    ins, args = {}, []
    for name, a in arrays.items():
        a = np.ascontiguousarray(a)
        ins[f"in_{name}"] = a
        args.append(nc.dram_tensor(f"in_{name}", a.shape, mybir.dt.from_np(a.dtype), kind="ExternalInput").ap())
    args.append(nc.dram_tensor("out_0", (T, D), mybir.dt.float32, kind="ExternalOutput").ap())
    hybrid_block(nc, *args)
    r = run_bass_kernel_spmd(nc, [ins], core_ids=[0])
    return r.results[0]["out_0"].reshape(1, T, D)
```

```python
import numpy as np
import concourse.bass as bass
from concourse import mybir
from contextlib import ExitStack

T, D = 512, 1024
P = 128
NT, KT = T // P, D // P
NQ, NKV, HD = 8, 2, 64
GQ = NQ // NKV
BW = D // 2
CT = BW // P
NBR = 3
COL_K, COL_V = BW, BW + NKV * HD
COL_XR = BW + 2 * NKV * HD
COL_GR, COL_U = COL_XR + BW, COL_XR + 2 * BW
COL_GATE = COL_XR + 3 * BW
CONV = 4
LB = 64
LRU_C = 8.0
G, C, N = 32, 16, 64
L = 8
NC = T // L
GP = G // 2
E, FE, NGRP = 16, 256, 4
SLAB = 2048
ROUND = E * P
MAXR = T // P
IW = 8
KC = 4
KC_K = KT // KC
EPS = 1e-6
NEG = -1e30
SCALE = HD ** -0.5

K_ID, K_DIST, K_TRI, K_ONE, K_E128, K_REV, K_DLT, K_END = 0, 128, 512, 640, 768, 784, 800, 816

R_G1, R_CW, R_CB, R_BR, R_BI, R_LAM, R_BG, R_END = 0, 8, 24, 28, 36, 44, 52, 60


def constants():
    c = np.zeros((P, K_END), np.float32)
    p = np.arange(P)
    c[:, K_ID:K_ID + P] = np.eye(P)
    rel = p[:, None] - np.arange(3 * P)[None, :] + P
    c[:, K_DIST:K_DIST + 3 * P] = np.where(np.abs(rel) <= P, -np.abs(rel), NEG * 256.0)
    c[:, K_TRI:K_TRI + P] = p[:, None] < p[None, :]
    c[:, K_ONE:K_ONE + P] = 1.0
    c[:, K_E128:K_E128 + E] = np.arange(E) * P
    c[:, K_REV:K_REV + E] = E - np.arange(E)
    c[:, K_DLT:K_DLT + C] = (p[:, None] % C) == np.arange(C)[None, :]
    token = p[:, None, None] + P * np.arange(NT)[None, None, :] + 0 * np.arange(2)[None, :, None]
    ids = np.stack([token, 2 * token + np.arange(2)[None, :, None]], axis=-1).astype(np.int32)
    return c, ids


class Ring:

    def __init__(self, size):
        self.size, self.jobs = size, []

    def add(self, key, by):
        self.jobs.append((key, by))

    def index(self, key):
        return next(n for n, (k, _) in enumerate(self.jobs) if k == key)

    def emptied(self, n):
        by = self.jobs[n][1]
        return by, sum(1 for _, b in self.jobs[:n + 1] if b == by)


def key_blocks(nb):
    lo, hi = max(0, nb - 1), min(NT - 1, nb + 1)
    return lo, hi - lo + 1


SSM_STEPS = {
    (0, 0): [("R", 0)], (0, 2): [("K", 0)], (0, 3): [("M", 0)], (0, 4): [("K", 1), ("Y", 0)], (0, 5): [("Z", 0), ("M", 1)],
    (0, 6): [("Y", 1)], (0, 7): [("K", 2), ("Z", 1)],
    (2, 0): [("M", 2)], (2, 2): [("K", 3), ("Y", 2)], (2, 3): [("Z", 2), ("M", 3)],
    (2, 5): [("Y", 3)], (2, 6): [("Z", 3)],
}
EARLY = [("P", ("xr", 0)), ("P", ("xr", 1)), ("P", ("xr", 2)), ("P", ("xr", 3)), ("C", 0), ("P", ("u", 0)),
         ("G", 0), ("P", ("gr", 0)), ("H", 0), ("P", ("u", 1)), ("P", ("u", 2)),
         ("G", 1), ("P", ("gr", 1)), ("H", 1), ("P", ("u", 3)), ("X", 0), ("P", "k"), ("W", 0), ("U", 0), ("X", 1),
         ("G", 2), ("P", ("gr", 2)), ("U", 1), ("S", 0), ("X", 2), ("H", 2), ("P", "v"), ("W", 1), ("U", 2), ("X", 3),
         ("P", ("gr", 3)), ("U", 3), ("S", 1), ("G", 3), ("P", ("q", 0)), ("V", 0), ("W", 2), ("H", 3),
         ("P", ("q", 1)), ("S", 2), ("P", ("q", 2)), ("W", 3), ("P", ("q", 3)), ("S", 3), ("A", 0),
         ("P", ("g", 1, 0))]


def gates_order():
    order = [arg for step, arg in EARLY if step == "P"]
    order += [("g", 1, d) for d in range(1, KT)]
    return order + [("g", b, d) for b in (0, 2) for d in range(KT)]


def plan():
    big, tp, sc = Ring(4), Ring(2), Ring(2)
    tp.add("prm", "a")
    tp.add("s5p", "v")
    for k in range(KT):
        big.add(("x", k), "v")
    for step, arg in EARLY:
        if step == "P":
            big.add(arg, "a")
        if step == "C":
            for r in range(2):
                tp.add(("c", r), "v")
        if step == "G":
            for w in range(2):
                for d in range(2):
                    big.add(("lru", arg, w, d), "a")
        if step == "X":
            for half in range(2):
                tp.add(("x2", arg, half), "a")
        if step == "U":
            tp.add(("U", arg), "a")
        if step == "W":
            for g4 in range(4):
                tp.add(("w", arg, g4), "a")
        if step == "S":
            for h in range(2):
                sc.add(("st", 2 * arg + h), "v")
        if step == "V":
            tp.add("v", "a")
        if step == "A":
            for i in range(GQ):
                sc.add(("s", 0, i), "v")
    for d in range(KT):
        for i in range(GQ if d + 1 < KT else 0):
            sc.add(("s", d + 1, i), "v")
        for k in range(key_blocks(d // 2)[1]):
            tp.add(("p", d, k), "av"[k % 2])
        big.add(("pv", d), "v")
        if d + 1 < KT:
            big.add(("g", 1, d + 1), "a")
        big.add(("p", 1, d), "v")
    for b in (0, 2):
        for d in range(KT):
            big.add(("g", b, d), "a")
            if b == 0:
                big.add(("p", 0, d), "v")
            for step, ct in SSM_STEPS.get((b, d), []):
                if step == "K":
                    sc.add(("kf", ct), "v")
                    sc.add(("kb", ct), "v")
                if step == "Y":
                    for h in range(2):
                        big.add(("y1", ct, h), "av"[h])
                if step == "Z":
                    tp.add(("y3", ct), "a")
    for n in range(CT):
        big.add(("z1", n), "a")
        big.add(("z0", n), "v")
    for d in range(KT):
        big.add(("p", 2, d), "v")
    for t in range(NT):
        for h in range(2):
            big.add(("wo", t, h), "v")
    for t in range(NT):
        for h in range(2):
            tp.add(("h2", t, h), "av"[h])
    sc.add("logits", "v")
    sc.add("rank", "v")
    return big, tp, sc


def hybrid_block(nc, x, norm1_g, w_in, attn_sink, conv_w, conv_b, w_r, b_r, w_i, b_i, lam,
                 a_re, a_im, log_step, b_re, b_im, c_re, c_im, d_skip, w_glu, b_glu, w_branch,
                 w_out, norm2_g, w_group, b_group, w_expert, b_expert, w1, w3, w2, final_g,
                 consts, token_ids, out):
    f32, i32, f32r = mybir.dt.float32, mybir.dt.int32, mybir.dt.float32r
    ALU, ACT, AX = mybir.AluOpType, mybir.ActivationFunctionType, mybir.AxisListType
    MUL, ADD, SUB, MAX = ALU.mult, ALU.add, ALU.subtract, ALU.max
    BIG, TP, SC = plan()
    ORDER = gates_order()
    POOL_SPLITS = range(2, 8)

    ctx = ExitStack()
    with ctx:
        def sb(name, shape, dt=f32):
            return ctx.enter_context(nc.sbuf_tensor(name, shape, dt))

        def sem(name):
            return ctx.enter_context(nc.semaphore(name))

        def bc(ap, axis, n):
            a = ap.unsqueeze(axis)
            shape = list(a.shape)
            shape[axis] = n
            return a.broadcast_to(shape)

        NSLOT = MAXR * ROUND
        slot_table = nc.dram_tensor("slot_table", [NSLOT + (IW + 2) * P, 2], i32, kind="Internal").ap()
        hn2_rows = nc.dram_tensor("hn2_rows", [T, D], f32, kind="Internal").ap()
        pair_rows = nc.dram_tensor("pair_rows", [2 * T, D], f32, kind="Internal").ap()

        HS = SLAB // 2
        WR, WP, WL = 2, 2, 8
        cst = sb("cst", [P, K_END])
        tok = sb("tok", [P, 2, NT, 2], i32)
        prm = sb("prm", [P, R_END])
        with ExitStack() as early:
            hnh = early.enter_context(nc.sbuf_tensor("hnh", [P, KT, T], f32r))
            hnl = early.enter_context(nc.sbuf_tensor("hnl", [P, KT, T], f32r))
            wplain = early.enter_context(nc.sbuf_tensor("wplain", [P, WP, HS], f32))
            wraw = early.enter_context(nc.sbuf_tensor("wraw", [P, WR, HS], f32))
            wh = early.enter_context(nc.sbuf_tensor("wh", [P, 2, HS], f32r))
            wl = early.enter_context(nc.sbuf_tensor("wl", [P, 2, HS], f32r))
        xres = sb("xres", [P, NT, D])
        h2 = sb("h2", [P, NT, D])
        with ExitStack() as experts:
            w13h = experts.enter_context(nc.sbuf_tensor("w13h", [P, 2, KT, FE], f32r))
            w13l = experts.enter_context(nc.sbuf_tensor("w13l", [P, 2, KT, FE], f32r))
            xgTh = experts.enter_context(nc.sbuf_tensor("xgTh", [P, 2, KT, P], f32r))
            xgTl = experts.enter_context(nc.sbuf_tensor("xgTl", [P, 2, KT, P], f32r))
        wlate = sb("wlate", [P, WL, HS])
        mix = sb("mix", [P, NT * D])
        act = sb("act", [P, 2 * CT * T])
        late = sb("late", [P, 2176])
        xrp = sb("xrp", [P, CT * (T + CONV - 1)])
        xc = sb("xc", [P, CT * T])
        r1 = sb("r1", [P, 6 * SLAB])
        X = sb("X", [P, 4 * GP * (NC + 1)])
        U = sb("U", [P, G * NC])
        bb = sb("bb", [P, 4, GP, C])
        cc = sb("cc", [P, 2, GP, C])
        pw = sb("pw", [P, 2, L + 1, 2 * GP])
        aa = sb("aa", [P, 2, 4, GP])
        sm = sb("sm", [P, 96])
        lt = sb("lt", [P, 4, 8])
        dskip = sb("dskip", [2 * C, GP])
        dd = sb("dd", [2 * C, GP, C])
        slot_i = sb("slot_i", [P, 2, NT], i32)
        idx = sb("idx", [P, IW, 2], i32)
        ntot = sb("ntot", [1, 1], i32)

        xt = r1[:, 0:4096].rearrange("p (t d) -> p t d", t=NT)
        xs = r1[:, 4096:8192].rearrange("p (t d) -> p t d", t=NT)
        mixed = mix[:, :].rearrange("p (k t) -> p k t", k=KT)
        oatt, olru = [act[:, i * 2048:(i + 1) * 2048].rearrange("p (c t) -> p c t", c=CT) for i in range(2)]
        ossm = U[:, :].rearrange("p (c t) -> p c t", c=CT)
        branch_in = (oatt, olru, ossm)
        uT = oatt
        xrv = xrp[:, :].rearrange("p (c t) -> p c t", c=CT)
        xcv = xc[:, :].rearrange("p (c t) -> p c t", c=CT)
        Xv = X[:, :].rearrange("p (d g s) -> p d g s", d=4, g=GP)
        Xd = X[:, :].rearrange("p (d r g s) -> p d r g s", d=2, r=2, g=GP)
        Uv = U[:, :].rearrange("p (g k) -> p g k", g=G)
        wri = mix[:, 0:1024].rearrange("p (w d c j) -> p w d c j", w=2, d=2, c=CT)
        btmp = mix[:, 1024:2048].rearrange("p (a g c) -> p a g c", a=2, g=2 * GP)
        bin_ = mix[:, 2048:3072].rearrange("p (r g c) -> p r g c", r=2, g=2 * GP)
        crow = mix[:, 3072:4096].rearrange("p (r t h n) -> p r t h n", r=2, t=CT, h=2)
        l_r, l_i, l_v, l_a, l_q = [r1[:, 6144 + i * 1024:7168 + i * 1024].rearrange("p (d t) -> p d t", d=2)
                                   for i in range(5)]
        wn = mix[:, 1024:3072].rearrange("p (d g m) -> p d g m", d=4, g=4)
        tmpA, tmpB = mix[:, 3072:3584], mix[:, 3584:4096]
        wt = late[:, 0:2048].rearrange("p (b d n) -> p b d n", b=4, d=4)
        sgate = act[:, :].rearrange("p (k t) -> p k t", k=KT)
        qT = r1[:, 0:2048].rearrange("p (a t) -> p a t", a=GQ)
        kT = r1[:, 2048:2560]
        vT = xrp[:, 1024:1536]
        vS = r1[:, 2560:3072].rearrange("p (a t) -> p a t", a=NT)
        btab = r1[:, 3072:6144].rearrange("p (h k) -> p h k", h=NQ)
        prs = [r1[:, 6144 + i * 1536:7680 + i * 1536].rearrange("p (h k) -> p h k", h=GQ) for i in range(2)]
        pT = r1[:, 9216:10752].rearrange("p (k q) -> p k q", k=3)
        prows = r1[0:R_END, 11264:11264 + P]
        srows = r1[0:96, 11392:11392 + P]
        lstep = r1[0:96, 11520:11522]
        s5p = r1[:, 11522:11618]
        cs = r1[:, 11618:11682].rearrange("p (i g) -> p i g", i=2)
        s5t = r1[:, 11776:12288].rearrange("p (i g) -> p i g", i=16)
        cp = r1[:, 0:4608].rearrange("p (b d g m) -> p b d g m", b=2, d=4, g=4)
        tmpC, tmpD = r1[:, 4608:5184], r1[:, 5184:5760]
        kx = r1[0:2 * C, 5760:6720].rearrange("p (g m) -> p g m", g=4)
        y2 = r1[0:NC, 6720:7744].rearrange("p (j g c) -> p j g c", j=L, g=8)
        mms = [(late[:, 0:1024], late[:, 1024:2048], r1[:, 7744:8768], r1[:, 8768:9792])[i]
               .rearrange("p (g m) -> p g m", g=8) for i in range(CT)]
        Xb = r1[:, 9792:11840].rearrange("p (d g s) -> p d g s", d=2, g=GP)
        sct = late[:, 2048:2176].rearrange("p (i d g) -> p i d g", i=2, d=4)
        x2 = xrp[0:NC, 0:1024].rearrange("p (g j c) -> p g j c", g=8, j=L)
        gbuf = xrp[:, 0:1024].rearrange("p (b t) -> p b t", b=2)
        bbd = xrp[:, 1024:1536].rearrange("p (d g h c) -> p d g h c", d=4, g=4, h=2)
        g2b, fgb = X[:, 0:1024], X[:, 1024:2048]
        wge = X[:, 2048:2208].rearrange("p (k c) -> p k c", k=KT)
        bge = X[:, 2208:2228]
        blank = X[:, 2240:2240 + 2 * (NSLOT // P + 2)].bitcast(i32).rearrange("p (n c) -> p n c", c=2)
        h2T = late[:, 0:2048].rearrange("p (b k s) -> p b k s", b=2, k=KT)
        pair = (h2, mix[:, :].rearrange("p (t d) -> p t d", t=NT))
        xg = xrp[:, 0:2048].rearrange("p (b d) -> p b d", b=2)
        w13 = [a.rearrange("p (w k f) -> p w k f", w=2, k=KT)
               for a in (r1[:, 0:2 * SLAB], r1[:, 2 * SLAB:4 * SLAB],
                         h2[:, :, :].rearrange("p t d -> p (t d)"), act[:, :])]
        w2s = [r1[:, (4 + i) * SLAB:(5 + i) * SLAB].rearrange("p (k f) -> p k f", k=2) for i in range(2)]
        sg = late[:, 0:512].rearrange("p (b f) -> p b f", b=2)
        hh = late[:, 512:1024].rearrange("p (b f) -> p b f", b=2)
        hT = late[:, 1024:1536].rearrange("p (b k s) -> p b k s", b=2, k=2)
        yb = U[:, :].rearrange("p (b d) -> p b d", b=2)
        ssq, rstd = sm[:, 0:4], sm[:, 4:8]
        sink = sm[:, 8:16]
        cl = sm[:, 16:24]
        am, anm, aes, asum, ard = [sm[:, 24 + 8 * i:32 + 8 * i].rearrange("p (b h) -> p b h", b=2)
                                   for i in range(5)]
        ssq2, rstd2, ssq3, rstd3 = [sm[:, 64 + 4 * i:68 + 4 * i] for i in range(4)]
        epsb = sm[:, 80:81]
        rt = [xc[:, 64 * i:64 * i + 64].rearrange("p (t e) -> p t e", t=NT) for i in range(12)]
        rs = [xc[:, 768 + 4 * i:772 + 4 * i] for i in range(16)]
        rg = [xc[:, 832 + 16 * i:848 + 16 * i].rearrange("p (t e) -> p t e", t=NT) for i in range(8)]

        banks = {"big": [ctx.enter_context(nc.psum_tensor(f"big{i}", [P, 512], f32)) for i in range(4)],
                 "tp": [ctx.enter_context(nc.psum_tensor(f"tp{i}", [P, 512], f32)) for i in range(2)],
                 "sc": [ctx.enter_context(nc.psum_tensor(f"sc{i}", [P, 512], f32)) for i in range(2)]}
        rings = {"big": BIG, "tp": TP, "sc": SC}
        full = {r: sem(f"{r}_full") for r in rings}
        free = {(r, by): sem(f"{r}_emptied_{by}") for r in rings for by in "av"}

        cst_in, prow_in, srow_in = sem("cst_in"), sem("prow_in"), sem("srow_in")
        x_in = [sem(f"x_in{t}") for t in range(NT)]
        early_in, lru_w_in, late_in = sem("early_in"), sem("lru_w_in"), sem("late_in")
        raw_in, plain_in, last_in = ([sem(f"{name}_in{i}") for i in range(n)]
                                     for name, n in (("raw", WR), ("plain", WP), ("last", WL)))
        x_hi = sem("x_hi")
        hi_ready, lo_pool, lo_dve = sem("hi_ready"), sem("lo_pool"), sem("lo_dve")
        dve_step, act_step, pool_step = sem("dve_step"), sem("act_step"), sem("pool_step")
        squares, root_ready, xs_ready = sem("squares"), sem("root_ready"), sem("xs_ready")
        step_exp, srows_ready, s5_arg, s5_act, s5_tab = sem("step_exp"), sem("srows_ready"), sem("s5_arg"), sem("s5_act"), sem("s5_tab")
        cl_arg, cl_exp, cl_ready = sem("cl_arg"), sem("cl_exp"), sem("cl_ready")
        pad_zero, x_zero, dskip_in, sink_in = sem("pad_zero"), sem("x_zero"), sem("dskip_in"), sem("sink_in")
        conv_done, btab_ready = sem("conv_done"), sem("btab_ready")
        lru_ta, lru_q, lru_s, lru_out = sem("lru_ta"), sem("lru_q"), sem("lru_s"), sem("lru_out")
        s_max, s_exp, s_prob, pv_done = sem("s_max"), sem("s_exp"), sem("s_prob"), sem("pv_done")
        gate_used = sem("gate_used")
        yg_in = [sem(f"yg_in{t}") for t in range(NT)]
        wn_ready, scan_mul, scan_add = sem("wn_ready"), sem("scan_mul"), sem("scan_add")
        bbd_zero, bbd_ready, cp_ready, kx_ready, mm_in = sem("bbd_zero"), sem("bbd_ready"), sem("cp_ready"), sem("kx_ready"), [sem("mm_in0"), sem("mm_in1")]
        glu_ready, x_again, x1_sq, x1_root, h2_ready, h2_out = sem("glu_ready"), sem("x_again"), sem("x1_sq"), sem("x1_root"), sem("h2_ready"), sem("h2_out")
        pool_pass, logits_done, eps_ready, x_turned = sem("pool_pass"), sem("logits_done"), sem("eps_ready"), sem("x_turned")
        zero_ready, slot_zero, w_arg, w_exp = sem("zero_ready"), sem("slot_zero"), sem("w_arg"), sem("w_exp")
        mask_ready, n_ready, slots_ready, slot_out = sem("mask_ready"), sem("n_ready"), sem("slots_ready"), sem("slot_out")
        w13_in, w2_in = [sem(f"w13_in{i}") for i in range(4)], [sem(f"w2_in{i}") for i in range(2)]
        w13_hi, w13_lo, w13_used, idx_in, xg_in = sem("w13_hi"), sem("w13_lo"), sem("w13_used"), [sem("idx_in0"), sem("idx_in1")], [sem("xg_in0"), sem("xg_in1")]
        xg_turned, rows_hi, rows_lo, hid_full, silu_done, hh_ready = sem("xg_turned"), sem("rows_hi"), sem("rows_lo"), sem("hid_full"), sem("silu_done"), sem("hh_ready")
        hT_full, hT_ready, y_full, yb_a, yb_v = sem("hT_full"), sem("hT_ready"), sem("y_full"), sem("yb_a"), sem("yb_v")
        rows_out = [sem("rows_out0"), sem("rows_out1")]
        acc_ready, out_sq, out_root, out_ready, out_in = sem("acc_ready"), sem("out_sq"), sem("out_root"), sem("out_ready"), sem("out_in")

        w_in_v = w_in.rearrange("(k p) c -> p k c", p=P)
        w_glu_v = w_glu.rearrange("(k p) c -> p k c", p=P)
        w_out_v = w_out.rearrange("(k p) c -> p k c", p=P)
        raw_slabs, plain_slabs, last_slabs = [], [], []

        def in_slab(key, col):
            raw_slabs.append((key, [(lambda w: w.rearrange("p (k c) -> p k c", k=KT), w_in_v[:, :, col:col + P])]))

        def q_slab(i):
            raw_slabs.append((("q", i), [
                (lambda w, h=h: w.rearrange("p (k h c) -> p k h c", k=KT, h=2)[:, :, h, :],
                 w_in_v[:, :, (h * GQ + i) * HD:(h * GQ + i + 1) * HD]) for h in range(2)]))

        def branch_slab(slabs, b, n):
            cols = slice(n * 256, n * 256 + 256)
            if b:
                parts = [(lambda w: w.rearrange("p (k c) -> p k c", k=CT),
                          w_branch[b].rearrange("(k p) c -> p k c", p=P)[:, :, cols])]
            else:
                parts = [(lambda w, h=h: w[h * HD:(h + 1) * HD].rearrange("p (k c) -> p k c", k=CT),
                          w_branch[0, h * GQ * HD:(h + 1) * GQ * HD].rearrange("(k p) c -> p k c", p=HD)[:, :, cols])
                         for h in range(2)]
            slabs.append((("p", b, n), parts))

        column = {"u": COL_U, "xr": COL_XR, "gr": COL_GR, "k": COL_K, "v": COL_V}
        for key in ORDER:
            if key[0] == "q":
                q_slab(key[1])
            elif key[0] == "g":
                in_slab(key, COL_GATE + key[1] * D + P * key[2])
            else:
                in_slab(key, column[key] if key in column else column[key[0]] + P * key[1])
        for b in (1, 0):
            for n in range(4):
                branch_slab(plain_slabs, b, n)
        for n in range(CT):
            last_slabs.append((("z", n), [(lambda w, h=h: w.rearrange("p (k h c) -> p k h c", k=CT, h=2)[:, :, h, :],
                                           w_glu_v[:, :, h * BW + P * n:h * BW + P * n + P]) for h in range(2)]))
        for n in range(4):
            branch_slab(last_slabs, 2, n)
        for h in range(2):
            for n in range(4):
                last_slabs.append((("wo", h, n), [(lambda w: w.rearrange("p (k c) -> p k c", k=2),
                                                   w_out_v[:, 2 * n:2 * n + 2, h * 512:h * 512 + 512])]))

        def slab_count(slabs, n, slots):
            return 16 * sum(len(slabs[m][1]) for m in range(n % slots, n + 1, slots))

        def index_of(slabs, key):
            return next(n for n, (k, _) in enumerate(slabs) if k == key)

        def lo_done(m):
            if m in POOL_SPLITS:
                return lo_pool, m - POOL_SPLITS.start + 1
            return lo_dve, m + 1 - (len(POOL_SPLITS) if m >= POOL_SPLITS.stop else 0)

        def split_lo(eng, tensor_tensor, m):
            eng.wait_ge(hi_ready, m + 1)
            tensor_tensor(wl[:, m % 2, :], wraw[:, m % WR, :], wh[:, m % 2, :].bitcast(f32), SUB).then_inc(lo_done(m)[0], 1)

        def pe_bank(eng, ring, key):
            r = rings[ring]
            n = r.index(key)
            if n >= r.size:
                by, count = r.emptied(n - r.size)
                eng.wait_ge(free[ring, by], count)
            return banks[ring][n % r.size]

        def full_bank(eng, ring, key):
            r = rings[ring]
            n = r.index(key)
            eng.wait_ge(full[ring], n + 1)
            return banks[ring][n % r.size]

        def emptied(ring, key):
            by, count = rings[ring].emptied(rings[ring].index(key))
            return free[ring, by], count

        def slab_last_job(key):
            if key[0] == "p":
                return BIG.index(("p", key[1], 2 * key[2] + 1))
            if key[0] == "wo":
                return BIG.index(("wo", NT - 1, key[1]))
            if key[0] == "z":
                return BIG.index(("z0", key[1]))
            return BIG.index(key)

        block = ctx.enter_context(nc.Block())

        @block.sync
        def _(sp):
            for t in range(NT):
                sp.dma_start(xt[:, t, :], x[t * P:(t + 1) * P, :]).then_inc(x_in[t], 16)
            load = sp.dma_start
            load(lstep[64:96, :], log_step.rearrange("d (g h) -> (d g) h", h=2)).then_inc(srow_in, 16)
            load(srows[0:32, :], a_re.rearrange("d (g h) n -> (d g) (h n)", h=2)).then_inc(srow_in, 16)
            load(srows[32:64, :], a_im.rearrange("d (g h) n -> (d g) (h n)", h=2)).then_inc(srow_in, 16)
            for row, rows, src in ((R_G1, KT, norm1_g.rearrange("(r p) -> r p", p=P)),
                                   (R_CW, CONV * CT, conv_w.rearrange("w (r p) -> (w r) p", p=P)),
                                   (R_CB, CT, conv_b.rearrange("(r p) -> r p", p=P)),
                                   (R_BR, 2 * CT, b_r.rearrange("d (r p) -> (d r) p", p=P)),
                                   (R_BI, 2 * CT, b_i.rearrange("d (r p) -> (d r) p", p=P)),
                                   (R_LAM, 2 * CT, lam.rearrange("d (r p) -> (d r) p", p=P)),
                                   (R_BG, 2 * CT, b_glu.rearrange("(r p) -> r p", p=P))):
                load(prows[row:row + rows, :], src).then_inc(prow_in, 16)

            def load_slab(slabs, n, slots, ring, done):
                for shape, src in slabs[n][1]:
                    sp.dma_start(shape(ring[:, n % slots, :]), src).then_inc(done[n % slots], 16)

            def load_plain(n):
                if n >= WP:
                    sp.wait_ge(full["big"], slab_last_job(plain_slabs[n - WP][0]) + 1)
                load_slab(plain_slabs, n, WP, wplain, plain_in)

            def ssm_matrices(ct):
                sp.wait_ge(kx_ready, ct + 1)
                for j in range(L):
                    sp.dma_start(mms[ct][j * C:(j + 1) * C].rearrange("p (g h) m -> p g h m", h=2)[:, :, 0, :],
                                 kx[0:C, :, (L - 1 - j) * C:(L - 1 - j) * C + P]).then_inc(mm_in[0], 16)

            for m, key in enumerate(ORDER):
                if m >= WR:
                    sp.wait_ge(*lo_done(m - WR))
                load_slab(raw_slabs, m, WR, wraw, raw_in)
                for step, ct in SSM_STEPS.get(ORDER[m - 2][1:], []) if ORDER[m - 2][0] == "g" else ():
                    if step == "M":
                        ssm_matrices(ct)
                if key[0] == "g" and key[1] != 2 and key[2] % 2 == 0:
                    load_plain((4 if key[1] == 0 else 0) + key[2] // 2)
            for n in range(len(last_slabs)):
                if n < WL:
                    if n == 0:
                        sp.wait_ge(full["big"], BIG.index(("p", 0, KT - 1)) + 1)
                    if n == WP:
                        sp.wait_ge(full["big"], BIG.index(("g", 2, KT - 1)) + 1)
                else:
                    sp.wait_ge(full["big"], slab_last_job(last_slabs[n - WL][0]) + 1)
                load_slab(last_slabs, n, WL, wlate, last_in)
                if n == WL - 1:
                    for t in range(NT):
                        sp.dma_start(xres[:, t, :], x[t * P:(t + 1) * P, :]).then_inc(x_again, 16)

            def expert_w13(e, slot):
                for j, w in enumerate((w1, w3)):
                    src = w[bass.ds(e, 1)].rearrange("o (k p) f -> p (o k) f", p=P)
                    sp.dma_start(w13[slot][:, j], src).then_inc(w13_in[slot], 16)

            def expert_w2(e, h):
                src = w2[bass.ds(e, 1)].rearrange("o (k p) f -> p (o k) f", p=P)
                sp.dma_start(w2s[h], src).then_inc(w2_in[h], 16)

            sp.wait_ge(full["tp"], TP.index(("y3", CT - 1)) + 1)
            for h in range(2):
                expert_w13(h, h)
                expert_w2(h, h)
            for t in range(NT):
                sp.wait_ge(h2_ready, t + 1)
                sp.dma_start(hn2_rows[t * P:(t + 1) * P, :], h2[:, t, :]).then_inc(h2_out, 16)
            sp.wait_ge(h2_out, 16 * NT)
            sp.wait_ge(full["tp"], TP.index(("h2", NT - 1, 1)) + 1)
            expert_w13(2, 2)
            sp.wait_ge(x1_sq, NT)
            expert_w13(3, 3)
            sp.wait_ge(w13_lo, KC)
            expert_w13(4, 0)

            def next_weights(e, w13_expert, slot, w2_expert, h):
                sp.wait_ge(w13_lo, e * KC)
                expert_w13(w13_expert, slot)
                sp.wait_ge(y_full, e - 1)
                expert_w2(w2_expert, h)

            for e in range(2, 5):
                next_weights(e, e + 3, (e + 3) % 4, e, e % 2)
            sp.wait_ge(n_ready, 1)
            rest = sp.value_load(ntot[0:1, 0:1], min_val=E - 4, max_val=MAXR * E - 4)
            with sp.Fori(5, rest + 1, 4) as g:
                for j in range(4):
                    next_weights(g + j, (g + (j + 3)) % E, j, (g + j) % E, (j + 1) % 2)
            for j in range(1, 4):
                sp.wait_ge(y_full, rest + (j - 1))
                expert_w2(E - 4 + j, j % 2)
            sp.wait_ge(rows_out[0], rest * 8 + 32)
            sp.wait_ge(rows_out[1], rest * 8 + 32)
            sp.wait_ge(n_ready, 1)
            pairs = pair_rows.rearrange("(t p c) d -> t p c d", p=P, c=2)
            for t in range(NT):
                for c in range(2):
                    sp.dma_start(pair[c][:, t, :], pairs[t, :, c, :]).then_inc(yg_in[t], 16)
            for t in range(NT):
                sp.wait_ge(out_ready, t + 1)
                sp.dma_start(out[t * P:(t + 1) * P, :], xres[:, t, :]).then_inc(out_in, 16)
            sp.wait_ge(out_in, 16 * NT)

        @block.gpsimd
        def _(pool):
            steps = [0]

            def link(ins):
                steps[0] += 1
                ins.then_inc(pool_step, 1)
                pool.wait_ge(pool_step, steps[0])

            nc.gpsimd.memset(xrv[:, :, 0:2], 0.0).then_inc(pad_zero, 1)
            nc.gpsimd.memset(xrv[:, :, T + 2:T + 3], 0.0).then_inc(pad_zero, 1)
            nc.gpsimd.memset(Xv[:, :, :, 0:1], 0.0).then_inc(x_zero, 1)
            load = pool.dma_start
            for w, src in enumerate((w_r, w_i)):
                for h in range(2):
                    for d in range(2):
                        load(wri[h * LB:(h + 1) * LB, w, d],
                             src[d].rearrange("(c h) i j -> h i c j", h=2)[h]).then_inc(lru_w_in, 16)
            for r, src in enumerate((b_re, b_im)):
                for d in range(2):
                    load(bin_[:, r, d * GP:(d + 1) * GP, :],
                         src[d].rearrange("(g h) n c -> (h n) g c", h=2)).then_inc(early_in, 16)
            for r, src in enumerate((c_re, c_im)):
                for h in range(2):
                    load(crow[:, r, :, h, :], src.rearrange("(t g) c n -> (g c) t n", t=CT)).then_inc(early_in, 16)
            load(sink, attn_sink.partition_broadcast(P)).then_inc(sink_in, 16)
            load(dskip[:, :], d_skip.rearrange("(g q) -> q g", q=2 * C), allow_slow_non_contiguous=True).then_inc(dskip_in, 16)
            for n, m in enumerate(POOL_SPLITS):
                split_lo(pool, nc.gpsimd.tensor_tensor, m)
                if n == 0:
                    pool.wait_ge(full["big"], BIG.index(("x", KT - 1)) + 1)
                for h in range(2 * n, min(2 * n + 2, NQ)):
                    nc.gpsimd.tensor_scalar(btab[:, h, :], cst[:, K_DIST:K_DIST + 3 * P],
                                            float(2.0 ** (-8.0 * (h + 1) / NQ)), None, MUL).then_inc(btab_ready, 1)
            pool.wait_ge(s5_tab, 1)
            pool.wait_ge(full["tp"], TP.index(("c", 1)) + 1)
            for ct in range(CT):
                if ct:
                    pool.wait_ge(full["tp"], TP.index(("w", ct - 1, 3)) + 1)
                tv = [t.rearrange("p (g j c) -> p g j c", g=4, j=L) for t in (tmpA, tmpB)]
                for d in range(2):
                    cols = slice(d * GP + 4 * ct, d * GP + 4 * ct + 4)

                    def power(r):
                        rows = pw[:, r, L - 1::-1, cols] if d == 0 else pw[:, r, 0:L, cols]
                        return bc(rows.rearrange("p j g -> p g j"), 3, C)

                    def b_of(r):
                        return bc(bb[:, 2 * d + r, 4 * ct:4 * ct + 4, :], 2, L)

                    dst = [wn[:, 2 * d + r].rearrange("p g (j c) -> p g j c", j=L) for r in range(2)]
                    link(nc.gpsimd.tensor_tensor(tv[0], power(0), b_of(0), MUL))
                    link(nc.gpsimd.tensor_tensor(tv[1], power(1), b_of(1), MUL))
                    link(nc.gpsimd.tensor_tensor(dst[0], tv[0], tv[1], SUB))
                    link(nc.gpsimd.tensor_tensor(tv[0], power(0), b_of(1), MUL))
                    link(nc.gpsimd.tensor_tensor(tv[1], power(1), b_of(0), MUL))
                    nc.gpsimd.tensor_tensor(dst[1], tv[0], tv[1], ADD).then_inc(wn_ready, 1)
                    pool.wait_ge(wn_ready, 2 * ct + d + 1)
            pool.wait_ge(*emptied("sc", ("st", KT - 1)))
            with pool.Fori(1, NC - 1, 2) as s0:
                for h in range(2):
                    s = s0 + h
                    now = Xv[:, :, :, bass.ds(s, 1)].rearrange("p d g s -> p d (g s)")
                    nxt = Xv[:, :, :, bass.ds(s + 1, 1)].rearrange("p d g s -> p d (g s)")
                    nxtd = Xd[:, :, :, :, bass.ds(s + 1, 1)].rearrange("p d r g s -> p d r (g s)")
                    swapped = sct[:, 1].rearrange("p (d r) g -> p d r g", d=2)[:, :, ::-1, :]
                    nc.gpsimd.tensor_tensor(sct[:, 0], aa[:, 0], now, MUL).then_inc(scan_mul, 1)
                    nc.gpsimd.tensor_tensor(sct[:, 1], aa[:, 1], now, MUL).then_inc(scan_mul, 1)
                    pool.wait_ge(scan_mul, s * 2 - 1)
                    pool.sem_inc(pool_pass, 1)
                    nc.gpsimd.tensor_tensor(nxt, nxt, sct[:, 0], ADD).then_inc(scan_add, 1)
                    pool.wait_ge(scan_mul, s * 2)
                    pool.wait_ge(scan_add, s * 2 - 1)
                    pool.sem_inc(pool_pass, 1)
                    nc.gpsimd.tensor_tensor(nxtd, nxtd, swapped, ADD).then_inc(scan_add, 1)
                    pool.wait_ge(scan_add, s * 2)
                    pool.sem_inc(pool_pass, 1)
            pool.wait_ge(full["big"], BIG.index(("pv", KT - 1)) + 1)
            for ct in range(CT):
                b = ct % 2
                if ct >= 2:
                    pool.wait_ge(full["big"], BIG.index(("y1", ct - 2, 1)) + 1)
                tv = [t.rearrange("p (g j c) -> p g j c", g=4, j=L + 1) for t in (tmpC, tmpD)]
                for d in range(2):
                    cols = slice(d * GP + 4 * ct, d * GP + 4 * ct + 4)

                    def power_up(r):
                        rows = pw[:, r, 0:L + 1, cols] if d == 0 else pw[:, r, L::-1, cols]
                        return bc(rows.rearrange("p j g -> p g j"), 3, C)

                    def c_of(r):
                        return bc(cc[:, r, 4 * ct:4 * ct + 4, :], 2, L + 1)

                    link(nc.gpsimd.tensor_tensor(tv[0], power_up(0), c_of(0), MUL))
                    link(nc.gpsimd.tensor_tensor(tv[1], power_up(1), c_of(1), MUL))
                    link(nc.gpsimd.tensor_tensor(cp[:, b, 2 * d].rearrange("p g m -> p (g m)"), tmpC, tmpD, SUB))
                    link(nc.gpsimd.tensor_tensor(tv[0], power_up(0), c_of(1), MUL))
                    link(nc.gpsimd.tensor_tensor(tv[1], power_up(1), c_of(0), MUL))
                    link(nc.gpsimd.tensor_tensor(tmpC, tmpC, tmpD, ADD))
                    nc.gpsimd.tensor_scalar(cp[:, b, 2 * d + 1].rearrange("p g m -> p (g m)"), tmpC, -1.0, None,
                                            MUL).then_inc(cp_ready, 1)
                    pool.wait_ge(cp_ready, 2 * ct + d + 1)
            pool.wait_ge(full["tp"], TP.index(("y3", CT - 1)) + 1)
            pool.dma_start(g2b, norm2_g.partition_broadcast(P)).then_inc(late_in, 16)
            pool.dma_start(fgb, final_g.partition_broadcast(P)).then_inc(late_in, 16)
            pool.dma_start(wge[:, :, 0:NGRP], w_group.rearrange("(k p) c -> p k c", p=P)).then_inc(late_in, 16)
            pool.dma_start(wge[:, :, NGRP:NGRP + E], w_expert.rearrange("(k p) c -> p k c", p=P)).then_inc(late_in, 16)
            pool.dma_start(bge[:, 0:NGRP], b_group.partition_broadcast(P)).then_inc(late_in, 16)
            pool.dma_start(bge[:, NGRP:NGRP + E], b_expert.partition_broadcast(P)).then_inc(late_in, 16)
            nc.gpsimd.memset(blank[:, :, 0:1], 0).then_inc(zero_ready, 1)
            nc.gpsimd.memset(blank[:, :, 1:2], 2 * T).then_inc(zero_ready, 1)
            pool.wait_ge(zero_ready, 2)
            pool.dma_start(slot_table[0:NSLOT + 2 * P].rearrange("(p n) c -> p n c", p=P), blank).then_inc(slot_zero, 16)
            pool.wait_ge(slot_zero, 16)
            pool.wait_ge(full["big"], BIG.index(("wo", NT - 1, 1)) + 1)
            for c in range(KC):
                pool.wait_ge(w13_hi, c + 1)
                nc.gpsimd.tensor_tensor(w13l[:, :, KC_K * c:KC_K * (c + 1)], w13[0][:, :, KC_K * c:KC_K * (c + 1)],
                                        w13h[:, :, KC_K * c:KC_K * (c + 1)].bitcast(f32), SUB).then_inc(w13_lo, 1)
            pool.wait_ge(slots_ready, 1)
            for c in range(2):
                for t in range(NT):
                    pool.indirect_dma_start(slot_table, bass.IndirectOffsetOnAxis(ap=slot_i[:, c, t:t + 1], axis=0),
                                            tok[:, c, t, :], None).then_inc(slot_out, 16)
            pool.wait_ge(slot_out, 16 * 2 * NT)
            pool.wait_ge(h2_out, 16 * NT)
            pool.wait_ge(n_ready, 1)
            rest = pool.value_load(ntot[0:1, 0:1], min_val=E - 4, max_val=MAXR * E - 4)

            def indices(i, h, b):
                pool.dma_start(idx[:, b, :], slot_table[bass.ds(i * P, P), :]).then_inc(idx_in[h], 16)

            def gather(i, h, b):
                pool.wait_ge(idx_in[h], (i + (2 - h)) * 8)
                pool.sem_inc(pool_pass, 1)
                pool.indirect_dma_start(xg[:, h, :], None, hn2_rows,
                                        bass.IndirectOffsetOnAxis(ap=idx[:, b, 0:1], axis=0)).then_inc(xg_in[h], 16)

            def scatter(i, h, b):
                pool.wait_ge(yb_a, i + 1)
                pool.wait_ge(yb_v, i + 1)
                pool.sem_inc(pool_pass, 1)
                pool.indirect_dma_start(pair_rows, bass.IndirectOffsetOnAxis(ap=idx[:, b, 1:2], axis=0), yb[:, h, :], None,
                                        bounds_check=2 * T - 1, oob_is_err=False).then_inc(rows_out[h], 16)

            for i in range(2):
                indices(i, i, i)
            for i in range(2):
                gather(i, i, i)
            for i in range(2):
                indices(i + 2, i, i + 2)
            for i in range(IW - 2):
                pool.wait_ge(xg_turned, i + 1)
                gather(i + 2, i % 2, i + 2)
                if i >= 2:
                    scatter(i - 2, i % 2, i - 2)
                if i >= 4:
                    pool.wait_ge(rows_out[i % 2], (i - i % 2 - 2) * 8)
                indices(i + 4, i % 2, (i + 4) % IW)
            with pool.Fori(IW - 2, rest + 2, IW) as g:
                for j in range(IW):
                    pool.wait_ge(xg_turned, g + (j + 1))
                    gather(g + (j + 2), j % 2, j)
                    scatter(g + (j - 2), j % 2, (j + IW - 4) % IW)
                    pool.wait_ge(rows_out[j % 2], (g + (j - j % 2 - 2)) * 8)
                    indices(g + (j + 4), j % 2, (j + 2) % IW)
            for j in range(4):
                scatter(rest + j, j % 2, (j + IW - 4) % IW)

        @block.tensor
        def _(pe):
            mmul = nc.tensor.matmul

            def turn(dst, src, n=P):
                return nc.tensor.transpose(dst, src, cst[0:n, K_ID:K_ID + n])

            def plain_weights(key):
                slabs, slots, ring, done = ((last_slabs, WL, wlate, last_in) if key[0] != "p" or key[1] == 2 else
                                            (plain_slabs, WP, wplain, plain_in))
                n = index_of(slabs, key)
                pe.wait_ge(done[n % slots], slab_count(slabs, n, slots))
                return ring[:, n % slots, :]

            def split_weights(key):
                m = ORDER.index(key)
                pe.wait_ge(*lo_done(m))
                return [w[:, m % 2, :].rearrange("p (k c) -> p k c", k=KT) for w in (wh, wl)]

            def channels(key, w, rhs, ks):
                bank = pe_bank(pe, "big", key)
                for k in range(ks):
                    ins = mmul(bank[:, :], w[:, k, :], rhs[:, k, :], start=(k == 0), stop=(k == ks - 1))
                ins.then_inc(full["big"], 1)

            def project(key):
                w = split_weights(key)
                bank = pe_bank(pe, "big", key)
                for k in range(KT):
                    if key == ORDER[0]:
                        pe.wait_ge(*emptied("big", ("x", k)))
                    mmul(bank[:, :], w[0][:, k, :], hnh[:, k, :], start=(k == 0), stop=False)
                    mmul(bank[:, :], w[0][:, k, :], hnl[:, k, :], start=False, stop=False)
                    ins = mmul(bank[:, :], w[1][:, k, :], hnh[:, k, :], start=False, stop=(k == KT - 1))
                ins.then_inc(full["big"], 1)

            def branch(b, d):
                w = plain_weights(("p", b, d // 2)).rearrange("p (k c) -> p k c", k=CT)
                channels(("p", b, d), w[:, :, (d % 2) * P:(d % 2 + 1) * P], branch_in[b], CT)

            pe.wait_ge(cst_in, 32)
            pe.wait_ge(prow_in, 16 * 7)
            turn(pe_bank(pe, "tp", "prm")[:, 0:R_END], prows[:, :], R_END).then_inc(full["tp"], 1)
            pe.wait_ge(srow_in, 16 * 3)
            pe.wait_ge(srows_ready, 1)
            turn(pe_bank(pe, "tp", "s5p")[:, 0:96], srows[:, :], 96).then_inc(full["tp"], 1)
            pe.wait_ge(xs_ready, NT)
            for k in range(KT):
                bank = pe_bank(pe, "big", ("x", k))
                for t in range(NT):
                    ins = turn(bank[:, t * P:(t + 1) * P], xs[:, t, k * P:(k + 1) * P])
                ins.then_inc(full["big"], 1)
            def turn_values(_):
                pe.wait_ge(*emptied("big", "v"))
                bank = pe_bank(pe, "tp", "v")
                for t in range(NT):
                    ins = turn(bank[:, t * P:(t + 1) * P], vT[:, t * P:(t + 1) * P])
                ins.then_inc(full["tp"], 1)

            def turn_c(_):
                pe.wait_ge(early_in, 16 * 8)
                for r in range(2):
                    bank = pe_bank(pe, "tp", ("c", r))
                    for q in range(CT):
                        ins = turn(bank[:, q * P:(q + 1) * P], crow[:, r, q].rearrange("p h n -> p (h n)"))
                    ins.then_inc(full["tp"], 1)

            def lru_gates(ct):
                if ct == 0:
                    pe.wait_ge(lru_w_in, 16 * 8)
                pe.wait_ge(conv_done, ct + 1)
                for w in range(2):
                    for d in range(2):
                        bank = pe_bank(pe, "big", ("lru", ct, w, d))
                        for h in range(2):
                            rows = slice(h * LB, (h + 1) * LB)
                            ins = mmul(bank[rows, :], wri[rows, w, d, ct, :], xcv[rows, ct, :], start=True, stop=True)
                        ins.then_inc(full["big"], 1)

            def turn_to_chunks(ct):
                pe.wait_ge(*emptied("big", ("u", ct)))
                for half in range(2):
                    bank = pe_bank(pe, "tp", ("x2", ct, half))
                    for j in range(4):
                        ins = turn(bank[0:NC, j * P:(j + 1) * P], uT[:, ct, half * 4 + j::L])
                    ins.then_inc(full["tp"], 1)

            def turn_to_tokens(ct):
                for half in range(2):
                    pe.wait_ge(*emptied("tp", ("x2", ct, half)))
                bank = pe_bank(pe, "tp", ("U", ct))
                for g in range(8):
                    ins = turn(bank[:, g * NC:(g + 1) * NC], x2[:, g].rearrange("p j c -> p (j c)"), NC)
                ins.then_inc(full["tp"], 1)

            def turn_input_matrices(ct):
                pe.wait_ge(wn_ready, 2 * ct + 2)
                for g4 in range(4):
                    bank = pe_bank(pe, "tp", ("w", ct, g4))
                    for q in range(4):
                        ins = turn(bank[:, q * P:(q + 1) * P], wn[:, q, g4, :])
                    ins.then_inc(full["tp"], 1)

            def chunk_inputs(ct):
                pe.wait_ge(*emptied("tp", ("U", ct)))
                for d in (2 * ct, 2 * ct + 1):
                    bank = pe_bank(pe, "sc", ("st", d))
                    for h in range(2):
                        g4 = 2 * (d % 2) + h
                        pe.wait_ge(*emptied("tp", ("w", ct, g4)))
                        for q in range(4):
                            for g2 in range(2):
                                g = 4 * d + 2 * h + g2
                                rhs = Uv[:, g, :] if q < 2 else Uv[:, g, ::-1]
                                ins = mmul(bank[g2 * N:(g2 + 1) * N, (q * 2 + h) * NC:(q * 2 + h + 1) * NC],
                                           wt[:, g4, q, g2 * N:(g2 + 1) * N], rhs, start=True, stop=True)
                    ins.then_inc(full["sc"], 1)

            def scores(u, heads=range(GQ)):
                if u == 0:
                    pe.wait_ge(*emptied("big", ("q", CT - 1)))
                nb, h = u // 2, u % 2
                lo, n = key_blocks(nb)
                rows = slice(h * HD, (h + 1) * HD)
                for i in heads:
                    bank = pe_bank(pe, "sc", ("s", u, i))
                    mmul(bank[:, 0:n * P], qT[rows, i, nb * P:(nb + 1) * P], kT[rows, lo * P:(lo + n) * P],
                         start=True, stop=True).then_inc(full["sc"], 1)

            work = {"P": project, "C": turn_c, "G": lru_gates, "X": turn_to_chunks, "U": turn_to_tokens,
                    "W": turn_input_matrices, "S": chunk_inputs, "V": turn_values, "A": scores}
            for step, arg in EARLY:
                if step in work:
                    work[step](arg)
            for d in range(KT):
                nb, h = d // 2, d % 2
                lo, n = key_blocks(nb)
                pe.wait_ge(s_prob, d + 1)
                for k in range(n):
                    bank = pe_bank(pe, "tp", ("p", d, k))
                    for i in range(GQ):
                        ins = turn(bank[:, i * P:(i + 1) * P], prs[d % 2][:, i, k * P:(k + 1) * P])
                    ins.then_inc(full["tp"], 1)
                if d + 1 < KT:
                    scores(d + 1, range(2))
                bank = pe_bank(pe, "big", ("pv", d))
                for k in range(n):
                    pe.wait_ge(*emptied("tp", ("p", d, k)))
                    ins = mmul(bank[h * HD:(h + 1) * HD, :], vS[:, lo + k, h * HD:(h + 1) * HD], pT[:, k, :],
                               start=(k == 0), stop=(k == n - 1))
                ins.then_inc(full["big"], 1)
                if d + 1 < KT:
                    scores(d + 1, range(2, GQ))
                    project(("g", 1, d + 1))
                pe.wait_ge(lru_out, CT)
                branch(1, d)
            def ssm_kernels(ct):
                pe.wait_ge(cp_ready, 2 * ct + 2)
                pe.wait_ge(bbd_ready, 2 * ct + 2)
                for name, d, off in (("kf", 0, 0), ("kb", 1, C)):
                    bank = pe_bank(pe, "sc", (name, ct))
                    for g4 in range(4):
                        for r in range(2):
                            ins = mmul(bank[0:2 * C, g4 * P:(g4 + 1) * P],
                                       bbd[:, 2 * d + r, g4].rearrange("p h c -> p (h c)"),
                                       cp[:, ct % 2, 2 * d + r, g4, off:off + P], start=(r == 0), stop=(r == 1))
                    ins.then_inc(full["sc"], 1)

            def ssm_products(ct):
                if ct == 0:
                    pe.wait_ge(x_turned, 1)
                for h in range(2):
                    pe.wait_ge(mm_in[h], 16 * L * (ct + 1))
                for g in (0, 2, 4, 6, 1, 3, 5, 7):
                    if g < 2:
                        bank = pe_bank(pe, "big", ("y1", ct, g))
                    dst = bank[0:NC, (g // 2) * P:(g // 2 + 1) * P]
                    rows = slice((g % 2) * N, (g % 2 + 1) * N)
                    gp = 4 * ct + g // 2
                    mmul(dst, Uv[:, 8 * ct + g, :], mms[ct][:, g, :], start=True, stop=False)
                    for q in range(4):
                        off = C if q < 2 else 0
                        st = Xv[rows, q, gp, 0:NC] if q < 2 else Xb[rows, q - 2, gp, :]
                        ins = mmul(dst, st, cp[rows, ct % 2, q, g // 2, off:off + P], start=False, stop=(q == 3))
                    if g >= 6:
                        ins.then_inc(full["big"], 1)

            def ssm_to_channels(ct):
                for half in range(2):
                    pe.wait_ge(*emptied("big", ("y1", ct, half)))
                bank = pe_bank(pe, "tp", ("y3", ct))
                for j in range(L):
                    ins = turn(bank[:, j * NC:(j + 1) * NC], y2[:, j].rearrange("p g c -> p (g c)"), NC)
                ins.then_inc(full["tp"], 1)

            steps = {"K": ssm_kernels, "Y": ssm_products, "Z": ssm_to_channels}
            pe.wait_ge(*emptied("big", ("pv", KT - 1)))
            for b in (0, 2):
                for d in range(KT):
                    project(("g", b, d))
                    if b == 0:
                        branch(0, d)
                    for step, ct in SSM_STEPS.get((b, d), []):
                        if step in steps:
                            steps[step](ct)
            pe.wait_ge(*emptied("tp", ("y3", CT - 1)))
            for n in range(CT):
                w = plain_weights(("z", n)).rearrange("p (k h c) -> p k h c", k=CT, h=2)
                channels(("z1", n), w[:, :, 1, :], xcv, CT)
                channels(("z0", n), w[:, :, 0, :], xcv, CT)
            pe.wait_ge(glu_ready, CT)
            for d in range(KT):
                branch(2, d)
            pe.wait_ge(gate_used, NBR * KT)
            def turn_h2(t):
                pe.wait_ge(h2_ready, t + 1)
                for half in range(2):
                    bank = pe_bank(pe, "tp", ("h2", t, half))
                    for k in range(4):
                        ins = turn(bank[:, k * P:(k + 1) * P], h2[:, t, (4 * half + k) * P:(4 * half + k + 1) * P])
                    ins.then_inc(full["tp"], 1)

            def logits(t):
                for half in range(2):
                    pe.wait_ge(*emptied("tp", ("h2", t, half)))
                for k in range(KT):
                    ins = mmul(lb[:, t * (NGRP + E):(t + 1) * (NGRP + E)], h2T[:, t % 2, k, :], wge[:, k, :],
                               start=(k == 0), stop=(k == KT - 1))
                ins.then_inc(full["sc"] if t == NT - 1 else logits_done, 1)

            for t in range(NT):
                for h in range(2):
                    bank = pe_bank(pe, "big", ("wo", t, h))
                    for k in range(KT):
                        w = plain_weights(("wo", h, k // 2)).rearrange("p (k c) -> p k c", k=2)
                        ins = mmul(bank[:, :], mixed[:, k, t * P:(t + 1) * P], w[:, k % 2, :],
                                   start=(k == 0), stop=(k == KT - 1))
                    ins.then_inc(full["big"], 1)
                if t == 0:
                    lb = pe_bank(pe, "sc", "logits")
                    pe.wait_ge(late_in, 16 * 6)
                if t >= 2:
                    logits(t - 2)
                if t >= 1:
                    turn_h2(t - 1)
            logits(NT - 2)
            turn_h2(NT - 1)
            logits(NT - 1)
            rb = pe_bank(pe, "sc", "rank")
            pe.wait_ge(mask_ready, 1)
            before = xc[:, 1040:1040 + (NT + 1) * E]
            mmul(rb[:, 0:NT * E], cst[:, K_ONE:K_ONE + P], before[:, 0:NT * E], start=True, stop=False)
            mmul(rb[:, 0:NT * E], cst[:, K_TRI:K_TRI + P], rt[7].rearrange("p t e -> p (t e)"), start=False, stop=True)
            mmul(rb[:, NT * E:(NT + 1) * E], cst[:, K_ONE:K_ONE + P], before[:, NT * E:], start=True,
                 stop=True).then_inc(full["sc"], 1)

            pe.wait_ge(n_ready, 1)
            rest = pe.value_load(ntot[0:1, 0:1], min_val=E - 4, max_val=MAXR * E - 4)

            def turn_rows(i, h, first):
                pe.wait_ge(xg_in[h], (i + (2 - h)) * 8)
                if not first:
                    pe.wait_ge(rows_lo, i)
                for k in range(KT):
                    ins = turn(banks["tp"][k // 4][:, (k % 4) * P:(k % 4 + 1) * P], xg[:, h, k * P:(k + 1) * P])
                ins.then_inc(xg_turned, 1)

            def hidden(i, h, first):
                pe.wait_ge(rows_lo, i + 1)
                if not first:
                    pe.wait_ge(hh_ready, i)
                bank = banks["sc"][0][:, :].rearrange("p (w f) -> p w f", w=2)
                for c in range(KC):
                    pe.wait_ge(w13_lo, i * KC + (c + 1))
                    for k in range(KC_K * c, KC_K * (c + 1)):
                        mmul(bank, xgTh[:, h, k, :], w13h[:, :, k], start=(k == 0), stop=False)
                        mmul(bank, xgTh[:, h, k, :], w13l[:, :, k], start=False, stop=False)
                        ins = mmul(bank, xgTl[:, h, k, :], w13h[:, :, k], start=False, stop=(k == KT - 1))
                    ins.then_inc(hid_full if c == KC - 1 else w13_used, 1)

            def turn_hidden(i, h, first):
                pe.wait_ge(hh_ready, i + 1)
                if not first:
                    pe.wait_ge(hT_ready, i)
                for k in range(2):
                    ins = turn(banks["sc"][1][:, k * P:(k + 1) * P], hh[:, h, k * P:(k + 1) * P])
                ins.then_inc(hT_full, 1)

            def outputs(i, h, second):
                pe.wait_ge(w2_in[h], (i + (2 - h)) * 8)
                pe.wait_ge(hT_ready, i + 1)
                if not second:
                    pe.wait_ge(yb_a, i - 1)
                    pe.wait_ge(yb_v, i - 1)
                w = w2s[h]
                for q in range(2):
                    for k in range(2):
                        ins = mmul(banks["big"][2 * h + q][:, :], hT[:, h, k, :], w[:, k, q * 512:(q + 1) * 512],
                                   start=(k == 0), stop=(k == 1))
                ins.then_inc(y_full, 1)

            def step(i, h):
                hidden(i, h, False)
                turn_rows(i + 1, 1 - h, False)
                outputs(i - 1, 1 - h, False)
                turn_hidden(i, h, False)

            turn_rows(0, 0, True)
            hidden(0, 0, True)
            turn_rows(1, 1, False)
            turn_hidden(0, 0, True)
            hidden(1, 1, False)
            turn_rows(2, 0, False)
            outputs(0, 0, True)
            turn_hidden(1, 1, False)
            hidden(2, 0, False)
            turn_rows(3, 1, False)
            outputs(1, 1, True)
            turn_hidden(2, 0, False)
            with pe.Fori(3, rest + 3, 2) as g:
                step(g, 1)
                step(g + 1, 0)
            hidden(rest + 3, 1, False)
            outputs(rest + 2, 0, False)
            turn_hidden(rest + 3, 1, False)
            outputs(rest + 3, 1, False)

        @block.scalar
        def _(act_e):
            steps = [0]
            fn = nc.scalar.activation

            def link(ins):
                steps[0] += 1
                ins.then_inc(act_step, 1)
                act_e.wait_ge(act_step, steps[0])

            def emptying(ring, ins):
                ins.then_inc(free[ring, "a"], 1)

            load = act_e.dma_start
            load(cst[:, :], consts).then_inc(cst_in, 16)
            load(tok[:, :], token_ids).then_inc(cst_in, 16)
            act_e.wait_ge(eps_ready, 1)
            for t in range(NT):
                act_e.wait_ge(x_in[t], 16)
                fn(act[:, t * D:(t + 1) * D], xt[:, t, :], ACT.Square, accum_out=ssq[:, t:t + 1]).then_inc(squares, 1)
            act_e.wait_ge(squares, NT)
            fn(rstd, ssq, ACT.Sqrt, scale=1.0 / D, bias=epsb).then_inc(root_ready, 1)
            act_e.wait_ge(srow_in, 16 * 3)
            fn(lstep[64:96, :], lstep[64:96, :], ACT.Exp).then_inc(step_exp, 1)
            bank = full_bank(act_e, "tp", "prm")
            emptying("tp", fn(prm[:, :], bank[:, 0:R_END], ACT.Copy))
            act_e.wait_ge(free["tp", "a"], 1)

            def split_hi(m):
                if m < len(ORDER):
                    act_e.wait_ge(raw_in[m % WR], slab_count(raw_slabs, m, WR))
                    fn(wh[:, m % 2, :], wraw[:, m % WR, :], ACT.Copy).then_inc(hi_ready, 1)

            def projected(key, dst, f, **more):
                bank = full_bank(act_e, "big", key)
                emptying("big", fn(dst, bank[:, :], f, **more))
                split_hi(ORDER.index(key) + 2)

            for m in range(2):
                split_hi(m)
            for k in range(KT):
                bank = full_bank(act_e, "big", ("x", k))
                fn(hnh[:, k, :], bank[:, :], ACT.Identity, scale=prm[:, R_G1 + k:R_G1 + k + 1]).then_inc(x_hi, 1)
            act_e.wait_ge(cl_arg, 1)
            fn(lt[:, 1, :], lt[:, 0, :], ACT.Exp).then_inc(cl_exp, 1)
            act_e.wait_ge(s5_arg, 1)
            fn(s5t[:, 1, :], s5t[:, 0, :], ACT.Exp).then_inc(s5_act, 1)
            act_e.wait_ge(s5_arg, 2)
            fn(cs[:, :, :], s5t[:, 2:4, :], ACT.Sin).then_inc(s5_act, 1)
            def softmax_exp(u):
                n = key_blocks(u // 2)[1]
                b = u % 2
                act_e.wait_ge(s_max, u + 1)
                for i in range(GQ):
                    fn(prs[b][:, i, 0:n * P], prs[b][:, i, 0:n * P], ACT.Exp, bias=anm[:, b, i:i + 1],
                       accum_out=asum[:, b, i:i + 1])
                fn(aes[:, b, :], aes[:, b, :], ACT.Exp).then_inc(s_exp, 1)

            def project_out(key):
                if key == "k":
                    projected(key, kT, ACT.Copy)
                elif key == "v":
                    projected(key, vT, ACT.Copy)
                elif key[0] == "xr":
                    projected(key, xrv[:, key[1], 2:T + 2], ACT.Copy)
                elif key[0] == "gr":
                    projected(key, olru[:, key[1], :], ACT.Gelu_apprx_tanh)
                elif key[0] == "u":
                    projected(key, uT[:, key[1], :], ACT.Copy)
                elif key[0] == "q":
                    projected(key, qT[:, key[1], :], ACT.Copy, scale=SCALE)
                else:
                    gate(1, 0)

            def lru_gates(ct):
                if ct:
                    act_e.wait_ge(lru_out, ct)
                else:
                    act_e.wait_ge(cl_ready, 1)
                for w, dst, row in ((0, l_r, R_BR), (1, l_i, R_BI)):
                    for d in range(2):
                        bank = full_bank(act_e, "big", ("lru", ct, w, d))
                        col = row + d * CT + ct
                        emptying("big", fn(dst[:, d, :], bank[:, :], ACT.Sigmoid, bias=prm[:, col:col + 1]))
                act_e.wait_ge(*emptied("big", ("lru", ct, 0, 1)))
                for f, dst in ((ACT.Tanh, l_v), (ACT.Exp, l_a)):
                    for d in range(2):
                        fn(dst[:, d, :], l_r[:, d, :], f, scale=cl[:, d * CT + ct:d * CT + ct + 1]).then_inc(lru_ta, 1)

            def lru_root(ct):
                act_e.wait_ge(lru_q, ct + 1)
                fn(l_q[:, :, :], l_v[:, :, :], ACT.Sqrt).then_inc(lru_s, 1)

            def chunks_out(ct):
                for half in range(2):
                    if ct:
                        act_e.wait_ge(full["tp"], TP.index(("U", ct - 1)) + 1)
                    else:
                        act_e.wait_ge(conv_done, CT)
                    bank = full_bank(act_e, "tp", ("x2", ct, half))
                    emptying("tp", fn(x2[:, :, half * 4:half * 4 + 4, :].rearrange("p g j c -> p j g c"),
                                      bank[0:NC, :].rearrange("p (j g c) -> p j g c", j=4, g=8), ACT.Copy))

            def tokens_out(ct):
                bank = full_bank(act_e, "tp", ("U", ct))
                emptying("tp", fn(Uv[:, 8 * ct:8 * ct + 8, :].rearrange("p g k -> p (g k)"), bank[:, :], ACT.Copy))

            def values_out(_):
                bank = full_bank(act_e, "tp", "v")
                emptying("tp", fn(vS.rearrange("p t c -> p (t c)"), bank[:, :], ACT.Copy))

            def input_matrices_out(ct):
                if ct:
                    act_e.wait_ge(full["sc"], SC.index(("st", 2 * ct - 1)) + 1)
                for g4 in range(4):
                    bank = full_bank(act_e, "tp", ("w", ct, g4))
                    emptying("tp", fn(wt[:, g4].rearrange("p d n -> p (d n)"), bank[:, :], ACT.Copy))

            def gate(b, d):
                n = gate_n[0]
                gate_n[0] += 1
                if b == 2:
                    dst = sgate[:, d, :]
                else:
                    if n >= 2:
                        act_e.wait_ge(gate_used, n - 1)
                    dst = gbuf[:, n % 2, :]
                projected(("g", b, d), dst, ACT.Sigmoid)

            gate_n = [0]
            work = {"P": project_out, "G": lru_gates, "H": lru_root, "X": chunks_out, "U": tokens_out, "W": input_matrices_out,
                    "V": values_out, "A": softmax_exp}
            for step, arg in EARLY:
                if step in work:
                    work[step](arg)
            for d in range(KT):
                for k in range(0, key_blocks(d // 2)[1], 2):
                    if d:
                        act_e.wait_ge(full["big"], BIG.index(("pv", d - 1)) + 1)
                    bank = full_bank(act_e, "tp", ("p", d, k))
                    emptying("tp", fn(pT[:, k, :], bank[:, :], ACT.Copy))
                if d + 1 < KT:
                    softmax_exp(d + 1)
                    gate(1, d + 1)
            def ssm_matrices(ct):
                act_e.wait_ge(kx_ready, ct + 1)
                for j in range(L):
                    load(mms[ct][j * C:(j + 1) * C].rearrange("p (g h) m -> p g h m", h=2)[:, :, 1, :],
                         kx[C:2 * C, :, (L - 1 - j) * C:(L - 1 - j) * C + P]).then_inc(mm_in[1], 16)

            def ssm_products(ct):
                bank = full_bank(act_e, "big", ("y1", ct, 0))
                if ct:
                    act_e.wait_ge(full["tp"], TP.index(("y3", ct - 1)) + 1)
                emptying("big", fn(y2.rearrange("p j (g h) c -> p h j g c", h=2)[:, 0],
                                   bank[0:NC, :].rearrange("p (g j c) -> p j g c", g=4, j=L), ACT.Copy))

            def ssm_to_channels(ct):
                bank = full_bank(act_e, "tp", ("y3", ct))
                emptying("tp", fn(xcv[:, ct, :].rearrange("p (k j) -> p j k", j=L),
                                  bank[:, :].rearrange("p (j k) -> p j k", j=L), ACT.Gelu_apprx_tanh))

            steps_of = {"M": ssm_matrices, "Y": ssm_products, "Z": ssm_to_channels}
            for b in (0, 2):
                for d in range(KT):
                    gate(b, d)
                    for step, ct in SSM_STEPS.get((b, d), []):
                        if step in steps_of:
                            steps_of[step](ct)
            for n in range(CT):
                bank = full_bank(act_e, "big", ("z1", n))
                if n == 0:
                    act_e.wait_ge(gate_used, 2 * KT)
                if n >= 2:
                    act_e.wait_ge(glu_ready, n - 1)
                emptying("big", fn(gbuf[:, n % 2, :], bank[:, :], ACT.Sigmoid, bias=prm[:, R_BG + CT + n:R_BG + CT + n + 1]))
            def rows_in(i, h, second):
                act_e.wait_ge(xg_turned, i + 1)
                if not second:
                    act_e.wait_ge(hid_full, i - 1)
                for q in range(2):
                    fn(xgTh[:, h, 4 * q:4 * q + 4, :], banks["tp"][q][:, :].rearrange("p (k s) -> p k s", k=4),
                       ACT.Copy).then_inc(rows_hi, 1)

            def w13_parts(i, slot, c, first=False):
                if c == 0:
                    act_e.wait_ge(w13_in[slot], (i + (4 - slot)) * 8)
                if not first:
                    if c == KC - 1:
                        act_e.wait_ge(hid_full, i)
                    else:
                        act_e.wait_ge(w13_used, i * (KC - 1) + (c + 2 - KC))
                fn(w13h[:, :, KC_K * c:KC_K * (c + 1)], w13[slot][:, :, KC_K * c:KC_K * (c + 1)], ACT.Copy).then_inc(w13_hi, 1)

            def silu(i, h, second):
                act_e.wait_ge(hid_full, i + 1)
                if not second:
                    act_e.wait_ge(hh_ready, i - 1)
                fn(sg[:, h, :], banks["sc"][0][:, 0:FE], ACT.Silu).then_inc(silu_done, 1)

            def rows_done(i, h):
                act_e.wait_ge(y_full, i + 1)
                act_e.wait_ge(rows_out[h], (i - h) * 8)
                fn(yb[:, h, 0:512], banks["big"][2 * h][:, :], ACT.Copy).then_inc(yb_a, 1)

            def h2_turned(t):
                bank = full_bank(act_e, "tp", ("h2", t, 0))
                if t >= 2:
                    act_e.wait_ge(logits_done, t - 1)
                emptying("tp", fn(h2T[:, t % 2, 0:4], bank[:, :].rearrange("p (k s) -> p k s", k=4), ACT.Copy))

            act_e.wait_ge(full["big"], BIG.index(("p", 2, KT - 1)) + 1)
            for t in range(NT):
                act_e.wait_ge(*emptied("big", ("wo", t, 1)))
                fn(act[:, t * D:(t + 1) * D], xres[:, t, :], ACT.Square, accum_out=ssq2[:, t:t + 1]).then_inc(x1_sq, 1)
                act_e.wait_ge(x1_sq, t + 1)
                fn(rstd2[:, t:t + 1], ssq2[:, t:t + 1], ACT.Sqrt, scale=1.0 / D, bias=epsb).then_inc(x1_root, 1)
                if t:
                    h2_turned(t - 1)
            act_e.wait_ge(full["big"], BIG.index(("wo", NT - 1, 1)) + 1)
            for c in range(KC):
                w13_parts(0, 0, c, first=True)
            h2_turned(NT - 1)
            act_e.wait_ge(w_arg, 1)
            fn(rg[3], rg[2], ACT.Exp).then_inc(w_exp, 1)
            act_e.wait_ge(w_arg, 2)
            fn(rs[8], rs[7], ACT.Exp).then_inc(w_exp, 1)

            act_e.wait_ge(n_ready, 1)
            rest = act_e.value_load(ntot[0:1, 0:1], min_val=E - 4, max_val=MAXR * E - 4)
            act_e.wait_ge(full["sc"], SC.index("rank") + 1)

            def step(i, slot, second, first=False, last=False):
                h = slot % 2
                for c in range(0 if last else KC - 1):
                    w13_parts(i + 1, (slot + 1) % 4, c)
                silu(i, h, second)
                if not last:
                    w13_parts(i + 1, (slot + 1) % 4, KC - 1)
                    rows_in(i + 1, 1 - h, first)
                if not first:
                    rows_done(i - 1, 1 - h)

            rows_in(0, 0, True)
            step(0, 0, True, first=True)
            step(1, 1, True)
            step(2, 2, False)
            with act_e.Fori(3, rest + 3, 4) as g:
                for j in range(4):
                    step(g + j, (3 + j) % 4, False)
            step(rest + 3, 3, False, last=True)
            rows_done(rest + 3, 1)
            for t in range(NT):
                act_e.wait_ge(acc_ready, t + 1)
                fn(act[:, t * D:(t + 1) * D], xres[:, t, :], ACT.Square, accum_out=ssq3[:, t:t + 1]).then_inc(out_sq, 1)
                act_e.wait_ge(out_sq, t + 1)
                fn(rstd3[:, t:t + 1], ssq3[:, t:t + 1], ACT.Sqrt, scale=1.0 / D, bias=epsb).then_inc(out_root, 1)

        @block.vector
        def _(dve):
            steps = [0]
            tt, ts, stt = nc.vector.tensor_tensor, nc.vector.tensor_scalar, nc.vector.scalar_tensor_tensor

            def link(ins):
                steps[0] += 1
                ins.then_inc(dve_step, 1)
                dve.wait_ge(dve_step, steps[0])

            def emptying(ring, ins):
                ins.then_inc(free[ring, "v"], 1)

            nc.vector.memset(epsb, EPS).then_inc(eps_ready, 1)
            dve.wait_ge(root_ready, 1)
            link(nc.vector.reciprocal(rstd, rstd))
            for t in range(NT):
                ts(xs[:, t, :], xt[:, t, :], rstd[:, t:t + 1], None, MUL).then_inc(xs_ready, 1)
            dve.wait_ge(step_exp, 1)
            nc.vector.tensor_copy(srows[64:96, :].rearrange("p (h n) -> p h n", h=2), bc(lstep[64:96, :], 2, N)).then_inc(srows_ready, 1)
            bank = full_bank(dve, "tp", "s5p")
            emptying("tp", nc.vector.tensor_copy(s5p[:, :], bank[:, 0:96]))
            for m in range(POOL_SPLITS.start):
                split_lo(dve, tt, m)
            dve.wait_ge(*emptied("tp", "prm"))
            for k in range(KT):
                bank = full_bank(dve, "big", ("x", k))
                dve.wait_ge(x_hi, k + 1)
                emptying("big", stt(hnl[:, k, :], bank[:, :], prm[:, R_G1 + k:R_G1 + k + 1],
                                   hnh[:, k, :].bitcast(f32), MUL, SUB))
            lm = prm[:, R_LAM:R_LAM + 2 * CT]
            stt(lt[:, 0, :], lm, -1.0, lm, MUL, ALU.min).then_inc(cl_arg, 1)
            dve.wait_ge(cl_exp, 1)
            link(ts(lt[:, 2, :], lt[:, 1, :], 2.0, None, ADD))
            link(nc.vector.reciprocal(lt[:, 2, :], lt[:, 2, :]))
            link(tt(lt[:, 0, :], lt[:, 1, :], lt[:, 2, :], MUL))
            link(tt(lt[:, 1, :], lt[:, 0, :], lt[:, 0, :], MUL))
            link(ts(lt[:, 2, :], lt[:, 1, :], 1.0 / 15, None, MUL))
            for m in (13, 11, 9, 7, 5, 3):
                link(stt(lt[:, 2, :], lt[:, 2, :], 1.0 / m, lt[:, 1, :], ADD, MUL))
            link(stt(lt[:, 2, :], lt[:, 2, :], 1.0, lt[:, 0, :], ADD, MUL))
            link(ts(lt[:, 3, :], lm, -1.0, 0.0, MUL, MAX))
            link(stt(lt[:, 3, :], lt[:, 2, :], 2.0, lt[:, 3, :], MUL, ADD))
            ts(cl, lt[:, 3, :], -LRU_C, None, MUL).then_inc(cl_ready, 1)
            ar, ai, st = s5p[:, 0:32], s5p[:, 32:64], s5p[:, 64:96]
            q = [s5t[:, i, :] for i in range(16)]
            dve.wait_ge(*emptied("tp", "s5p"))
            tt(q[0], ar, st, MUL).then_inc(s5_arg, 1)
            link(tt(q[4], ai, st, MUL))
            big = 1.5 * 2.0 ** 23
            link(ts(q[5], q[4], 1.0 / (2 * np.pi), big, MUL, ADD))
            link(ts(q[5], q[5], -big, None, ADD))
            c1 = 6.28125
            c2 = float(np.float32(np.round((2 * np.pi - c1) * 2.0 ** 20) / 2.0 ** 20))
            for c in (c1, c2, 2 * np.pi - c1 - c2):
                link(stt(q[4], q[5], -c, q[4], MUL, ADD))
            link(ts(q[3], q[4], 3.1415925, -3.1415925, ALU.min, MAX))
            link(stt(q[2], q[3], -1.0, q[3], MUL, ALU.min))
            ts(q[2], q[2], float(np.pi / 2), None, ADD).then_inc(s5_arg, 1)
            dve.wait_ge(s5_act, 2)
            link(tt(pw[:, 0, 1, :], q[1], cs[:, 0, :], MUL))
            link(tt(pw[:, 1, 1, :], q[1], cs[:, 1, :], MUL))
            link(nc.vector.memset(pw[:, 0, 0, :], 1.0))
            link(nc.vector.memset(pw[:, 1, 0, :], 0.0))
            nr, ni = q[5], pw[:, 1, 1, :]
            link(ts(nr, pw[:, 0, 1, :], -1.0, None, ADD))
            link(tt(q[6], ar, ar, MUL))
            link(tt(q[7], ai, ai, MUL))
            link(tt(q[6], q[6], q[7], ADD))
            link(nc.vector.reciprocal(q[6], q[6]))
            link(tt(q[7], nr, ar, MUL))
            link(tt(q[8], ni, ai, MUL))
            link(tt(q[7], q[7], q[8], ADD))
            link(tt(q[7], q[7], q[6], MUL))
            link(tt(q[8], ni, ar, MUL))
            link(tt(q[9], nr, ai, MUL))
            link(tt(q[8], q[8], q[9], SUB))
            link(tt(q[8], q[8], q[6], MUL))
            dve.wait_ge(early_in, 16 * 8)
            sr, si = bc(q[7], 2, C), bc(q[8], 2, C)
            bbv = bb[:, :, :, :].rearrange("p (d r) g c -> p d r g c", d=2)
            bt = [btmp[:, a].rearrange("p (d g) c -> p d g c", d=2) for a in range(2)]
            for r, (x0, x1, op) in enumerate(((0, 1, SUB), (1, 0, ADD))):
                link(tt(btmp[:, 0], sr, bin_[:, x0], MUL))
                link(tt(btmp[:, 1], si, bin_[:, x1], MUL))
                link(tt(bbv[:, :, r], bt[0], bt[1], op))
            for lo, n, by in ((1, 1, 1), (1, 2, 2), (1, 4, 4)):
                xr_, xi_ = pw[:, 0, lo:lo + n, :], pw[:, 1, lo:lo + n, :]
                yr_, yi_ = bc(pw[:, 0, by, :], 1, n), bc(pw[:, 1, by, :], 1, n)
                dst = slice(lo + by, lo + by + n)
                ta = s5t[:, 8:8 + n, :]
                tb = s5t[:, 12:12 + n, :]
                link(tt(ta, xr_, yr_, MUL))
                link(tt(tb, xi_, yi_, MUL))
                link(tt(pw[:, 0, dst, :], ta, tb, SUB))
                link(tt(ta, xr_, yi_, MUL))
                link(tt(tb, xi_, yr_, MUL))
                link(tt(pw[:, 1, dst, :], ta, tb, ADD))
            for d in range(2):
                cols = slice(d * GP, (d + 1) * GP)
                link(nc.vector.tensor_copy(aa[:, 0, 2 * d, :], pw[:, 0, L, cols]))
                link(nc.vector.tensor_copy(aa[:, 0, 2 * d + 1, :], pw[:, 0, L, cols]))
                link(nc.vector.tensor_copy(aa[:, 1, 2 * d, :], pw[:, 1, L, cols]))
                link(ts(aa[:, 1, 2 * d + 1, :], pw[:, 1, L, cols], -1.0, None, MUL))
            dve.wait_ge(dskip_in, 16)
            tt(dd[:, :, :], bc(dskip[:, :], 2, C), bc(cst[0:2 * C, K_DLT:K_DLT + C], 1, GP), MUL).then_inc(s5_tab, 1)
            def softmax_max(u):
                nb, hk = u // 2, u % 2
                lo, n = key_blocks(nb)
                off = (lo - nb + 1) * P
                b = u % 2
                for i in range(GQ):
                    bank = full_bank(dve, "sc", ("s", u, i))
                    h = hk * GQ + i
                    if i == 0 and u >= 2:
                        dve.wait_ge(full["tp"], TP.index(("p", u - 2, key_blocks((u - 2) // 2)[1] - 1)) + 1)
                    emptying("sc", nc.vector.tensor_tensor_reduce(
                        out=prs[b][:, i, 0:n * P], in0=bank[:, 0:n * P], in1=btab[:, h, off:off + n * P], scale=1.0,
                        scalar=sink[:, h:h + 1], op0=ADD, op1=MAX, accum_out=am[:, b, i:i + 1]))
                dve.wait_ge(*emptied("sc", ("s", u, GQ - 1)))
                ts(anm[:, b, :], am[:, b, :], -1.0, None, MUL)
                tt(aes[:, b, :], sink[:, hk * GQ:(hk + 1) * GQ], am[:, b, :], SUB).then_inc(s_max, 1)

            def softmax_scale(u):
                n = key_blocks(u // 2)[1]
                b = u % 2
                dve.wait_ge(s_exp, u + 1)
                link(tt(ard[:, b, :], asum[:, b, :], aes[:, b, :], ADD))
                link(nc.vector.reciprocal(ard[:, b, :], ard[:, b, :]))
                for i in range(GQ):
                    ins = ts(prs[b][:, i, 0:n * P], prs[b][:, i, 0:n * P], ard[:, b, i:i + 1], None, MUL)
                ins.then_inc(s_prob, 1)

            def rest_of(key):
                m = ORDER.index(key) + 2
                if POOL_SPLITS.stop <= m < len(ORDER):
                    split_lo(dve, tt, m)
                if key[0] == "xr":
                    convolve(key[1])

            def convolve(ct):
                dve.wait_ge(pad_zero, 2)
                dve.wait_ge(*emptied("big", ("xr", ct)))
                w = [prm[:, R_CW + i * CT + ct:R_CW + i * CT + ct + 1] for i in range(CONV)]
                link(ts(xcv[:, ct, :], xrv[:, ct, 0:T], w[0], prm[:, R_CB + ct:R_CB + ct + 1], MUL, ADD))
                for i in range(1, CONV - 1):
                    link(stt(xcv[:, ct, :], xrv[:, ct, i:i + T], w[i], xcv[:, ct, :], MUL, ADD))
                stt(xcv[:, ct, :], xrv[:, ct, 3:3 + T], w[3], xcv[:, ct, :], MUL, ADD).then_inc(conv_done, 1)

            def c_out(_):
                for r in range(2):
                    bank = full_bank(dve, "tp", ("c", r))
                    for h in range(2):
                        rows = slice(h * N, (h + 1) * N)
                        src = bank[rows, :].rearrange("p (g h c) -> p g h c", h=2, c=C)[:, :, h, :]
                        ins = nc.vector.tensor_copy(cc[rows, r], src)
                    emptying("tp", ins)

            def lru_squares(ct):
                dve.wait_ge(*emptied("big", ("lru", ct, 1, 1)))
                dve.wait_ge(conv_done, CT)
                tt(l_i[:, :, :], l_i[:, :, :], bc(xcv[:, ct, :], 1, 2), MUL)
                dve.wait_ge(lru_ta, 4 * ct + 2)
                link(ts(l_q[:, :, :], l_v[:, :, :], -1.0, 1.0, MUL, ADD))
                link(nc.vector.reciprocal(l_q[:, :, :], l_q[:, :, :]))
                stt(l_v[:, :, :], l_v[:, :, :], -2.0, l_q[:, :, :], MUL, MUL).then_inc(lru_q, 1)

            def lru_scans(ct):
                dve.wait_ge(lru_s, ct + 1)
                dve.wait_ge(lru_ta, 4 * ct + 4)
                link(tt(l_i[:, :, :], l_i[:, :, :], l_q[:, :, :], MUL))
                nc.vector.tensor_tensor_scan(l_v[:, 0, :], l_a[:, 0, :], l_i[:, 0, :], 0.0, MUL, ADD)
                link(nc.vector.tensor_tensor_scan(l_v[:, 1, ::-1], l_a[:, 1, ::-1], l_i[:, 1, ::-1], 0.0, MUL, ADD))
                link(tt(l_v[:, 0, :], l_v[:, 0, :], l_v[:, 1, :], ADD))
                dve.wait_ge(*emptied("big", ("gr", ct)))
                tt(olru[:, ct, :], olru[:, ct, :], l_v[:, 0, :], MUL).then_inc(lru_out, 1)

            def chunk_inputs_out(ct):
                dve.wait_ge(x_zero, 1)
                for d in (2 * ct, 2 * ct + 1):
                    bank = full_bank(dve, "sc", ("st", d))
                    emptying("sc", nc.vector.tensor_copy(Xv[:, :, 2 * d:2 * d + 2, 1:NC + 1],
                                                         bank[:, :].rearrange("p (q g k) -> p q g k", q=4, g=2)))

            def first_softmax(u):
                dve.wait_ge(btab_ready, NQ)
                dve.wait_ge(sink_in, 16)
                softmax_max(u)
                softmax_scale(u)

            work = {"P": rest_of, "C": c_out, "G": lru_squares, "H": lru_scans,
                    "S": chunk_inputs_out, "A": first_softmax}
            for step, arg in EARLY:
                if step in work:
                    work[step](arg)

            gate_n = [0]

            def gated(b, d):
                bank = full_bank(dve, "big", ("p", b, d))
                dve.wait_ge(*emptied("big", ("g", b, d)))
                g = sgate[:, d, :] if b == 2 else gbuf[:, gate_n[0] % 2, :]
                gate_n[0] += 1
                if b == 1:
                    emptying("big", tt(mixed[:, d, :], bank[:, :], g, MUL))
                    dve.wait_ge(*emptied("big", ("p", b, d)))
                    dve.nop().then_inc(gate_used, 1)
                else:
                    emptying("big", tt(g, bank[:, :], g, MUL))
                    dve.wait_ge(*emptied("big", ("p", b, d)))
                    tt(mixed[:, d, :], mixed[:, d, :], g, ADD).then_inc(gate_used, 1)

            for d in range(KT):
                if d:
                    rest_of(("g", 1, d))
                for k in range(1, key_blocks(d // 2)[1], 2):
                    if d:
                        dve.wait_ge(full["big"], BIG.index(("pv", d - 1)) + 1)
                    bank = full_bank(dve, "tp", ("p", d, k))
                    emptying("tp", nc.vector.tensor_copy(pT[:, k, :], bank[:, :]))
                if d + 1 < KT:
                    softmax_max(d + 1)
                rows = slice((d % 2) * HD, (d % 2 + 1) * HD)
                bank = full_bank(dve, "big", ("pv", d))
                emptying("big", nc.vector.tensor_copy(oatt[rows, :, (d // 2) * P:(d // 2 + 1) * P],
                                                      bank[rows, :].rearrange("p (i q) -> p i q", i=GQ)))
                if d + 1 < KT:
                    softmax_scale(d + 1)
                gated(1, d)
            def block_diagonal(ct):
                if ct:
                    dve.wait_ge(full["sc"], SC.index(("kb", ct - 1)) + 1)
                for h in range(2):
                    rows = slice(h * N, (h + 1) * N)
                    nc.vector.tensor_copy(bbd[rows, :, :, h, :], bb[rows, :, 4 * ct:4 * ct + 4, :]).then_inc(bbd_ready, 1)

            def lag_kernels(ct):
                kf = full_bank(dve, "sc", ("kf", ct))[0:2 * C, :].rearrange("p (g m) -> p g m", g=4)
                kb = full_bank(dve, "sc", ("kb", ct))[0:2 * C, :].rearrange("p (g m) -> p g m", g=4)
                if ct:
                    for h in range(2):
                        dve.wait_ge(mm_in[h], 16 * L * ct)
                link(nc.vector.tensor_copy(kx[:, :, (L - 1) * C:], kf))
                emptying("sc", tt(kx[:, :, (L - 1) * C:L * C], kx[:, :, (L - 1) * C:L * C], kb[:, :, (L - 1) * C:], ADD))
                emptying("sc", nc.vector.tensor_copy(kx[:, :, 0:(L - 1) * C], kb[:, :, 0:(L - 1) * C]))
                dve.wait_ge(*emptied("sc", ("kb", ct)))
                tt(kx[:, :, (L - 1) * C:L * C], kx[:, :, (L - 1) * C:L * C], dd[:, 4 * ct:4 * ct + 4, :], ADD).then_inc(kx_ready, 1)

            def backward_states():
                dve.wait_ge(scan_add, 2 * (NC - 2))
                nc.vector.tensor_copy(Xb[:, :, :, :], Xv[:, 2:4, :, NC - 1::-1]).then_inc(x_turned, 1)

            def ssm_products(ct):
                bank = full_bank(dve, "big", ("y1", ct, 1))
                if ct:
                    dve.wait_ge(full["tp"], TP.index(("y3", ct - 1)) + 1)
                emptying("big", nc.vector.tensor_copy(y2.rearrange("p j (g h) c -> p h g j c", h=2)[:, 1],
                                                      bank[0:NC, :].rearrange("p (g j c) -> p g j c", g=4, j=L)))

            link(nc.vector.memset(xrp[:, 1024:1536], 0.0))
            block_diagonal(0)
            for b in (0, 2):
                for d in range(KT):
                    if (b, d) != (0, 0):
                        rest_of(("g", 0, d - 1) if b == 0 else ("g", 2, d - 1) if d else ("g", 0, KT - 1))
                    if b == 0:
                        gated(0, d)
                    for step, ct in SSM_STEPS.get((b, d), []):
                        if step == "K":
                            lag_kernels(ct)
                            if ct + 1 < CT:
                                block_diagonal(ct + 1)
                        if step == "R":
                            backward_states()
                        if step == "Y":
                            ssm_products(ct)
            for n in range(CT):
                bank = full_bank(dve, "big", ("z0", n))
                dve.wait_ge(*emptied("big", ("z1", n)))
                col = prm[:, R_BG + n:R_BG + n + 1]
                ins = stt(ossm[:, n, :], bank[:, :], col, gbuf[:, n % 2, :], ADD, MUL)
                emptying("big", ins)
                dve.wait_ge(*emptied("big", ("z0", n)))
                dve.nop().then_inc(glu_ready, 1)
            for d in range(KT):
                gated(2, d)
            def h2_turned(t):
                bank = full_bank(dve, "tp", ("h2", t, 1))
                if t >= 2:
                    dve.wait_ge(logits_done, t - 1)
                emptying("tp", nc.vector.tensor_copy(h2T[:, t % 2, 4:8], bank[:, :].rearrange("p (k s) -> p k s", k=4)))

            dve.wait_ge(x_again, 16 * NT)
            dve.wait_ge(late_in, 16 * 6)
            for t in range(NT):
                for h in range(2):
                    bank = full_bank(dve, "big", ("wo", t, h))
                    half = xres[:, t, h * 512:(h + 1) * 512]
                    emptying("big", tt(half, bank[:, :], half, ADD))
                dve.wait_ge(x1_root, t + 1)
                link(nc.vector.reciprocal(rstd2[:, t:t + 1], rstd2[:, t:t + 1]))
                stt(h2[:, t, :], xres[:, t, :], rstd2[:, t:t + 1], g2b, MUL, MUL).then_inc(h2_ready, 1)
                if t:
                    h2_turned(t - 1)
            h2_turned(NT - 1)
            lg = xc[:, 960:1040].rearrange("p (t c) -> p t c", t=NT)
            bank = full_bank(dve, "sc", "logits")
            emptying("sc", tt(lg, bank[:, 0:NT * (NGRP + E)].rearrange("p (t c) -> p t c", t=NT), bc(bge, 1, NT), ADD))
            dve.wait_ge(*emptied("sc", "logits"))
            lgg, lge = lg[:, :, 0:NGRP], lg[:, :, NGRP:]

            def top(mask, values, peak, score, rank, n):
                link(nc.vector.tensor_reduce(peak, values, AX.X, MAX))
                link(tt(score, values, bc(peak, 2, n), ALU.is_equal))
                link(tt(score, score, bc(cst[:, K_REV:K_REV + n], 1, NT), MUL))
                link(nc.vector.tensor_reduce(rank, score, AX.X, MAX))
                link(tt(mask, score, bc(rank, 2, n), ALU.is_equal))

            top(rg[1], lgg, rs[0], rg[0], rs[1], NGRP)
            tt(rg[2], lgg, bc(rs[0], 2, NGRP), SUB).then_inc(w_arg, 1)
            link(ts(rg[4], rg[1], -NEG, NEG, MUL, ADD))
            g4 = "p t (g e) -> p t g e"
            link(tt(rt[1].rearrange(g4, g=NGRP), lge.rearrange(g4, g=NGRP), bc(rg[1], 3, 4), MUL))
            link(tt(rt[1].rearrange(g4, g=NGRP), rt[1].rearrange(g4, g=NGRP), bc(rg[4], 3, 4), ADD))
            top(rt[3], rt[1], rs[2], rt[2], rs[3], E)
            link(stt(rt[4], rt[3], 2 * NEG, rt[1], MUL, ADD))
            top(rt[5], rt[4], rs[4], rt[2], rs[5], E)
            tt(rs[7], rs[4], rs[2], SUB).then_inc(w_arg, 1)
            link(tt(rt[7], rt[3], rt[5], ADD))
            before = xc[:, 1040:1040 + (NT + 1) * E].rearrange("p (t e) -> p t e", e=E)
            nc.vector.memset(before[:, 0], 0.0)
            link(nc.vector.tensor_copy(before[:, 1], rt[7][:, 0]))
            for t in range(1, NT):
                ins = tt(before[:, t + 1], before[:, t], rt[7][:, t], ADD)
                if t + 1 < NT:
                    link(ins)
            ins.then_inc(mask_ready, 1)
            dve.wait_ge(w_exp, 2)
            link(nc.vector.tensor_reduce(rs[9], rg[3], AX.X, ADD))
            link(ts(rs[10], rs[8], 1.0, None, ADD))
            link(tt(rs[10], rs[10], rs[9], MUL))
            link(nc.vector.reciprocal(rs[11], rs[10]))
            link(tt(rs[12], rs[11], rs[8], MUL))
            bank = full_bank(dve, "sc", "rank")
            rank = bank[:, 0:NT * E].rearrange("p (t e) -> p t e", t=NT)
            cnt = rs[13][0:1, 0:1]
            rounds = rs[14][0:1, 0:1]
            link(ts(rt[9], rank, P - 0.5, None, ALU.is_gt))
            for r in range(2, MAXR):
                link(stt(rt[9], rank, r * P - 0.5, rt[9], ALU.is_gt, ADD))
            tt(rt[8], rank, bc(cst[:, K_E128:K_E128 + E], 1, NT), ADD)
            emptying("sc", nc.vector.tensor_reduce(cnt, bank[0:1, NT * E:(NT + 1) * E], AX.X, MAX))
            dve.wait_ge(*emptied("sc", "rank"))
            link(stt(rt[8], rt[9], float(ROUND - P), rt[8], MUL, ADD))
            masked = xc[:, 640:768].rearrange("p (c t e) -> p c t e", c=2, t=NT)
            masks = xc[:, 192:448].rearrange("p (c t e) -> p c t e", c=2, t=2 * NT)[:, :, 0:NT]
            link(tt(masked, bc(rt[8], 1, 2), masks, MUL))
            places = xc[:, 788:796].rearrange("p (c t) -> p c t", c=2)
            link(nc.vector.tensor_reduce(places, masked, AX.X, ADD))
            nc.vector.tensor_copy(slot_i[:, :, :], places).then_inc(slots_ready, 1)
            link(ts(rounds, cnt, P + 0.5, 1.0, ALU.is_gt, ADD))
            for r in range(2, MAXR):
                link(stt(rounds, cnt, r * P + 0.5, rounds, ALU.is_gt, ADD))
            link(ts(rounds, rounds, float(E), -4.0, MUL, ADD))
            nc.vector.tensor_copy(ntot[0:1, 0:1], rounds).then_inc(n_ready, 1)
            dve.wait_ge(n_ready, 1)

            rest = dve.value_load(ntot[0:1, 0:1], min_val=E - 4, max_val=MAXR * E - 4)

            def rows_in(i, h):
                for q in range(2):
                    dve.wait_ge(rows_hi, i * 2 + (q + 1))
                    ins = tt(xgTl[:, h, 4 * q:4 * q + 4, :], banks["tp"][q][:, :].rearrange("p (k s) -> p k s", k=4),
                             xgTh[:, h, 4 * q:4 * q + 4, :].bitcast(f32), SUB)
                ins.then_inc(rows_lo, 1)

            def w13_parts(i, slot, c):
                dve.wait_ge(w13_hi, i * KC + (c + 1))
                tt(w13l[:, :, KC_K * c:KC_K * (c + 1)], w13[slot][:, :, KC_K * c:KC_K * (c + 1)],
                   w13h[:, :, KC_K * c:KC_K * (c + 1)].bitcast(f32), SUB).then_inc(w13_lo, 1)

            def gated_hidden(i, h):
                dve.wait_ge(silu_done, i + 1)
                tt(hh[:, h, :], banks["sc"][0][:, FE:2 * FE], sg[:, h, :], MUL).then_inc(hh_ready, 1)

            def hidden_turned(i, h):
                dve.wait_ge(hT_full, i + 1)
                nc.vector.tensor_copy(hT[:, h].rearrange("p k s -> p (k s)"), banks["sc"][1][:, 0:2 * P]).then_inc(hT_ready, 1)

            def rows_done(i, h):
                dve.wait_ge(y_full, i + 1)
                dve.wait_ge(rows_out[h], (i - h) * 8)
                nc.vector.tensor_copy(yb[:, h, 512:1024], banks["big"][2 * h + 1][:, :]).then_inc(yb_v, 1)

            def step(i, slot, first=False, last=False):
                h = slot % 2
                for c in range(0 if last else KC - 1):
                    w13_parts(i + 1, (slot + 1) % 4, c)
                gated_hidden(i, h)
                if not last:
                    w13_parts(i + 1, (slot + 1) % 4, KC - 1)
                    rows_in(i + 1, 1 - h)
                if not first:
                    rows_done(i - 1, 1 - h)
                hidden_turned(i, h)

            dve.wait_ge(w13_lo, KC)
            rows_in(0, 0)
            step(0, 0, first=True)
            step(1, 1)
            step(2, 2)
            with dve.Fori(3, rest + 3, 4) as g:
                for j in range(4):
                    step(g + j, (3 + j) % 4)
            step(rest + 3, 3, last=True)
            rows_done(rest + 3, 1)
            def final_scale(t):
                dve.wait_ge(out_root, t + 1)
                link(nc.vector.reciprocal(rstd3[:, t:t + 1], rstd3[:, t:t + 1]))
                stt(xres[:, t, :], xres[:, t, :], rstd3[:, t:t + 1], fgb, MUL, MUL).then_inc(out_ready, 1)

            for t in range(NT):
                dve.wait_ge(yg_in[t], 32)
                for c in range(2):
                    ins = stt(xres[:, t, :], pair[c][:, t, :], rs[11 + c][:, t:t + 1], xres[:, t, :], MUL, ADD)
                    if c:
                        ins.then_inc(acc_ready, 1)
                    else:
                        link(ins)
                if t:
                    final_scale(t - 1)
            final_scale(NT - 1)


_LAYERED = ["norm1_g", "w_in", "attn_sink", "lru_conv_w", "lru_conv_b", "lru_w_r", "lru_b_r", "lru_w_i", "lru_b_i",
            "lru_lambda", "ssm_a_re", "ssm_a_im", "ssm_log_step", "ssm_b_re", "ssm_b_im", "ssm_c_re", "ssm_c_im",
            "ssm_d", "ssm_w_glu", "ssm_b_glu", "w_branch", "w_out", "norm2_g", "moe_w_group", "moe_b_group",
            "moe_w_expert", "moe_b_expert", "moe_w1", "moe_w3", "moe_w2"]


def kernel(**inputs):
    import concourse.bacc as bacc
    from concourse.bass_utils import run_bass_kernel_spmd

    arrays = {"x": inputs["x"][0]}
    for name in _LAYERED:
        a = np.asarray(inputs[name])[0]
        if name.startswith("moe_w") and a.ndim == 4:
            a = a.reshape((E,) + a.shape[2:])
        arrays[name] = a
    arrays["final_norm_g"] = inputs["final_norm_g"]
    arrays["consts"], arrays["token_ids"] = constants()

    nc = bacc.Bacc("TRN2", target_bir_lowering=False, num_devices=1)
    ins, args = {}, []
    for name, a in arrays.items():
        a = np.ascontiguousarray(a)
        ins[f"in_{name}"] = a
        args.append(nc.dram_tensor(f"in_{name}", a.shape, mybir.dt.from_np(a.dtype), kind="ExternalInput").ap())
    args.append(nc.dram_tensor("out_0", (T, D), mybir.dt.float32, kind="ExternalOutput").ap())
    hybrid_block(nc, *args)
    r = run_bass_kernel_spmd(nc, [ins], core_ids=[0])
    return r.results[0]["out_0"].reshape(1, T, D)
```
